# Optimizing a Trainium2 kernel written in Bass

```python
import jax, jax.numpy as jnp
from jax import lax
import numpy as np

D_MODEL = 1024
BATCH = 1
SEQ = 1024
DEPTH = 1

D_MIX = D_MODEL
GLA_HEADS = 4
GLA_HEAD_K = D_MIX // 16
GLA_HEAD_V = D_MIX // 8
GLA_GATE_RANK = 16
GLA_GATE_NORMALIZER = 16.0
HGRN_HEADS = 4
HGRN_HEAD_F = D_MIX // 16
HGRN_HEAD_I = D_MIX // 16
CONV_CHANNELS = D_MIX // 4
CONV_WIDTH = 3
CHUNK = 64
N_EXPERTS = 32
TOP_K = 4
D_FF = D_MODEL
SWIGLU_LIMIT = 7.0
SWIGLU_ALPHA = 1.702
MOE_BLOCK = 128
LN_EPS = 1e-5
RMS_EPS = 1e-6
DEEPNORM_ALPHA = (2 * DEPTH) ** 0.25
DEEPNORM_BETA = (8 * DEPTH) ** -0.25

GLA_K_DIM = GLA_HEADS * GLA_HEAD_K
GLA_V_DIM = GLA_HEADS * GLA_HEAD_V
HGRN_F_DIM = HGRN_HEADS * HGRN_HEAD_F
HGRN_I_DIM = HGRN_HEADS * HGRN_HEAD_I
IN_SPLITS = (GLA_K_DIM, GLA_K_DIM, GLA_V_DIM, GLA_GATE_RANK, GLA_V_DIM,
             HGRN_F_DIM, HGRN_F_DIM, HGRN_I_DIM, HGRN_I_DIM,
             CONV_CHANNELS, CONV_CHANNELS, CONV_CHANNELS)
D_IN_PROJ = sum(IN_SPLITS)

kernel_name = "hybrid_gla_hgrn2_shortconv_moe_deepnorm"

def layer_norm(x, g, b):
    xf = x.astype(jnp.float32)
    mu = jnp.mean(xf, axis=-1, keepdims=True)
    var = jnp.mean(jnp.square(xf - mu), axis=-1, keepdims=True)
    y = (xf - mu) * lax.rsqrt(var + LN_EPS) * g.astype(jnp.float32) + b.astype(jnp.float32)
    return y.astype(x.dtype)

def gated_head_rmsnorm(o, gate, g):
    bsz, t, h, dv = o.shape
    of = o.astype(jnp.float32)
    of = of * lax.rsqrt(jnp.mean(of * of, axis=-1, keepdims=True) + RMS_EPS) * g.astype(jnp.float32)
    return (of.reshape(bsz, t, h * dv) * jax.nn.silu(gate.astype(jnp.float32))).astype(gate.dtype)

def chunk_gated_linear_attention(q, k, v, log_a):
    bsz, t, h, dk = q.shape
    dv = v.shape[-1]
    n_chunks = t // CHUNK

    def to_chunks(z):
        return z.astype(jnp.float32).reshape(bsz, n_chunks, CHUNK, h, z.shape[-1]).transpose(1, 0, 3, 2, 4)

    causal = jnp.tril(jnp.ones((CHUNK, CHUNK), dtype=bool))[:, :, None]

    def step(state, blk):
        qb, kb, vb, gb = blk
        g_cum = jnp.cumsum(gb, axis=2)
        rel = g_cum[:, :, :, None, :] - g_cum[:, :, None, :, :]
        decay = jnp.where(causal, jnp.exp(jnp.minimum(rel, 0.0)), 0.0)
        scores = jnp.einsum("bhid,bhjd,bhijd->bhij", qb, kb, decay)
        o_intra = jnp.einsum("bhij,bhjv->bhiv", scores, vb)
        o_inter = jnp.einsum("bhid,bhdv->bhiv", qb * jnp.exp(g_cum), state)
        g_last = g_cum[:, :, -1:, :]
        new_state = (jnp.exp(g_last[:, :, 0, :, None]) * state
                     + jnp.einsum("bhjd,bhjv->bhdv", kb * jnp.exp(g_last - g_cum), vb))
        return new_state, o_intra + o_inter

    state0 = jnp.zeros((bsz, h, dk, dv), jnp.float32)
    _, o = lax.scan(step, state0, (to_chunks(q), to_chunks(k), to_chunks(v), to_chunks(log_a)))
    return o.transpose(1, 0, 3, 2, 4).reshape(bsz, t, h, dv).astype(v.dtype)

def hybrid_mixer(h, w_in, w_gla_gate_expand, b_gla_gate, gla_norm_g, lower_bound, hgrn_norm_g, conv_w, w_out):
    bsz, t, _ = h.shape
    proj = jnp.einsum("btd,de->bte", h, w_in)
    split_idx = np.cumsum(IN_SPLITS)[:-1].tolist()
    (gla_q, gla_k, gla_v, gla_lr, gla_og,
     hg_q, hg_f, hg_i, hg_og,
     cv_b, cv_c, cv_h) = jnp.split(proj, split_idx, axis=-1)

    q = gla_q.reshape(bsz, t, GLA_HEADS, GLA_HEAD_K) * (GLA_HEAD_K ** -0.5)
    k = gla_k.reshape(bsz, t, GLA_HEADS, GLA_HEAD_K)
    v = gla_v.reshape(bsz, t, GLA_HEADS, GLA_HEAD_V)
    gate_logits = jnp.einsum("btr,rk->btk", gla_lr, w_gla_gate_expand) + b_gla_gate
    log_a = (jax.nn.log_sigmoid(gate_logits.astype(jnp.float32)) / GLA_GATE_NORMALIZER)
    o_gla = chunk_gated_linear_attention(q, k, v, log_a.reshape(bsz, t, GLA_HEADS, GLA_HEAD_K))
    y_gla = gated_head_rmsnorm(o_gla, gla_og, gla_norm_g)

    z = hg_f.astype(jnp.float32)
    lb = lower_bound.astype(jnp.float32)
    f = lb + (1.0 - lb) * jax.nn.sigmoid(z)
    log_f = jnp.log(f)
    k_h = 1.0 - f
    q_h = jax.nn.silu(hg_q)
    o_h = chunk_gated_linear_attention(
        q_h.reshape(bsz, t, HGRN_HEADS, HGRN_HEAD_F),
        k_h.reshape(bsz, t, HGRN_HEADS, HGRN_HEAD_F),
        hg_i.reshape(bsz, t, HGRN_HEADS, HGRN_HEAD_I),
        log_f.reshape(bsz, t, HGRN_HEADS, HGRN_HEAD_F))
    y_hgrn = gated_head_rmsnorm(o_h, hg_og, hgrn_norm_g)

    u = cv_c * cv_h
    u_pad = jnp.pad(u, ((0, 0), (CONV_WIDTH - 1, 0), (0, 0)))
    conv = sum(conv_w[j] * u_pad[:, j:j + t, :] for j in range(CONV_WIDTH))
    y_conv = cv_b * conv

    y = jnp.concatenate([y_gla, y_hgrn, y_conv.astype(y_gla.dtype)], axis=-1)
    return jnp.einsum("bte,ed->btd", y, w_out)

def moe_sequence(xs, w_router, b_router, w_gate_up, b_gate_up, w_down, b_down):
    s = xs.shape[0]
    logits = jnp.einsum("sd,de->se", xs.astype(jnp.float32), w_router.astype(jnp.float32)) + b_router.astype(jnp.float32)
    top_logits, top_idx = lax.top_k(logits, TOP_K)
    gates = jax.nn.softmax(top_logits, axis=-1)
    m = s * TOP_K
    n_pad = m + N_EXPERTS * MOE_BLOCK
    n_blocks = n_pad // MOE_BLOCK
    expert_flat = top_idx.reshape(m)
    token_flat = jnp.arange(m, dtype=jnp.int32) // TOP_K
    order = jnp.argsort(expert_flat)
    expert_sorted = expert_flat[order]
    counts = jnp.zeros((N_EXPERTS,), jnp.int32).at[expert_flat].add(1)
    padded = (counts + MOE_BLOCK - 1) // MOE_BLOCK * MOE_BLOCK
    starts = jnp.cumsum(counts) - counts
    padded_ends = jnp.cumsum(padded)
    padded_starts = padded_ends - padded
    dest = padded_starts[expert_sorted] + jnp.arange(m, dtype=jnp.int32) - starts[expert_sorted]
    slot_token = jnp.zeros((n_pad,), jnp.int32).at[dest].set(token_flat[order])
    slot_gate = jnp.zeros((n_pad,), jnp.float32).at[dest].set(gates.reshape(m)[order])
    block_expert = jnp.minimum(
        jnp.searchsorted(padded_ends, jnp.arange(n_blocks, dtype=jnp.int32) * MOE_BLOCK, side="right"),
        N_EXPERTS - 1)
    x_slots = xs[slot_token].reshape(n_blocks, MOE_BLOCK, xs.shape[-1])

    def expert_block(args):
        xb, e = args
        gu = xb @ w_gate_up[e] + b_gate_up[e]
        gate, up = jnp.split(gu, 2, axis=-1)
        gate = jnp.minimum(gate, SWIGLU_LIMIT)
        up = jnp.clip(up, -SWIGLU_LIMIT, SWIGLU_LIMIT)
        act = (up + 1.0) * gate * jax.nn.sigmoid(SWIGLU_ALPHA * gate)
        return act @ w_down[e] + b_down[e]

    y_slots = lax.map(expert_block, (x_slots, block_expert)).reshape(n_pad, xs.shape[-1])
    weighted = y_slots * slot_gate[:, None].astype(y_slots.dtype)
    return jax.ops.segment_sum(weighted, slot_token, num_segments=s)

def setup_inputs(seed: int = 0) -> dict:
    key = jax.random.key(seed)
    ks = jax.random.split(key, 24)

    def nrm(k, shape, scale):
        return jax.random.normal(k, shape, jnp.float32) * scale

    L = DEPTH
    return {
        "x": nrm(ks[0], (BATCH, SEQ, D_MODEL), 1.0),
        "ln_in_g": 1.0 + nrm(ks[1], (D_MODEL,), 0.02),
        "ln_in_b": nrm(ks[2], (D_MODEL,), 0.02),
        "w_in": nrm(ks[3], (L, D_MODEL, D_IN_PROJ), D_MODEL ** -0.5),
        "w_gla_gate_expand": nrm(ks[4], (L, GLA_GATE_RANK, GLA_K_DIM), GLA_GATE_RANK ** -0.5),
        "b_gla_gate": nrm(ks[5], (L, GLA_K_DIM), 0.1),
        "gla_norm_g": 1.0 + nrm(ks[6], (L, GLA_HEAD_V), 0.02),
        "hgrn_lb_raw": nrm(ks[7], (L, HGRN_F_DIM), 0.5),
        "hgrn_norm_g": 1.0 + nrm(ks[8], (L, HGRN_HEAD_I), 0.02),
        "conv_w": nrm(ks[9], (L, CONV_WIDTH, CONV_CHANNELS), CONV_WIDTH ** -0.5),
        "w_out": nrm(ks[10], (L, D_MIX, D_MODEL), DEEPNORM_BETA * D_MIX ** -0.5),
        "ln_mix_g": 1.0 + nrm(ks[11], (L, D_MODEL), 0.02),
        "ln_mix_b": nrm(ks[12], (L, D_MODEL), 0.02),
        "w_router": nrm(ks[13], (L, D_MODEL, N_EXPERTS), D_MODEL ** -0.5),
        "b_router": nrm(ks[14], (L, N_EXPERTS), 0.01),
        "w_gate_up": nrm(ks[15], (L, N_EXPERTS, D_MODEL, 2 * D_FF), D_MODEL ** -0.5),
        "b_gate_up": nrm(ks[16], (L, N_EXPERTS, 2 * D_FF), 0.01),
        "w_down": nrm(ks[17], (L, N_EXPERTS, D_FF, D_MODEL), DEEPNORM_BETA * D_FF ** -0.5),
        "b_down": nrm(ks[18], (L, N_EXPERTS, D_MODEL), 0.01),
        "ln_ffn_g": 1.0 + nrm(ks[19], (L, D_MODEL), 0.02),
        "ln_ffn_b": nrm(ks[20], (L, D_MODEL), 0.02),
    }

def reference(x, ln_in_g, ln_in_b, w_in, w_gla_gate_expand, b_gla_gate, gla_norm_g, hgrn_lb_raw,
              hgrn_norm_g, conv_w, w_out, ln_mix_g, ln_mix_b, w_router, b_router, w_gate_up,
              b_gate_up, w_down, b_down, ln_ffn_g, ln_ffn_b):
    lb_p = jax.nn.softmax(hgrn_lb_raw.astype(jnp.float32), axis=0)
    lower_bounds = jnp.cumsum(lb_p, axis=0) - lb_p[0]

    h = layer_norm(x, ln_in_g, ln_in_b)
    for l in range(DEPTH):
        mix = hybrid_mixer(h, w_in[l], w_gla_gate_expand[l], b_gla_gate[l], gla_norm_g[l],
                           lower_bounds[l], hgrn_norm_g[l], conv_w[l], w_out[l])
        h = layer_norm(DEEPNORM_ALPHA * h + mix, ln_mix_g[l], ln_mix_b[l])
        ffn = lax.map(lambda xs: moe_sequence(xs, w_router[l], b_router[l], w_gate_up[l],
                                               b_gate_up[l], w_down[l], b_down[l]), h)
        h = layer_norm(DEEPNORM_ALPHA * h + ffn.astype(h.dtype), ln_ffn_g[l], ln_ffn_b[l])
    return h


_drawn_inputs = setup_inputs


def setup_inputs(seed=0):
    import zlib

    import numpy as np

    out = dict(_drawn_inputs(seed))
    spreads = {}
    factors = {'b_gla_gate': 2.88,
     'gla_norm_g': 5.996,
     'hgrn_norm_g': 7.469,
     'b_router': 4.016,
     'b_gate_up': 8.0,
     'b_down': 8.0,
     'ln_ffn_g': 2.831,
     'ln_ffn_b': 2.949}
    for name, (base, spread) in spreads.items():
        noise = np.random.default_rng([zlib.crc32(name.encode()), seed]).standard_normal(out[name].shape)
        drawn = base * np.exp(spread * noise) if base else spread * noise
        out[name] = __import__('jax').numpy.asarray(drawn.astype(out[name].dtype))
    for name, factor in factors.items():
        out[name] = (out[name] * factor).astype(out[name].dtype)
    return out
```

```python
from contextlib import ExitStack

import concourse.bass as bass
from concourse import mybir
import numpy as np

F32 = mybir.dt.float32
F32R = mybir.dt.float32r
I32 = mybir.dt.int32
U32 = mybir.dt.uint32
ACT = mybir.ActivationFunctionType
ALU = mybir.AluOpType
AX = mybir.AxisListType

P = 128
SEQ = 1024
D = 1024
KT = D // P
NT = SEQ // P
GLA_H, GLA_K, GLA_V, RANK = 4, D // 16, D // 8, 16
HG_H, HG_F, HG_I = 4, D // 16, D // 16
CONV_C, CONV_W = D // 4, 3
NE, TOPK, DFF = 32, 4, D
LN_EPS, RMS_EPS = 1e-5, 1e-6
ALPHA = 2.0 ** 0.25
SWIGLU_LIMIT, SWIGLU_ALPHA = 7.0, 1.702
CC = 256
NFM = 7
NTM = 6


class Kit:

    def __init__(self, nc, stack):
        self.nc, self.stack = nc, stack

    def sb(self, name, shape, dt=F32):
        return self.stack.enter_context(self.nc.sbuf_tensor(name, shape, dt))

    def ps(self, name, shape, dt=F32):
        return self.stack.enter_context(self.nc.psum_tensor(name, shape, dt))

    def sem(self, name):
        return self.stack.enter_context(self.nc.semaphore(name))


def project(nc, a, keep):
    with ExitStack() as stack:
        k = Kit(nc, stack)
        x_all = k.sb("x_all", [P, NT, D])
        hbuf = k.sb("hbuf", [P, 2, D])
        lng = k.sb("lng", [P, D])
        lnb = k.sb("lnb", [P, D])
        stat = k.sb("stat", [P, NT, 2, 6])
        mv = k.sb("mv", [P, NT, 2])
        rstd = k.sb("rstd", [P, NT])
        shift = k.sb("shift", [P, NT])
        hT_hi = k.sb("hT_hi", [P, KT, SEQ], F32R)
        hT_lo = k.sb("hT_lo", [P, KT, SEQ], F32R)
        w_raw = k.sb("w_raw", [P, 2, KT, CC])
        w_hi = k.sb("w_hi", [P, 2, KT, CC], F32R)
        w_lo = k.sb("w_lo", [P, 2, KT, CC], F32R)
        stage = x_all
        wlr = k.sb("wlr", [P, KT, RANK])
        ps = k.ps("psA", [P, 8, 512])
        s_ln, s_wlr = k.sem("ln_params_loaded"), k.sem("wlr_loaded")
        s_x = [k.sem(f"x_half{p}_loaded") for p in range(2)]
        s_w = [k.sem(f"w_raw{p}_loaded") for p in range(2)]
        s_hout = [k.sem(f"hbuf{p}_stored") for p in range(2)]
        s_out = [k.sem(f"stage{p}_stored") for p in range(2)]
        s_st, s_mv, s_ve, s_sq, s_rs = (k.sem(n) for n in ("stats_done", "mean_var_done", "var_eps_done", "sqrt_done", "shift_done"))
        s_xg, s_h = k.sem("x_times_g"), k.sem("h_ready")
        s_tp, s_hi, s_lo = k.sem("h_transposed"), k.sem("hT_hi_ready"), k.sem("hT_lo_ready")
        s_whi, s_wlo = k.sem("w_hi_ready"), k.sem("w_lo_ready")
        s_mm, s_ev = k.sem("chunk_multiplied"), k.sem("chunk_evacuated")
        s_lr = k.sem("lr_multiplied")
        n_chunks = NFM + NTM
        half = NT // 2

        def ps_tp(p):
            return ps[:, 2 * p:2 * p + 2, :].rearrange("p a (b c) -> p (a b) c", c=P)

        def w_high(act, m, p, again=False):
            j = m * 2 + p
            act.wait_ge(s_w[p], m * 16 + 16)
            if again:
                act.wait_ge(s_mm, j - 1)
            nc.scalar.copy(w_hi[:, p], w_raw[:, p]).then_inc(s_whi, 1)

        def w_low(dve, m, p):
            j = m * 2 + p
            dve.wait_ge(s_whi, j + 1)
            nc.vector.tensor_tensor(w_lo[:, p], w_raw[:, p], w_hi[:, p].bitcast(F32), ALU.subtract).then_inc(s_wlo, 1)

        def evacuate(act, m, p, feature, first=False):
            j = m * 2 + p
            """PSUM to the stage, and the stage to DRAM."""
            act.wait_ge(s_mm, j + 1)
            if not first:
                act.wait_ge(s_out[p], m * 16)
            dst = stage[:, 2 * p:2 * p + 2, :]
            nc.scalar.copy(dst.rearrange("p a b -> p (a b)"), ps[:, 4 * p:4 * p + 4, :].rearrange("p a b -> p (a b)")).then_inc(s_ev, 1)
            act.wait_ge(s_ev, j + 1)
            if feature:
                act.dma_start(a["projT_d"][bass.ds(j * CC, CC), :].rearrange("(f p) t -> p f t", p=P), dst).then_inc(s_out[p], 16)
            else:
                act.dma_start(a["projM_d"][:, bass.ds(j * CC - NFM * CC, CC)].rearrange("(t p) c -> p t c", p=P),
                              dst.rearrange("p a (b c) -> p (a b) c", c=CC)).then_inc(s_out[p], 16)

        with nc.Block() as block:
            @block.sync
            def _(sp):
                for q in range(2):
                    sp.dma_start(x_all[:, q * half:(q + 1) * half, :],
                                 a["x"][q * half * P:(q + 1) * half * P, :].rearrange("(t p) d -> p t d", p=P)).then_inc(s_x[q], 16)
                sp.dma_start(lng[:], a["ln_in_g"].partition_broadcast(P)).then_inc(s_ln, 16)
                sp.dma_start(lnb[:], a["ln_in_b"].partition_broadcast(P)).then_inc(s_ln, 16)
                sp.dma_start(wlr[:], a["w_lr"]).then_inc(s_wlr, 16)
                for j in range(2):
                    sp.dma_start(w_raw[:, j], a["w_cols"][j]).then_inc(s_w[j % 2], 16)
                with sp.Fori(0, half) as i:
                    for p in range(2):
                        sp.wait_ge(s_h, i * 2 + p + 1)
                        sp.dma_start(a["h_d"][bass.ds(i * 2 * P + p * P, P), :], hbuf[:, p]).then_inc(s_hout[p], 16)
                for j in range(2, n_chunks):
                    sp.wait_ge(s_wlo, j - 1)
                    sp.dma_start(w_raw[:, j % 2], a["w_cols"][j]).then_inc(s_w[j % 2], 16)
                for p in range(2):
                    sp.wait_ge(s_hout[p], 16 * half)

            @block.vector
            def _(dve):
                for t in range(NT):
                    dve.wait_ge(s_x[t // half], 16)
                    for c in range(2):
                        nc.vector.bn_stats(stat[:, t, c, :], x_all[:, t, c * 512:(c + 1) * 512]).then_inc(s_st, 1)
                dve.wait_ge(s_st, 2 * NT)
                for t in range(NT):
                    nc.vector.bn_aggr(mv[:, t, :], stat[:, t]).then_inc(s_mv, 1)
                dve.wait_ge(s_mv, NT)
                nc.vector.tensor_scalar(rstd[:], mv[:, :, 1], LN_EPS, None, ALU.add).then_inc(s_ve, 1)
                dve.wait_ge(s_sq, 1)
                nc.vector.reciprocal(rstd[:], rstd[:]).then_inc(s_rs, 1)
                dve.wait_ge(s_rs, 1)
                dve.wait_ge(s_ln, 32)

                def normalise(t, p):
                    x = x_all[:, bass.ds(t, 1), :].rearrange("p a b -> p (a b)")
                    nc.vector.scalar_tensor_tensor(x, x, mv[:, bass.ds(t, 1), 0], lng[:], ALU.subtract, ALU.mult).then_inc(s_xg, 1)
                    dve.wait_ge(s_xg, t + 1)
                    nc.vector.scalar_tensor_tensor(hbuf[:, p], x, rstd[:, bass.ds(t, 1)], lnb[:], ALU.mult, ALU.add).then_inc(s_h, 1)

                def low_part(t, p):
                    dve.wait_ge(s_hi, t + 1)
                    nc.vector.tensor_tensor(hT_lo[:, :, bass.ds(t * P, P)], ps_tp(p),
                                            hT_hi[:, :, bass.ds(t * P, P)].bitcast(F32), ALU.subtract).then_inc(s_lo, 1)

                for p in range(2):
                    normalise(p, p)
                with dve.Fori(1, NT // 2) as i:
                    for p in range(2):
                        low_part(i * 2 + p - 2, p)
                        dve.wait_ge(s_hout[p], i * 16)
                        normalise(i * 2 + p, p)
                for p in range(2):
                    low_part(NT - 2 + p, p)
                with dve.Fori(0, n_chunks // 2) as i:
                    for p in range(2):
                        w_low(dve, i, p)
                w_low(dve, n_chunks // 2, 0)

            @block.scalar
            def _(act):
                act.wait_ge(s_ve, 1)
                nc.scalar.activation(rstd[:], rstd[:], ACT.Sqrt).then_inc(s_sq, 1)
                with act.Fori(0, NT // 2) as i:
                    for p in range(2):
                        act.wait_ge(s_tp, i * 2 + p + 1)
                        nc.scalar.copy(hT_hi[:, :, bass.ds(i * 2 * P + p * P, P)], ps_tp(p)).then_inc(s_hi, 1)
                for p in range(2):
                    w_high(act, 0, p)
                for p in range(2):
                    evacuate(act, 0, p, True, first=True)
                    w_high(act, 1, p, True)
                with act.Fori(1, NFM // 2) as m:
                    for p in range(2):
                        evacuate(act, m, p, True)
                        w_high(act, m + 1, p, True)
                evacuate(act, NFM // 2, 0, True)
                w_high(act, NFM // 2 + 1, 0, True)
                with act.Fori(NFM // 2, n_chunks // 2 - 1) as m:
                    evacuate(act, m, 1, False)
                    w_high(act, m + 1, 1, True)
                    evacuate(act, m + 1, 0, False)
                    w_high(act, m + 2, 0, True)
                evacuate(act, n_chunks // 2 - 1, 1, False)
                evacuate(act, n_chunks // 2, 0, False)
                act.wait_ge(s_lr, 1)
                nc.scalar.copy(stage[0:RANK, 6, :], ps[0:RANK, 4:6, :].rearrange("p a b -> p (a b)")).then_inc(s_ev, 1)
                act.wait_ge(s_ev, n_chunks + 1)
                act.dma_start(a["lrT_d"], stage[0:RANK, 6, :]).then_inc(s_out[1], 16)
                act.wait_ge(s_out[0], 16 * (n_chunks // 2 + 1))
                act.wait_ge(s_out[1], 16 * (n_chunks // 2 + 1))

            @block.tensor
            def _(pe):
                pe.wait_ge(a["consts_loaded"], 16)

                def transpose_tile(t, p, first):
                    pe.wait_ge(s_h, t + 1)
                    if not first:
                        pe.wait_ge(s_lo, t - 1)
                    for kt in range(KT):
                        last = nc.tensor.transpose(ps_tp(p)[:, kt, :], hbuf[:, p, kt * P:(kt + 1) * P], a["ident"][:])
                    last.then_inc(s_tp, 1)

                for p in range(2):
                    transpose_tile(p, p, True)
                with pe.Fori(1, NT // 2) as i:
                    for p in range(2):
                        transpose_tile(i * 2 + p, p, False)
                pe.wait_ge(s_lo, NT)

                def feature_major(j, p, first=False):
                    pe.wait_ge(s_wlo, j + 1)
                    if not first:
                        pe.wait_ge(s_ev, j - 1)
                    for ft in range(2):
                        for kt in range(KT):
                            w = slice(ft * P, (ft + 1) * P)
                            for n, (wt, ht) in enumerate(((w_hi, hT_hi), (w_hi, hT_lo), (w_lo, hT_hi))):
                                for h in range(2):
                                    last = nc.tensor.matmul(ps[:, p * 4 + ft * 2 + h, :], wt[:, p, kt, w], ht[:, kt, h * 512:(h + 1) * 512],
                                                            start=(kt == 0 and n == 0), stop=(kt == KT - 1 and n == 2))
                    last.then_inc(s_mm, 1)

                def token_major(j, p):
                    pe.wait_ge(s_wlo, j + 1)
                    pe.wait_ge(s_ev, j - 1)
                    for t in range(NT):
                        for kt in range(KT):
                            for n, (wt, ht) in enumerate(((w_hi, hT_hi), (w_lo, hT_hi), (w_hi, hT_lo))):
                                last = nc.tensor.matmul(ps[:, p * 4 + t // 2, (t % 2) * CC:(t % 2 + 1) * CC], ht[:, kt, t * P:(t + 1) * P],
                                                        wt[:, p, kt, :], start=(kt == 0 and n == 0), stop=(kt == KT - 1 and n == 2))
                    last.then_inc(s_mm, 1)

                for p in range(2):
                    feature_major(p, p, True)
                with pe.Fori(1, (NFM - 1) // 2) as i:
                    for p in range(2):
                        feature_major(i * 2 + p, p)
                feature_major(NFM - 1, 0)
                with pe.Fori(0, NTM // 2) as i:
                    for p in (1, 0):
                        token_major(i * 2 + (NFM + 1 - p), p)
                pe.wait_ge(s_wlr, 16)
                pe.wait_ge(s_ev, n_chunks - 1)
                for h in range(2):
                    for kt in range(KT):
                        for n, (wt, ht) in enumerate(((wlr, hT_hi), (wlr, hT_lo))):
                            last = nc.tensor.matmul(ps[0:RANK, 4 + h, :], wt[:, kt, :], ht[:, kt, h * 512:(h + 1) * 512].bitcast(F32),
                                                    start=(kt == 0 and n == 0), stop=(kt == KT - 1 and n == 1))
                last.then_inc(s_lr, 1)


NG = 4
LEVELS = 7
CH = P


def group_dv(g):
    return GLA_V if g < 2 else HG_I


def group_cols(g):
    return slice(2 * GLA_V * g, 2 * GLA_V * (g + 1)) if g < 2 else \
        slice(GLA_H * GLA_V + 2 * HG_I * (g - 2), GLA_H * GLA_V + 2 * HG_I * (g - 1))


def group_scale(g):
    return 1.0 / 16.0 if g < 2 else 1.0


def mix(nc, a, v_all, q_all, k_all, G, EG):
    with ExitStack() as stack:
        k = Kit(nc, stack)
        KL = k.sb("KL", [P, 2, LEVELS, SEQ])
        QL = k.sb("QL", [P, 2, LEVELS, SEQ // 2])
        QH = k.sb("QH", [P, 2, SEQ])
        KH = k.sb("KH", [P, 2, SEQ])
        E = k.sb("E", [P, 2, SEQ])
        EF = k.sb("EF", [P, SEQ])
        S = k.sb("S", [P, 2, 2, CH])
        khat = k.sb("khat", [P, 2, P])
        state = k.sb("state", [P, 2, 2, 2 * GLA_V])
        masks = k.sb("masks", [P, 6, CH // 2], I32)
        diag = k.sb("diag", [P, CH], I32)
        psX = k.ps("psX", [P, 2, 2, 512])
        psC = k.ps("psC", [P, 2, 512])
        psO = k.ps("psO", [P, 512])
        psU = k.ps("psU", [P, 512])
        s_zero, s_mask = k.sem("zeroed"), k.sem("masks_loaded")
        s_sub, s_exp, s_qm, s_km = k.sem("exponents_ready"), k.sem("decays_ready"), k.sem("q_decayed"), k.sem("k_decayed")
        s_sc, s_xd, s_xa, s_ap, s_st, s_o = (k.sem(n) for n in (
            "scores_done", "fine_levels_copied", "coarse_levels_copied", "chunk_applied", "state_ready", "o_ready"))
        s_lv = k.sem("level_copied")
        zrow = k.sb("zrow", [P, D])
        s_zrow, s_yz = k.sem("zero_row_ready"), k.sem("y_overflow_zeroed")
        steps = NG * NT

        def halves(x, level):
            return x.rearrange("p (b h s) -> p b h s", h=2, s=1 << level)

        def exponents(g, item):
            m = 8 * g + item
            if m >= 2:
                nc.vector.wait_ge(s_km, m - 1)
                nc.vector.wait_ge(s_qm, m - 1)
            e = E[:, item % 2]
            if item == 0:
                gc = G[:, g].rearrange("p (c t) -> p c t", t=CH)
                nc.vector.tensor_tensor(e.rearrange("p (c t) -> p c t", t=CH), gc[:, :, CH - 1:CH].broadcast_to((P, NT, CH)), gc,
                                        ALU.subtract).then_inc(s_sub, 1)
                return
            level, s = item - 1, 1 << (item - 1)
            gh, eh = halves(G[:, g], level), halves(e, level)
            ref = gh[:, :, 0, s - 1:s].broadcast_to((P, SEQ // (2 * s), s))
            nc.vector.tensor_tensor(eh[:, :, 0, :], ref, gh[:, :, 0, :], ALU.subtract)
            nc.vector.tensor_tensor(eh[:, :, 1, :], gh[:, :, 1, :], ref, ALU.subtract).then_inc(s_sub, 1)

        def decay_q(g, item):
            nc.vector.wait_ge(s_exp, 8 * g + item + 1)
            if item == 0:
                nc.vector.tensor_tensor(QH[:, g % 2], q_all[:, g], EF[:], ALU.mult).then_inc(s_qm, 1)
                return
            level, s = item - 1, 1 << (item - 1)
            nc.vector.tensor_tensor(QL[:, g % 2, level].rearrange("p (b s) -> p b s", s=s), halves(q_all[:, g], level)[:, :, 1, :],
                                    halves(E[:, item % 2], level)[:, :, 1, :], ALU.mult).then_inc(s_qm, 1)

        with nc.Block() as block:
            @block.sync
            def _(sp):
                sp.dma_start(masks[:], a["level_masks"]).then_inc(s_mask, 16)
                sp.dma_start(diag[:], a["diag_mask"]).then_inc(s_mask, 16)
                sp.wait_ge(s_zrow, 1)
                over = a["y_d"][NE * CAP:, :]
                n = NB_OVER * CAP // P
                sp.dma_start(over[0:n * P].rearrange("(n p) d -> p n d", p=P), zrow[:].unsqueeze(1).broadcast_to((P, n, D))).then_inc(s_yz, 16)
                sp.dma_start(over[n * P:], zrow[0:NB_OVER * CAP - n * P]).then_inc(s_yz, 16)
                sp.wait_ge(s_yz, 32)

            @block.gpsimd
            def _(pool):
                nc.gpsimd.memset(zrow[:], 0.0).then_inc(s_zrow, 1)
                nc.gpsimd.memset(S[:], 0.0).then_inc(s_zero, 1)
                nc.gpsimd.memset(KL[:], 0.0).then_inc(s_zero, 1)
                nc.gpsimd.memset(state[:], 0.0).then_inc(s_zero, 1)
                pool.wait_ge(s_zero, 3)
                for g in range(NG):
                    if g >= 2:
                        pool.wait_ge(s_ap, NT * (g - 1))
                    for item in range(8):
                        pool.wait_ge(s_exp, 8 * g + item + 1)
                        if item == 0:
                            nc.gpsimd.tensor_tensor(KH[:, g % 2], k_all[:, g], E[:, 0], ALU.mult).then_inc(s_km, 1)
                        else:
                            nc.gpsimd.tensor_tensor(halves(KL[:, g % 2, item - 1], item - 1)[:, :, 0, :], halves(k_all[:, g], item - 1)[:, :, 0, :],
                                                    halves(E[:, item % 2], item - 1)[:, :, 0, :], ALU.mult).then_inc(s_km, 1)

            @block.vector
            def _(dve):
                def prepare(g, step):
                    if step < 8:
                        exponents(g, step)
                    if step > 0:
                        decay_q(g, step - 1)

                for step in range(9):
                    prepare(0, step)
                dve.wait_ge(s_zero, 3)
                dve.wait_ge(s_mask, 32)
                for n in range(steps):
                    g, c, p = n // NT, n % NT, n % 2
                    dve.wait_ge(s_sc, n + 1)
                    for level in range(6):
                        s = 1 << level
                        out = S[:, p].rearrange("p n (b h s) -> p n b h s", h=2, s=s)[:, :, :, 1, :]
                        mask = masks[:, level].rearrange("p (b s) -> p b s", s=s).unsqueeze(1).broadcast_to((P, 2, CH // (2 * s), s))
                        src = psX[:, p, :, level * 64:level * 64 + 64].rearrange("p n (b s) -> p n b s", s=s)
                        nc.vector.copy_predicated(out, mask, src).then_inc(s_lv, 1)
                        dve.wait_ge(s_lv, 6 * n + level + 1)
                    nc.vector.copy_predicated(S[:, p], diag[:].unsqueeze(1).broadcast_to((P, 2, CH)),
                                              psX[:, p, :, 6 * 64:6 * 64 + CH]).then_inc(s_xd, 1)
                    if g + 1 < NG:
                        if c == 0 and g >= 1:
                            dve.wait_ge(s_ap, NT * g)
                        prepare(g + 1, c)
                        if c == NT - 1:
                            prepare(g + 1, NT)
                    dv = group_dv(g)
                    dve.wait_ge(s_ap, n + 1)
                    if c:
                        dve.wait_ge(s_st, n)
                    for h in range(2):
                        f, cols = slice(64 * h, 64 * h + 64), slice(h * dv, (h + 1) * dv)
                        new, update = state[f, g // 2, p, cols], psU[f, cols]
                        if c == 0:
                            last = nc.vector.tensor_copy(new, update)
                        else:
                            last = nc.vector.scalar_tensor_tensor(new, state[f, g // 2, 1 - p, cols], EG[f, g, c:c + 1], update, ALU.mult, ALU.add)
                    last.then_inc(s_st, 1)

            @block.scalar
            def _(act):
                def decays(g, item):
                    act.wait_ge(s_sub, 8 * g + item + 1)
                    if item == 0:
                        if g:
                            act.wait_ge(s_qm, 8 * g - 7)
                        nc.scalar.activation(EF[:], G[:, g], ACT.Exp, scale=group_scale(g))
                    nc.scalar.activation(E[:, item % 2], E[:, item % 2], ACT.Exp, scale=group_scale(g)).then_inc(s_exp, 1)

                for item in range(8):
                    decays(0, item)
                act.wait_ge(s_zero, 3)
                for n in range(steps):
                    g, c, p = n // NT, n % NT, n % 2
                    act.wait_ge(s_sc, n + 1)
                    if n >= 2:
                        act.wait_ge(s_ap, n - 1)
                    nc.scalar.copy(khat[:, p], psC[:, 0, 64:64 + P])
                    act.wait_ge(s_xd, n + 1)
                    nc.scalar.copy(S[0:64, p, :, 64:128], psC[0:64, :, 0:64]).then_inc(s_xa, 1)
                    if g + 1 < NG:
                        decays(g + 1, c)
                    act.wait_ge(s_ap, n + 1)
                    nc.scalar.copy(v_all[:, c, group_cols(g)], psO[:, 0:2 * group_dv(g)]).then_inc(s_o, 1)

            @block.tensor
            def _(pe):
                def scores(n):
                    g, c, p = n // NT, n % NT, n % 2
                    pe.wait_ge(s_qm, 8 * g + 8)
                    pe.wait_ge(s_km, 8 * g + 8)
                    if n >= 2:
                        pe.wait_ge(s_xd, n - 1)
                    t = slice(c * CH, (c + 1) * CH)

                    def level_scores(out, level):
                        nc.tensor.matmul(out, KL[f, g % 2, level, t], QL[f, g % 2, level, c * 64:c * 64 + 64], start=True, stop=True)

                    for h in range(2):
                        f = slice(64 * h, 64 * h + 64)
                        for level in range(6):
                            level_scores(psX[:, p, h, level * 64:level * 64 + 64], level)
                        nc.tensor.matmul(psX[:, p, h, 6 * 64:6 * 64 + CH], k_all[f, g, t], q_all[f, g, t], start=True, stop=True)
                    if n >= 1:
                        pe.wait_ge(s_xa, n)
                    for h in range(2):
                        f = slice(64 * h, 64 * h + 64)
                        level_scores(psC[:, h, 0:64], 6)
                    nc.tensor.transpose(psC[:, 0, 64:64 + P], KH[:, g % 2, t], a["ident"][:]).then_inc(s_sc, 1)

                def apply(n):
                    g, c, p = n // NT, n % NT, n % 2
                    dv = group_dv(g)
                    v = v_all[:, c, group_cols(g)]
                    pe.wait_ge(s_xd, n + 1)
                    pe.wait_ge(s_xa, n + 1)
                    if n >= 1:
                        pe.wait_ge(s_o, n)
                        pe.wait_ge(s_st, n)
                    if c:
                        nc.tensor.matmul(psO[:, 0:2 * dv], QH[:, g % 2, c * CH:(c + 1) * CH], state[:, g // 2, 1 - p, 0:2 * dv],
                                         start=True, stop=False)
                    for h in range(2):
                        cols = slice(h * dv, (h + 1) * dv)
                        nc.tensor.matmul(psO[:, cols], S[:, p, h], v[:, cols], start=(c == 0), stop=(c == 0 or h == 1))
                    nc.tensor.matmul(psU[:, 0:2 * dv], khat[:, p], v, start=True, stop=True).then_inc(s_ap, 1)

                scores(0)
                for n in range(steps):
                    if n + 1 < steps:
                        scores(n + 1)
                    apply(n)


def gates(nc, a, v_all, q_all, k_all, G, EG):
    with ExitStack() as stack:
        k = Kit(nc, stack)
        lrT = k.sb("lrT", [RANK, SEQ])
        expand = k.sb("expand", [RANK, GLA_H * GLA_K])
        col = k.sb("col", [P, 4])
        lb = k.sb("lb", [P, 6])
        tmp = k.sb("tmp", [P, 4])
        T = k.sb("T", [P, 3, 2 * SEQ])
        restart = k.sb("restart", [P, SEQ])
        ps = k.ps("psG", [P, 2, SEQ])
        s_par, s_q, s_k, s_v = k.sem("params_loaded"), k.sem("q_loaded"), k.sem("k_loaded"), k.sem("v_loaded")
        s_z, s_d, s_a, s_a2 = k.sem("logits_ready"), k.sem("dve_steps"), k.sem("act_steps"), k.sem("exp_ready")
        flat = lambda x: x.rearrange("p a b -> p (a b)")
        z, u, t = T[:, 0], T[:, 1], T[:, 2]
        row = lambda x, f: x[:, f * SEQ:(f + 1) * SEQ]

        with nc.Block() as block:
            @block.sync
            def _(sp):
                for dst, src in ((lrT, "lrT_d"), (expand, "w_expand"), (restart, "restart_c")):
                    sp.dma_start(dst[:], a[src]).then_inc(s_par, 16)
                sp.dma_start(col[:], a["gate_cols"]).then_inc(s_par, 16)
                rows = lambda r: a["projT_d"][r:r + 2 * P, :].rearrange("(f p) t -> p f t", p=P)
                sp.dma_start(k_all[:, 2:4, :], rows(768)).then_inc(s_k, 16)
                sp.dma_start(q_all[:, 2:4, :], rows(512)).then_inc(s_q, 16)
                sp.dma_start(q_all[:, 0:2, :], rows(0)).then_inc(s_q, 16)
                sp.dma_start(k_all[:, 0:2, :], rows(256)).then_inc(s_v, 16)
                m = a["projM_d"].rearrange("(t p) c -> p t c", p=P)
                sp.dma_start(v_all[:, :, 0:512], m[:, :, 0:512]).then_inc(s_v, 16)
                sp.dma_start(v_all[:, :, 512:768], m[:, :, 1024:1280]).then_inc(s_v, 16)
                sp.wait_ge(s_v, 48)

            @block.tensor
            def _(pe):
                pe.wait_ge(s_par, 64)
                for f in range(2):
                    for h in range(2):
                        last = nc.tensor.matmul(ps[:, f, h * 512:(h + 1) * 512], expand[:, f * P:(f + 1) * P], lrT[:, h * 512:(h + 1) * 512],
                                                start=True, stop=True)
                last.then_inc(s_z, 1)

            done = {"dve": 0, "act": 0}

            @block.vector
            def _(dve):
                def step(ins, wait=True):
                    done["dve"] += 1
                    ins.then_inc(s_d, 1)
                    if wait:
                        dve.wait_ge(s_d, done["dve"])

                dve.wait_ge(s_par, 64)
                step(nc.vector.tensor_tensor(tmp[:, 0:2], col[:, 2:4], col[:, 2:4], ALU.subtract))
                dve.wait_ge(s_a, 1)
                step(nc.vector.reciprocal(tmp[:, 2:4], tmp[:, 0:2]))
                step(nc.vector.tensor_tensor(tmp[:, 0:2], tmp[:, 0:2], tmp[:, 2:4], ALU.mult))
                step(nc.vector.tensor_tensor(lb[:, 0:2], tmp[:, 0:2], tmp[:, 0:2], ALU.subtract))
                step(nc.vector.tensor_scalar(lb[:, 2:4], lb[:, 0:2], -1.0, 1.0, ALU.mult, ALU.add))
                step(nc.vector.tensor_scalar(lb[:, 4:6], lb[:, 2:4], -1.0, None, ALU.mult))
                dve.wait_ge(s_k, 16)
                step(nc.vector.scalar_tensor_tensor(t, flat(k_all[:, 2:4]), -1.0, flat(k_all[:, 2:4]), ALU.mult, ALU.min), False)
                dve.wait_ge(s_z, 1)
                for f in range(2):
                    step(nc.vector.tensor_scalar(row(z, f), ps[:, f], col[:, f:f + 1], None, ALU.add))
                dve.wait_ge(s_a, 2)
                step(nc.vector.scalar_tensor_tensor(u, flat(k_all[:, 2:4]), 0.0, t, ALU.min, ALU.subtract))
                step(nc.vector.tensor_scalar(t, u, -1.0, 80.0, ALU.mult, ALU.min))
                dve.wait_ge(s_a, 4)
                for f in range(2):
                    step(nc.vector.tensor_scalar(k_all[:, 2 + f], k_all[:, 2 + f], lb[:, 4 + f:5 + f], lb[:, 2 + f:3 + f], ALU.mult, ALU.add), False)
                    step(nc.vector.tensor_scalar(row(t, f), row(t, f), -1.0, lb[:, f:f + 1], ALU.add, ALU.mult))
                dve.wait_ge(s_a, 5)
                step(nc.vector.tensor_tensor(u, u, t, ALU.add))
                for f in range(2):
                    step(nc.vector.tensor_tensor_scan(G[:, 2 + f], restart[:], row(u, f), 0.0, ALU.mult, ALU.add))
                step(nc.vector.scalar_tensor_tensor(t, z, -1.0, z, ALU.mult, ALU.min))
                dve.wait_ge(s_a, 6)
                step(nc.vector.scalar_tensor_tensor(u, z, 0.0, t, ALU.min, ALU.subtract))
                for f in range(2):
                    step(nc.vector.tensor_tensor_scan(G[:, f], restart[:], row(u, f), 0.0, ALU.mult, ALU.add))
                dve.wait_ge(s_q, 32)
                step(nc.vector.tensor_scalar(q_all[:, 0:2], q_all[:, 0:2], GLA_K ** -0.5, None, ALU.mult), False)
                dve.wait_ge(s_a, 7)
                step(nc.vector.tensor_scalar(z, z, 1.0, None, ALU.add))
                step(nc.vector.reciprocal(z, z))
                step(nc.vector.tensor_tensor(flat(q_all[:, 2:4]), flat(q_all[:, 2:4]), z, ALU.mult))

            @block.scalar
            def _(act):
                def step(ins):
                    done["act"] += 1
                    ins.then_inc(s_a, 1)
                    act.wait_ge(s_a, done["act"])

                act.wait_ge(s_d, 1)
                step(nc.scalar.activation(tmp[:, 0:2], tmp[:, 0:2], ACT.Exp))
                act.wait_ge(s_d, 7)
                nc.scalar.activation(t, t, ACT.Exp).then_inc(s_a2, 1)
                act.wait_ge(s_a2, 1)
                step(nc.scalar.activation(t, t, ACT.Ln, bias=1.0))
                act.wait_ge(s_d, 11)
                step(nc.scalar.activation(flat(k_all[:, 2:4]), u, ACT.Exp))
                step(nc.scalar.activation(t, t, ACT.Exp))
                act.wait_ge(s_d, 15)
                step(nc.scalar.activation(t, t, ACT.Ln, bias=1.0))
                act.wait_ge(s_d, 19)
                nc.scalar.activation(t, t, ACT.Exp).then_inc(s_a2, 1)
                act.wait_ge(s_a2, 2)
                step(nc.scalar.activation(t, t, ACT.Ln, bias=1.0))
                act.wait_ge(s_d, 20)
                act.wait_ge(s_q, 32)
                step(nc.scalar.activation(z, flat(q_all[:, 2:4]), ACT.Exp, scale=-1.0))
                act.wait_ge(s_d, 22)
                last = G[:].rearrange("p g (c t) -> p g c t", t=CH)[:, :, :, CH - 1]
                nc.scalar.activation(EG[:, 0:2], last[:, 0:2], ACT.Exp, scale=group_scale(0))
                nc.scalar.activation(EG[:, 2:4], last[:, 2:4], ACT.Exp)


def mixers(nc, a):
    with ExitStack() as outer:
        v_all = Kit(nc, outer).sb("v_all", [P, NT, 768])
        with ExitStack() as stack:
            k = Kit(nc, stack)
            q_all, k_all, G = (k.sb(n, [P, NG, SEQ]) for n in ("q_all", "k_all", "G"))
            EG = k.sb("EG", [P, NG, NT])
            gates(nc, a, v_all, q_all, k_all, G, EG)
            mix(nc, a, v_all, q_all, k_all, G, EG)
        with ExitStack() as stack:
            k = Kit(nc, stack)
            yT_hi = k.sb("yT_hi", [P, KT, SEQ], F32R)
            yT_lo = k.sb("yT_lo", [P, KT, SEQ], F32R)
            mixer_outputs(nc, a, v_all, yT_hi, yT_lo)
            project_out(nc, a, yT_hi, yT_lo)


def mixer_outputs(nc, a, o_all, yT_hi, yT_lo):
    with ExitStack() as stack:
        k = Kit(nc, stack)
        gate = k.sb("out_gate", [P, NT, 768])
        gn = k.sb("gn", [P, 768])
        sq = k.sb("sq", [P, 2, 768])
        ms = k.sb("ms", [P, NT, 8])
        cv = k.sb("cv", [P, 4, SEQ])
        u = k.sb("u", [P, SEQ])
        cw = k.sb("cw", [P, 2, CONV_W])
        ps = k.ps("psY", [P, 2, 1024])
        s_g, s_p = k.sem("gates_loaded"), k.sem("norm_params_loaded")
        s_cv = [k.sem(f"conv{f}_loaded") for f in range(2)]
        s_silu, s_sq, s_ms, s_d, s_sqrt, s_rms = (k.sem(n) for n in (
            "silu_done", "squared", "sums_done", "dve_steps", "sqrt_done", "rms_ready"))
        s_n, s_y, s_tp, s_hi, s_lo = (k.sem(n) for n in ("normed", "y_ready", "y_transposed", "yT_hi_ready", "yT_lo_ready"))
        s_gn = k.sem("gates_scaled")
        s_cs, s_chi, s_clo = k.sem("conv_steps"), k.sem("conv_hi_ready"), k.sem("conv_lo_ready")
        heads = lambda x, part: (x[:, 0:512] if part == 0 else x[:, 512:768]).rearrange("p (n d) -> p n d", n=4)

        def ps_tile(p):
            return ps[:, p, 0:768].rearrange("p (f t) -> p f t", t=P)

        with nc.Block() as block:
            @block.sync
            def _(sp):
                m = a["projM_d"].rearrange("(t p) c -> p t c", p=P)
                sp.dma_start(gate[:, :, 0:512], m[:, :, 512:1024]).then_inc(s_g, 16)
                sp.dma_start(gate[:, :, 512:768], m[:, :, 1280:1536]).then_inc(s_g, 16)
                sp.dma_start(gn[:], a["norm_row"].partition_broadcast(P)).then_inc(s_p, 16)
                sp.dma_start(cw[:], a["conv_cols"]).then_inc(s_p, 16)
                for f in range(2):
                    if f:
                        sp.wait_ge(s_clo, f)
                    for n in range(3):
                        r = 1024 + 256 * n + f * P
                        sp.dma_start(cv[:, n], a["projT_d"][r:r + P, :]).then_inc(s_cv[f], 16)
                sp.wait_ge(s_cv[1], 48)

            @block.vector
            def _(dve):
                steps = [0]

                def step(ins):
                    steps[0] += 1
                    ins.then_inc(s_cs, 1)
                    dve.wait_ge(s_cs, steps[0])

                for t in range(NT):
                    dve.wait_ge(s_sq, t + 1)
                    for part in range(2):
                        last = nc.vector.tensor_reduce(ms[:, t, 4 * part:4 * part + 4], heads(sq[:, t % 2], part), AX.X, ALU.add)
                    last.then_inc(s_ms, 1)
                dve.wait_ge(s_ms, NT)
                nc.vector.tensor_scalar(ms[:, :, 0:4], ms[:, :, 0:4], 1.0 / GLA_V, RMS_EPS, ALU.mult, ALU.add)
                nc.vector.tensor_scalar(ms[:, :, 4:8], ms[:, :, 4:8], 1.0 / HG_I, RMS_EPS, ALU.mult, ALU.add).then_inc(s_d, 1)
                dve.wait_ge(s_sqrt, 1)
                nc.vector.reciprocal(ms[:], ms[:]).then_inc(s_rms, 1)
                dve.wait_ge(s_rms, 1)

                def low_part(t):
                    dve.wait_ge(s_hi, t + 1)
                    nc.vector.tensor_tensor(yT_lo[:, 0:6, t * P:(t + 1) * P], ps_tile(t % 2), yT_hi[:, 0:6, t * P:(t + 1) * P].bitcast(F32),
                                            ALU.subtract).then_inc(s_lo, 1)

                for t in range(NT):
                    for part, dv in ((0, GLA_V), (1, HG_I)):
                        o = heads(o_all[:, t], part)
                        last = nc.vector.tensor_tensor(o, o, ms[:, t, 4 * part:4 * part + 4].unsqueeze(2).broadcast_to((P, 4, dv)), ALU.mult)
                    last.then_inc(s_n, 1)
                    if t > 1:
                        low_part(t - 2)
                    dve.wait_ge(s_n, t + 1)
                    dve.wait_ge(s_gn, t + 1)
                    nc.vector.tensor_tensor(o_all[:, t], o_all[:, t], gate[:, t], ALU.mult).then_inc(s_y, 1)
                low_part(NT - 2)
                low_part(NT - 1)
                dve.wait_ge(s_p, 32)
                for f in range(2):
                    dve.wait_ge(s_cv[f], 48)
                    acc = cv[:, 3]
                    step(nc.vector.tensor_tensor(u[:], cv[:, 1], cv[:, 2], ALU.mult))
                    step(nc.vector.tensor_scalar(acc, u[:], cw[:, f, 2:3], None, ALU.mult))
                    for lag in (1, 2):
                        step(nc.vector.scalar_tensor_tensor(acc[:, lag:], u[:, :SEQ - lag], cw[:, f, 2 - lag:3 - lag], acc[:, lag:], ALU.mult, ALU.add))
                    step(nc.vector.tensor_tensor(acc, acc, cv[:, 0], ALU.mult))
                    dve.wait_ge(s_chi, f + 1)
                    nc.vector.tensor_tensor(yT_lo[:, 6 + f], acc, yT_hi[:, 6 + f].bitcast(F32), ALU.subtract).then_inc(s_clo, 1)
                    dve.wait_ge(s_clo, f + 1)

            @block.gpsimd
            def _(pool):
                pool.wait_ge(s_p, 32)
                for t in range(NT):
                    pool.wait_ge(s_silu, t + 1)
                    nc.gpsimd.tensor_tensor(gate[:, t], gate[:, t], gn[:], ALU.mult).then_inc(s_gn, 1)

            @block.scalar
            def _(act):
                for t in range(NT):
                    if t >= 2:
                        act.wait_ge(s_ms, t - 1)
                    nc.scalar.activation(sq[:, t % 2], o_all[:, t], ACT.Square).then_inc(s_sq, 1)
                act.wait_ge(s_g, 32)
                for t in range(NT):
                    nc.scalar.activation(gate[:, t], gate[:, t], ACT.Silu).then_inc(s_silu, 1)
                act.wait_ge(s_d, 1)
                nc.scalar.activation(ms[:], ms[:], ACT.Sqrt).then_inc(s_sqrt, 1)
                for t in range(NT):
                    act.wait_ge(s_tp, t + 1)
                    nc.scalar.copy(yT_hi[:, 0:6, t * P:(t + 1) * P], ps_tile(t % 2)).then_inc(s_hi, 1)
                for f in range(2):
                    act.wait_ge(s_cs, 5 * f + 5)
                    nc.scalar.copy(yT_hi[:, 6 + f], cv[:, 3]).then_inc(s_chi, 1)

            @block.tensor
            def _(pe):
                for t in range(NT):
                    pe.wait_ge(s_y, t + 1)
                    if t >= 2:
                        pe.wait_ge(s_lo, t - 1)
                    for f in range(6):
                        last = nc.tensor.transpose(ps_tile(t % 2)[:, f], o_all[:, t, f * P:(f + 1) * P], a["ident"][:])
                    last.then_inc(s_tp, 1)


def project_out(nc, a, yT_hi, yT_lo):
    with ExitStack() as stack:
        k = Kit(nc, stack)
        wo_raw = k.sb("wo_raw", [P, 2, KT, CC])
        wo_hi = k.sb("wo_hi", [P, KT, D], F32R)
        wo_lo = k.sb("wo_lo", [P, KT, D], F32R)
        lng, lnb = k.sb("mixg", [P, D]), k.sb("mixb", [P, D])
        h = k.sb("h_in", [P, 2, D])
        r = k.sb("r", [P, 2, D])
        hT = k.sb("h2T", [P, 2, D])
        wr, br = k.sb("wr", [P, KT, NE]), k.sb("br", [P, NE])
        stat, mv, rs = k.sb("stat2", [P, 2, 2, 6]), k.sb("mv2", [P, 2, 2]), k.sb("rs2", [P, 2])
        logits = a["logits"]
        psM = k.ps("psM", [P, 2, D])
        psT = k.ps("psT", [P, D])
        psL = k.ps("psL", [P, 512])
        s_w = [k.sem(f"wo_raw{p}_loaded") for p in range(2)]
        s_h = [k.sem(f"h_in{p}_loaded") for p in range(2)]
        s_st = [k.sem(f"h2_{p}_stored") for p in range(2)]
        s_p, s_hi, s_lo, s_mm, s_d, s_sq, s_h2, s_tp, s_hT, s_lg, s_ev = (k.sem(n) for n in (
            "mix_params_loaded", "wo_hi_ready", "wo_lo_ready", "mix_multiplied", "dve_steps", "sqrt_done", "h2_ready",
            "h2_transposed", "h2T_ready", "logits_multiplied", "logits_ready"))
        n_cols = D // CC

        with nc.Block() as block:
            @block.sync
            def _(sp):
                for dst, src in ((lng, "ln_mix_g"), (lnb, "ln_mix_b"), (br, "b_router")):
                    sp.dma_start(dst[:], a[src].partition_broadcast(P)).then_inc(s_p, 16)
                sp.dma_start(wr[:], a["w_router"].rearrange("(k p) e -> p k e", p=P)).then_inc(s_p, 16)
                for c in range(n_cols):
                    if c >= 2:
                        sp.wait_ge(s_lo, c - 1)
                    sp.dma_start(wo_raw[:, c % 2], a["w_out"][:, c * CC:(c + 1) * CC].rearrange("(k p) n -> p k n", p=P)).then_inc(s_w[c % 2], 16)
                for t in range(NT):
                    p = t % 2
                    if t >= 2:
                        sp.wait_ge(s_d, 6 * (t - 2) + 1)
                    sp.dma_start(h[:, p], a["h_d"][t * P:(t + 1) * P, :]).then_inc(s_h[p], 16)
                    if t >= 1:
                        sp.wait_ge(s_h2, t)
                        sp.dma_start(a["h2_d"][(t - 1) * P:t * P, :], r[:, 1 - p]).then_inc(s_st[1 - p], 16)
                sp.wait_ge(s_h2, NT)
                sp.dma_start(a["h2_d"][(NT - 1) * P:, :], r[:, 1]).then_inc(s_st[1], 16)
                for p in range(2):
                    sp.wait_ge(s_st[p], 16 * (NT // 2))

            @block.vector
            def _(dve):
                for c in range(n_cols):
                    dve.wait_ge(s_hi, c + 1)
                    cols = slice(c * CC, (c + 1) * CC)
                    nc.vector.tensor_tensor(wo_lo[:, :, cols], wo_raw[:, c % 2], wo_hi[:, :, cols].bitcast(F32), ALU.subtract).then_inc(s_lo, 1)
                dve.wait_ge(s_p, 64)
                steps = [0]

                def step(ins, wait=True):
                    steps[0] += 1
                    ins.then_inc(s_d, 1)
                    if wait:
                        dve.wait_ge(s_d, steps[0])

                for t in range(NT):
                    p = t % 2
                    dve.wait_ge(s_mm, t + 1)
                    dve.wait_ge(s_h[p], 16 * (t // 2) + 16)
                    if t >= 2:
                        dve.wait_ge(s_st[p], 16 * (t // 2))
                        dve.wait_ge(s_tp, t - 1)
                    step(nc.vector.scalar_tensor_tensor(r[:, p], h[:, p], ALPHA, psM[:, p], ALU.mult, ALU.add))
                    nc.vector.bn_stats(stat[:, p, 0], r[:, p, 0:512])
                    step(nc.vector.bn_stats(stat[:, p, 1], r[:, p, 512:1024]))
                    step(nc.vector.bn_aggr(mv[:, p], stat[:, p]))
                    step(nc.vector.tensor_scalar(rs[:, p:p + 1], mv[:, p, 1:2], LN_EPS, None, ALU.add), False)
                    step(nc.vector.scalar_tensor_tensor(r[:, p], r[:, p], mv[:, p, 0:1], lng[:], ALU.subtract, ALU.mult), False)
                    if t >= 1:
                        dve.wait_ge(s_lg, t)
                        nc.vector.tensor_tensor(logits[:, t - 1], psL[:, 0:NE], br[:], ALU.add).then_inc(s_ev, 1)
                    dve.wait_ge(s_sq, t + 1)
                    step(nc.vector.reciprocal(rs[:, p:p + 1], rs[:, p:p + 1]))
                    nc.vector.scalar_tensor_tensor(r[:, p], r[:, p], rs[:, p:p + 1], lnb[:], ALU.mult, ALU.add).then_inc(s_h2, 1)
                dve.wait_ge(s_lg, NT)
                nc.vector.tensor_tensor(logits[:, NT - 1], psL[:, 0:NE], br[:], ALU.add).then_inc(s_ev, 1)

            @block.scalar
            def _(act):
                for c in range(n_cols):
                    act.wait_ge(s_w[c % 2], 16 * (c // 2) + 16)
                    nc.scalar.copy(wo_hi[:, :, c * CC:(c + 1) * CC], wo_raw[:, c % 2]).then_inc(s_hi, 1)
                for t in range(NT):
                    p = t % 2
                    act.wait_ge(s_d, 6 * t + 4)
                    nc.scalar.activation(rs[:, p:p + 1], rs[:, p:p + 1], ACT.Sqrt).then_inc(s_sq, 1)
                    act.wait_ge(s_tp, t + 1)
                    nc.scalar.copy(hT[:, p], psT[:]).then_inc(s_hT, 1)

            @block.tensor
            def _(pe):
                def output_tile(t):
                    p = t % 2
                    if t >= 2:
                        pe.wait_ge(s_d, 6 * (t - 2) + 1)
                    for kt in range(KT):
                        for n, (y, w) in enumerate(((yT_hi, wo_hi), (yT_hi, wo_lo), (yT_lo, wo_hi))):
                            for half in range(2):
                                c = slice(half * 512, half * 512 + 512)
                                last = nc.tensor.matmul(psM[:, p, c], y[:, kt, t * P:(t + 1) * P], w[:, kt, c],
                                                        start=(kt == 0 and n == 0), stop=(kt == KT - 1 and n == 2))
                    last.then_inc(s_mm, 1)

                def logit_tile(t):
                    p = t % 2
                    pe.wait_ge(s_h2, t + 1)
                    if t >= 1:
                        pe.wait_ge(s_hT, t)
                    for kt in range(KT):
                        last = nc.tensor.transpose(psT[:, kt * P:(kt + 1) * P], r[:, p, kt * P:(kt + 1) * P], a["ident"][:])
                    last.then_inc(s_tp, 1)
                    if t >= 1:
                        pe.wait_ge(s_ev, t)
                    pe.wait_ge(s_hT, t + 1)
                    for kt in range(KT):
                        last = nc.tensor.matmul(psL[:, 0:NE], hT[:, p, kt * P:(kt + 1) * P], wr[:, kt], start=(kt == 0), stop=(kt == KT - 1))
                    last.then_inc(s_lg, 1)

                pe.wait_ge(s_lo, n_cols)
                pe.wait_ge(s_p, 64)
                for t in range(NT):
                    output_tile(t)
                    if t >= 1:
                        logit_tile(t - 1)
                logit_tile(NT - 1)


CAP = 160
SIZES = (128, 144, CAP)
NB_OVER = 25
NSLOT = (NE + NB_OVER) * CAP


def route(nc, a, ex):
    before_exp = [0]
    gate, slot_i, idx, ids = a["gate"], a["slot_i"], a["idx"], a["block_expert"]
    with ExitStack() as stack:
        k = Kit(nc, stack)
        lg = a["logits"]
        top, topi = k.sb("top", [P, NT, 8]), k.sb("topi", [P, NT, 8], U32)
        topf = k.sb("topf", [P, NT, TOPK])
        nmax, den = k.sb("nmax", [P, NT]), k.sb("den", [P, NT])
        oh = k.sb("oh", [P, NT, TOPK, NE])
        M, T1, T2, SL = (k.sb(n, [P, NT, NE]) for n in ("M", "T1", "T2", "SL"))
        cnt, nb, first, sizef, B = (k.sb(n, [P, NE]) for n in ("count", "blocks_beyond", "blocks_before", "size", "offset"))
        cmp = k.sb("cmp", [P, NB_OVER, NE])
        bexp = k.sb("bexp", [P, NB_OVER + 1])
        cst = k.sb("cst", [P, 2 * NE + NB_OVER])
        tri, ones = k.sb("tri", [P, P]), k.sb("ones", [P, P])
        slotf = k.sb("slotf", [P, NT, TOPK])
        tok = k.sb("tok", [P, NT])
        zero = k.sb("zero", [P, NSLOT // P + 1])
        rows = k.sb("rows", [NE + NB_OVER, CAP])
        ps = ex.ps[:, 0, 0:NT * NE].rearrange("p (t e) -> p t e", e=NE)
        psC = ex.ps[:, 1]
        psI = ex.ps[:, 2:4]
        s_c, s_d, s_e, s_oh, s_pos, s_slot, s_z, s_m, s_tp, s_zero, s_rows = (k.sem(n) for n in (
            "route_consts_loaded", "dve_steps", "exp_done", "choices_ready", "positions_ready", "slots_ready", "map_zeroed",
            "map_scattered", "map_transposed", "zeros_ready", "map_rows_loaded"))
        n_iota, n_cap, n_blk = slice(0, NE), slice(NE, 2 * NE), slice(2 * NE, 2 * NE + NB_OVER)

        with nc.Block() as block:
            @block.sync
            def _(sp):
                for dst, src in ((cst, "route_c"), (tri, "tri_c"), (tok, "token_c")):
                    sp.dma_start(dst[:], a[src]).then_inc(s_c, 16)
                sp.wait_ge(s_zero, 2)
                flat = a["slot_token_d"].rearrange("s one -> (s one)")
                n = NSLOT // P
                sp.dma_start(flat[0:n * P].rearrange("(p n) -> p n", p=P), zero[:, 0:n]).then_inc(s_z, 16)
                sp.dma_start(flat[n * P:NSLOT].rearrange("(o n) -> o n", o=1), zero[0:1, 0:NSLOT - n * P]).then_inc(s_z, 16)
                sp.wait_ge(s_m, 16 * NT * TOPK)
                sp.dma_start(rows[:], a["slot_token_d"].rearrange("(b s) one -> b (s one)", s=CAP)).then_inc(s_rows, 16)

            @block.vector
            def _(dve):
                steps = [0]

                def step(ins, wait=True):
                    steps[0] += 1
                    ins.then_inc(s_d, 1)
                    if wait:
                        dve.wait_ge(s_d, steps[0])

                nc.vector.memset(idx[:], 0.0)
                nc.vector.memset(ones[:], 1.0).then_inc(s_zero, 1)
                nc.vector.memset(zero[:], 0.0).then_inc(s_zero, 1)
                for t in range(NT):
                    step(nc.vector.max(top[:, t], lg[:, t]), t == NT - 1)
                for t in range(NT):
                    step(nc.vector.max_index(topi[:, t], top[:, t], lg[:, t]), t == NT - 1)
                step(nc.vector.tensor_copy(topf[:], topi[:, :, 0:TOPK]), False)
                step(nc.vector.tensor_tensor(gate[:], top[:, :, 0:TOPK], top[:, :, 0:1].broadcast_to((P, NT, TOPK)), ALU.subtract))
                before_exp[0] = steps[0]
                dve.wait_ge(s_c, 48)
                step(nc.vector.tensor_tensor(oh[:].rearrange("p t k e -> p (t k) e"),
                                             topf[:].rearrange("p t k -> p (t k)").unsqueeze(2).broadcast_to((P, NT * TOPK, NE)),
                                             cst[:, n_iota].unsqueeze(1).broadcast_to((P, NT * TOPK, NE)), ALU.is_equal))
                nc.vector.tensor_reduce(M[:], oh[:].rearrange("p t k e -> p t e k"), AX.X, ALU.add).then_inc(s_oh, 1)
                dve.wait_ge(s_e, 1)
                step(nc.vector.tensor_reduce(den[:], gate[:], AX.X, ALU.add))
                step(nc.vector.reciprocal(den[:], den[:]))
                step(nc.vector.tensor_tensor(gate[:], gate[:], den[:].unsqueeze(2).broadcast_to((P, NT, TOPK)), ALU.mult), False)
                dve.wait_ge(s_pos, 1)
                step(nc.vector.tensor_copy(cnt[:], psC[:, 0:NE]))
                step(nc.vector.tensor_scalar(sizef[:], cnt[:], float(SIZES[0]), None, ALU.is_gt), False)
                step(nc.vector.tensor_scalar(nb[:], cnt[:], float(CAP), None, ALU.is_gt))
                step(nc.vector.scalar_tensor_tensor(sizef[:], cnt[:], float(SIZES[1]), sizef[:], ALU.is_gt, ALU.add))
                step(nc.vector.tensor_copy(a["block_size"][:], sizef[:]), False)
                for q in range(2, (SEQ - 1) // CAP + 1):
                    step(nc.vector.scalar_tensor_tensor(nb[:], cnt[:], float(q * CAP), nb[:], ALU.is_gt, ALU.add))
                step(nc.vector.tensor_tensor_scan(first[:], ones[:, 0:NE], nb[:], 0.0, ALU.mult, ALU.add))
                step(nc.vector.tensor_tensor(cmp[:], first[:].unsqueeze(1).broadcast_to((P, NB_OVER, NE)),
                                             cst[:, n_blk].unsqueeze(2).broadcast_to((P, NB_OVER, NE)), ALU.is_le), False)
                step(nc.vector.tensor_copy(bexp[:, NB_OVER:], first[:, NE - 1:NE]))
                step(nc.vector.tensor_reduce(bexp[:, 0:NB_OVER], cmp[:], AX.X, ALU.add), False)
                step(nc.vector.tensor_tensor(first[:], first[:], nb[:], ALU.subtract))
                step(nc.vector.tensor_scalar(bexp[:, 0:NB_OVER], bexp[:, 0:NB_OVER], float(NE - 1), None, ALU.min))
                step(nc.vector.tensor_copy(ids[:], bexp[:]), False)
                step(nc.vector.tensor_scalar(B[:], first[:], float(CAP), float(CAP * (NE - 1)), ALU.mult, ALU.add))
                step(nc.vector.tensor_tensor(B[:], B[:], cst[:, n_cap], ALU.subtract))
                wide = lambda x: x.unsqueeze(1).broadcast_to((P, NT, NE))
                step(nc.vector.tensor_scalar(T1[:], ps, float(CAP), None, ALU.is_ge))
                step(nc.vector.tensor_tensor(T1[:], T1[:], wide(B[:]), ALU.mult), False)
                step(nc.vector.tensor_tensor(T2[:], ps, wide(cst[:, n_cap]), ALU.add))
                step(nc.vector.tensor_tensor(SL[:], T1[:], T2[:], ALU.add))
                step(nc.vector.tensor_tensor(oh[:], oh[:], SL[:].unsqueeze(2).broadcast_to((P, NT, TOPK, NE)), ALU.mult))
                step(nc.vector.tensor_reduce(slotf[:], oh[:], AX.X, ALU.add))
                nc.vector.tensor_copy(slot_i[:], slotf[:]).then_inc(s_slot, 1)
                dve.wait_ge(s_tp, 1)
                nc.vector.tensor_copy(idx[:, 0, 0:NE + NB_OVER], psI[:, 0, 0:NE + NB_OVER])
                nc.vector.tensor_copy(idx[0:CAP - P, 1, 0:NE + NB_OVER], psI[0:CAP - P, 1, 0:NE + NB_OVER])

            @block.scalar
            def _(act):
                act.wait_ge(s_d, before_exp[0])
                nc.scalar.activation(gate[:], gate[:], ACT.Exp).then_inc(s_e, 1)

            @block.gpsimd
            def _(pool):
                pool.wait_ge(s_slot, 1)
                pool.wait_ge(s_z, 32)
                for t in range(NT):
                    for c in range(TOPK):
                        nc.gpsimd.indirect_dma_start(a["slot_token_d"], bass.IndirectOffsetOnAxis(slot_i[:, t, c:c + 1], 0),
                                                     tok[:, t:t + 1], None).then_inc(s_m, 16)

            @block.tensor
            def _(pe):
                pe.wait_ge(s_oh, 1)
                pe.wait_ge(s_c, 48)
                pe.wait_ge(s_zero, 2)
                for t in range(NT):
                    for q in range(t + 1):
                        nc.tensor.matmul(ps[:, t], (tri if q == t else ones)[:], M[:, q], start=(q == 0), stop=(q == t))
                for q in range(NT):
                    last = nc.tensor.matmul(psC[:, 0:NE], ones[:], M[:, q], start=(q == 0), stop=(q == NT - 1))
                last.then_inc(s_pos, 1)
                pe.wait_ge(s_rows, 16)
                n = NE + NB_OVER
                nc.tensor.transpose(psI[:, 0, 0:n], rows[:, 0:P], a["ident"][0:n, 0:n])
                nc.tensor.transpose(psI[0:CAP - P, 1, 0:n], rows[:, P:CAP], a["ident"][0:n, 0:n]).then_inc(s_tp, 1)


CW = 512
CHUNKS = 6


class Experts:

    def __init__(self, nc, a, k):
        self.nc, self.a = nc, a
        self.w = k.sb("w_expert", [P, CHUNKS, KT, CW])
        self.x0, self.x1 = k.sb("x0", [P, D]), k.sb("x1", [CAP - P, D])
        self.xT, self.actT = k.sb("xT", [P, KT, CAP]), k.sb("actT", [P, KT, CAP])
        self.g, self.sg, self.u = (k.sb(n, [P, 2, 4, CAP]) for n in ("g_clamped", "g_sigmoid", "u_clamped"))
        self.yT = k.sb("yT", [P, KT, CAP])
        self.y0, self.y1 = k.sb("y0", [P, D]), k.sb("y1", [CAP - P, D])
        self.bias = k.sb("bias", [P, 3 * KT, NE])
        self.cur = k.sb("cur_idx", [P, 2], U32)
        self.ps = k.ps("psE", [P, 8, 512])

    def open(self, k):
        names = dict(mm="chunk_multiplied", gu="gate_up_evacuated", dn="down_evacuated", sig="sigmoid_done", mul="up_times_gate",
                     act="actT_ready", xtp="x_transposed", xT="xT_ready", ytp="y_transposed", yev="y_evacuated", cur="idx_copied",
                     go="gather_released")
        self.s = {n: k.sem("ex_" + v) for n, v in names.items()}
        self.s_w = [k.sem(f"w_chunk{j}_loaded") for j in range(CHUNKS)]
        self.s_x = k.sem("x_gathered")
        self.s_y = k.sem("y_stored")

    def load_chunk(self, sp, expert, j):
        a = self.a
        if j < 4:
            src = a["w_gate_up"][bass.ds(expert, 1), :, (j % 2) * DFF + (j // 2) * CW:(j % 2) * DFF + (j // 2 + 1) * CW]
        else:
            src = a["w_down"][bass.ds(expert, 1), :, (j - 4) * CW:(j - 3) * CW]
        sp.dma_start(self.w[:, j], src.rearrange("o (k p) n -> p (o k) n", p=P)).then_inc(self.s_w[j], 16)

    def gather(self, pool, n, first=False):
        nc = self.nc
        if not first:
            pool.wait_ge(self.s["xtp"], n * 2)
        nc.gpsimd.tensor_copy(self.cur[:], self.a["idx"][:, :, bass.ds(n, 1)].rearrange("p a b -> p (a b)")).then_inc(self.s["cur"], 1)
        pool.wait_ge(self.s["cur"], n + 1)
        pool.sem_inc(self.s["go"], 1)
        nc.gpsimd.indirect_dma_start(self.x0[:], None, self.a["h2_d"], bass.IndirectOffsetOnAxis(self.cur[:, 0:1], 0)).then_inc(self.s_x, 16)
        nc.gpsimd.indirect_dma_start(self.x1[:], None, self.a["h2_d"], bass.IndirectOffsetOnAxis(self.cur[0:CAP - P, 1:2], 0)).then_inc(self.s_x, 16)

    def ps_x(self):
        return self.ps[:, 4:6, 0:2 * CAP].rearrange("p a (b t) -> p a b t", t=CAP)

    def x_transpose(self, pe, n, r, y_done):
        nc = self.nc
        if r == 0:
            pe.wait_ge(self.s_x, n * 32 + 32)
            if y_done is not None:
                pe.wait_ge(self.s["yev"], 2 * y_done)
        else:
            pe.wait_ge(self.s["xT"], 2 * n + 1)
        for q in range(4):
            cols = slice((4 * r + q) * P, (4 * r + q + 1) * P)
            out = self.ps_x()[:, q // 2, q % 2]
            nc.tensor.transpose(out[:, 0:P], self.x0[:, cols], self.a["ident"][:])
            last = nc.tensor.transpose(out[:, P:CAP], self.x1[:, cols], self.a["ident"][0:CAP - P, 0:CAP - P])
        last.then_inc(self.s["xtp"], 1)

    def x_evacuate(self, act, n, r):
        act.wait_ge(self.s["xtp"], 2 * n + r + 1)
        self.nc.scalar.copy(self.xT[:, 4 * r:4 * r + 4, :].rearrange("p (a b) t -> p a b t", b=2), self.ps_x()).then_inc(self.s["xT"], 1)

    def multiply(self, pe, n, j, first=False, slots=CAP):
        nc = self.nc
        moving = self.xT if j < 4 else self.actT
        pe.wait_ge(self.s_w[j], n * 16 + 16)
        if j == 0:
            pe.wait_ge(self.s["xT"], 2 * n + 2)
        if j < 2:
            if not first:
                pe.wait_ge(self.s["dn"], 2 * n + j - 1)
        else:
            pe.wait_ge(self.s["gu"], 4 * n + j - 1)

        def products(kts, qs=range(4)):
            for q in qs:
                out = self.ps[:, (j % 2) * 2 + q // 2, (q % 2) * CAP:(q % 2) * CAP + slots]
                for kt in kts:
                    last = nc.tensor.matmul(out, self.w[:, j, kt, q * P:(q + 1) * P], moving[:, kt, 0:slots],
                                            start=(kt == 0), stop=(kt == KT - 1))
            return last

        if j == 4:
            pe.wait_ge(self.s["act"], 2 * n + 1)
            products(range(KT // 2), (0, 2))
            pe.wait_ge(self.s["act"], 2 * n + 2)
            products(range(KT // 2, KT), (0, 2))
            products(range(KT), (1, 3)).then_inc(self.s["mm"], 1)
        else:
            products(range(KT)).then_inc(self.s["mm"], 1)

    def gate_evacuate(self, dve, n, half, expert):
        j = 2 * half
        dve.wait_ge(self.s["mm"], n * CHUNKS + j + 1)
        for q in range(4):
            last = self.nc.vector.tensor_scalar(self.g[:, half, q], self.ps[:, (j % 2) * 2 + q // 2, (q % 2) * CAP:(q % 2 + 1) * CAP],
                                                self.bias[:, 4 * half + q, bass.ds(expert, 1)], SWIGLU_LIMIT, ALU.add, ALU.min)
        last.then_inc(self.s["gu"], 1)

    def up_evacuate(self, dve, n, half, expert):
        nc, j = self.nc, 2 * half + 1
        dve.wait_ge(self.s["mm"], n * CHUNKS + j + 1)
        for q in range(4):
            last = nc.vector.tensor_scalar(self.u[:, half, q], self.ps[:, (j % 2) * 2 + q // 2, (q % 2) * CAP:(q % 2 + 1) * CAP],
                                           self.bias[:, KT + 4 * half + q, bass.ds(expert, 1)], SWIGLU_LIMIT + 1.0, ALU.add, ALU.min)
        last.then_inc(self.s["gu"], 1)
        dve.wait_ge(self.s["gu"], 4 * n + 2 * half + 2)
        nc.vector.scalar_tensor_tensor(self.u[:, half], self.u[:, half], 1.0 - SWIGLU_LIMIT, self.g[:, half], ALU.max, ALU.mult)\
            .then_inc(self.s["mul"], 1)
        dve.wait_ge(self.s["mul"], 2 * n + half + 1)
        dve.wait_ge(self.s["sig"], 2 * n + half + 1)
        nc.vector.tensor_tensor(self.actT[:, 4 * half:4 * half + 4], self.u[:, half], self.sg[:, half], ALU.mult).then_inc(self.s["act"], 1)

    def sigmoid(self, act, n, half):
        act.wait_ge(self.s["gu"], 4 * n + 2 * half + 1)
        self.nc.scalar.activation(self.sg[:, half], self.g[:, half], ACT.Sigmoid, scale=SWIGLU_ALPHA).then_inc(self.s["sig"], 1)

    def down_evacuate(self, act, n, half, expert):
        j = 4 + half
        act.wait_ge(self.s["mm"], n * CHUNKS + j + 1)
        for q in range(4):
            last = self.nc.scalar.activation(self.yT[:, 4 * half + q], self.ps[:, (j % 2) * 2 + q // 2, (q % 2) * CAP:(q % 2 + 1) * CAP],
                                             ACT.Identity, bias=self.bias[:, 2 * KT + 4 * half + q, bass.ds(expert, 1)])
        last.then_inc(self.s["dn"], 1)

    def y_transpose(self, pe, n, half, first=False):
        nc = self.nc
        pe.wait_ge(self.s["dn"], 2 * n + half + 1)
        if half == 0:
            if not first:
                pe.wait_ge(self.s["yev"], 2 * n - 1)
        bank = 6 - 2 * half
        for q in range(4):
            nc.tensor.transpose(self.ps[:, bank, q * P:(q + 1) * P], self.yT[:, 4 * half + q, 0:P], self.a["ident"][:])
            last = nc.tensor.transpose(self.ps[0:CAP - P, bank + 1, q * P:(q + 1) * P], self.yT[:, 4 * half + q, P:CAP], self.a["ident"][:])
        last.then_inc(self.s["ytp"], 1)

    def y_evacuate(self, act, n, half, first=False):
        nc = self.nc
        act.wait_ge(self.s["ytp"], 2 * n + half + 1)
        if not first and half == 0:
            act.wait_ge(self.s_y, n * 32)
        bank, cols = 6 - 2 * half, slice(half * 512, half * 512 + 512)
        nc.scalar.copy(self.y0[:, cols], self.ps[:, bank, :])
        nc.scalar.copy(self.y1[:, cols], self.ps[0:CAP - P, bank + 1, :]).then_inc(self.s["yev"], 1)

    def y_store(self, act, n):
        act.wait_ge(self.s["yev"], 2 * n + 2)
        act.dma_start(self.a["y_d"][bass.ds(n * CAP, P), :], self.y0[:]).then_inc(self.s_y, 16)
        act.dma_start(self.a["y_d"][bass.ds(n * CAP + P, CAP - P), :], self.y1[:]).then_inc(self.s_y, 16)


def expert_biases(nc, a, ex):
    with ExitStack() as stack:
        k = Kit(nc, stack)
        s_l, s_t, s_e = k.sem("biases_loaded"), k.sem("biases_transposed"), k.sem("biases_ready")
        rows = k.sb("bias_rows", [NE, 3 * D])
        with nc.Block() as block:
            @block.sync
            def _(sp):
                sp.dma_start(rows[:, 0:2 * DFF], a["b_gate_up"]).then_inc(s_l, 16)
                sp.dma_start(rows[:, 2 * DFF:2 * DFF + D], a["b_down"]).then_inc(s_l, 16)
                for j in range(CHUNKS):
                    ex.load_chunk(sp, 0, j)

            @block.tensor
            def _(pe):
                pe.wait_ge(s_l, 32)
                for f in range(3 * KT):
                    last = nc.tensor.transpose(ex.ps[:, f // 16, (f % 16) * NE:(f % 16 + 1) * NE], rows[:, f * P:(f + 1) * P], a["ident"][0:NE, 0:NE])
                last.then_inc(s_t, 1)

            @block.vector
            def _(dve):
                dve.wait_ge(s_t, 1)
                bank = lambda f: ex.ps[:, f // 16, (f % 16) * NE:(f % 16) * NE + KT * NE].rearrange("p (f e) -> p f e", e=NE)
                nc.vector.tensor_copy(ex.bias[:, 0:KT], bank(0))
                nc.vector.tensor_scalar(ex.bias[:, KT:2 * KT], bank(KT), 1.0, None, ALU.add)
                nc.vector.tensor_copy(ex.bias[:, 2 * KT:], bank(2 * KT)).then_inc(s_e, 1)


def experts(nc, a, ex):
    def over(engine, body):
        count = engine.value_load(a["block_expert"][0:1, NB_OVER:NB_OVER + 1], min_val=0, max_val=NB_OVER)
        with engine.If(count > 0):
            with engine.Fori(0, NB_OVER) as b:
                with engine.If(b < count):
                    body(b + NE, engine.value_load(a["block_expert"][0:1, bass.ds(b, 1)], min_val=0, max_val=NE - 1))

    with nc.Block() as block:
        @block.sync
        def _(sp):
            with sp.Fori(1, NE) as e:
                for j in range(CHUNKS):
                    sp.wait_ge(ex.s["mm"], (e - 1) * CHUNKS + j + 1)
                    ex.load_chunk(sp, e, j)

            def body(n, expert):
                for j in range(CHUNKS):
                    sp.wait_ge(ex.s["mm"], (n - 1) * CHUNKS + j + 1)
                    ex.load_chunk(sp, expert, j)
            over(sp, body)

        @block.gpsimd
        def _(pool):
            ex.gather(pool, 0, first=True)
            with pool.Fori(1, NE) as e:
                ex.gather(pool, e)
            over(pool, lambda n, expert: ex.gather(pool, n))

        @block.scalar
        def _(act):
            def body(n, expert, ahead, first=False, pending=True):
                if pending:
                    ex.y_evacuate(act, n - 1, 1)
                    ex.y_store(act, n - 1)
                for half in range(2):
                    ex.sigmoid(act, n, half)
                if ahead:
                    ex.x_evacuate(act, n + 1, 0)
                ex.down_evacuate(act, n, 0, expert)
                if ahead:
                    ex.x_evacuate(act, n + 1, 1)
                ex.down_evacuate(act, n, 1, expert)
                ex.y_evacuate(act, n, 0, first)
                if not ahead:
                    ex.y_evacuate(act, n, 1)
                    ex.y_store(act, n)

            for r in range(2):
                ex.x_evacuate(act, 0, r)
            body(0, 0, True, first=True, pending=False)
            with act.Fori(1, NE - 1) as e:
                body(e, e, True)
            body(NE - 1, NE - 1, False)

            def over_body(n, expert):
                for r in range(2):
                    ex.x_evacuate(act, n, r)
                body(n, expert, False, pending=False)
            over(act, over_body)
            blocks = act.value_load(a["block_expert"][0:1, NB_OVER:NB_OVER + 1], min_val=0, max_val=NB_OVER) + NE
            act.wait_ge(ex.s_y, blocks * 32)
            act.sem_inc(ex.s["go"], 1)

        @block.vector
        def _(dve):
            def body(n, expert):
                for half in range(2):
                    ex.gate_evacuate(dve, n, half, expert)
                    ex.up_evacuate(dve, n, half, expert)

            with dve.Fori(0, NE) as e:
                body(e, e)
            over(dve, body)

        @block.tensor
        def _(pe):
            def body(n, ahead, first=False, pending=True, slots=CAP):
                ex.multiply(pe, n, 0, first, slots)
                if pending:
                    ex.y_transpose(pe, n - 1, 1)
                for j in range(1, 4):
                    ex.multiply(pe, n, j, first, slots)
                if ahead:
                    ex.x_transpose(pe, n + 1, 0, None if first else n)
                ex.multiply(pe, n, 4, slots=slots)
                if ahead:
                    ex.x_transpose(pe, n + 1, 1, None)
                ex.multiply(pe, n, 5, slots=slots)
                ex.y_transpose(pe, n, 0, first)
                if not ahead:
                    ex.y_transpose(pe, n, 1)

            def sized(n, ahead):
                size = pe.value_load(a["block_size"][0:1, bass.ds(n, 1)], min_val=0, max_val=len(SIZES) - 1)
                for i, slots in enumerate(SIZES):
                    with pe.If(size == i):
                        body(n, ahead, slots=slots)

            for r in range(2):
                ex.x_transpose(pe, 0, r, None)
            body(0, True, first=True, pending=False)
            with pe.Fori(1, NE - 1) as e:
                sized(e, True)
            sized(NE - 1, False)

            def over_body(n, expert):
                for r in range(2):
                    ex.x_transpose(pe, n, r, n)
                body(n, False, pending=False)
            over(pe, over_body)


def combine(nc, a):
    with ExitStack() as stack:
        k = Kit(nc, stack)
        y = k.sb("y", [P, 2, TOPK, D])
        h2 = k.sb("h2_in", [P, 2, D])
        acc = k.sb("acc", [P, 2, D])
        lng, lnb = k.sb("ffng", [P, D]), k.sb("ffnb", [P, D])
        stat, mv, rs = k.sb("stat3", [P, 2, 2, 6]), k.sb("mv3", [P, 2, 2]), k.sb("rs3", [P, 2])
        s_p, s_d, s_sq, s_out = k.sem("ffn_params_loaded"), k.sem("dve_steps"), k.sem("sqrt_done"), k.sem("out_ready")
        s_y = [k.sem(f"y{p}_gathered") for p in range(2)]
        s_h = [k.sem(f"h2_in{p}_loaded") for p in range(2)]
        s_st = [k.sem(f"out{p}_stored") for p in range(2)]
        STEPS = 9

        with nc.Block() as block:
            @block.gpsimd
            def _(pool):
                for t in range(NT):
                    p = t % 2
                    if t >= 2:
                        pool.wait_ge(s_d, STEPS * (t - 2) + 5)
                    for c in range(TOPK):
                        nc.gpsimd.indirect_dma_start(y[:, p, c], None, a["y_d"], bass.IndirectOffsetOnAxis(a["slot_i"][:, t, c:c + 1], 0))\
                            .then_inc(s_y[p], 16)

            @block.sync
            def _(sp):
                for dst, src in ((lng, "ln_ffn_g"), (lnb, "ln_ffn_b")):
                    sp.dma_start(dst[:], a[src].partition_broadcast(P)).then_inc(s_p, 16)
                for t in range(NT + 1):
                    p = t % 2
                    if t < NT:
                        if t >= 2:
                            sp.wait_ge(s_d, STEPS * (t - 2) + 5)
                        sp.dma_start(h2[:, p], a["h2_d"][t * P:(t + 1) * P, :]).then_inc(s_h[p], 16)
                    if t >= 1:
                        sp.wait_ge(s_out, t)
                        sp.dma_start(a["out"][0, (t - 1) * P:t * P, :], acc[:, 1 - p]).then_inc(s_st[1 - p], 16)
                for p in range(2):
                    sp.wait_ge(s_st[p], 16 * (NT // 2))

            @block.vector
            def _(dve):
                steps = [0]

                def step(ins, wait=True):
                    steps[0] += 1
                    ins.then_inc(s_d, 1)
                    if wait:
                        dve.wait_ge(s_d, steps[0])

                for t in range(NT):
                    p = t % 2
                    dve.wait_ge(s_y[p], 64 * (t // 2) + 64)
                    dve.wait_ge(s_h[p], 16 * (t // 2) + 16)
                    if t >= 2:
                        dve.wait_ge(s_st[p], 16 * (t // 2))
                    g = a["gate"][:, t]
                    step(nc.vector.tensor_scalar(acc[:, p], y[:, p, 0], g[:, 0:1], None, ALU.mult))
                    for c in range(1, TOPK):
                        step(nc.vector.scalar_tensor_tensor(acc[:, p], y[:, p, c], g[:, c:c + 1], acc[:, p], ALU.mult, ALU.add))
                    step(nc.vector.scalar_tensor_tensor(acc[:, p], h2[:, p], ALPHA, acc[:, p], ALU.mult, ALU.add))
                    nc.vector.bn_stats(stat[:, p, 0], acc[:, p, 0:512])
                    step(nc.vector.bn_stats(stat[:, p, 1], acc[:, p, 512:1024]))
                    step(nc.vector.bn_aggr(mv[:, p], stat[:, p]))
                    step(nc.vector.tensor_scalar(rs[:, p:p + 1], mv[:, p, 1:2], LN_EPS, None, ALU.add), False)
                    if t == 0:
                        dve.wait_ge(s_p, 32)
                    nc.vector.scalar_tensor_tensor(acc[:, p], acc[:, p], mv[:, p, 0:1], lng[:], ALU.subtract, ALU.mult)
                    dve.wait_ge(s_sq, t + 1)
                    step(nc.vector.reciprocal(rs[:, p:p + 1], rs[:, p:p + 1]))
                    nc.vector.scalar_tensor_tensor(acc[:, p], acc[:, p], rs[:, p:p + 1], lnb[:], ALU.mult, ALU.add).then_inc(s_out, 1)

            @block.scalar
            def _(act):
                for t in range(NT):
                    act.wait_ge(s_d, STEPS * t + 8)
                    nc.scalar.activation(rs[:, t % 2:t % 2 + 1], rs[:, t % 2:t % 2 + 1], ACT.Sqrt).then_inc(s_sq, 1)


def build(nc, a):
    with ExitStack() as stack:
        k = Kit(nc, stack)
        a["ident"] = k.sb("ident", [P, P])
        a["consts_loaded"] = k.sem("consts_loaded")
        for name, shape in SCRATCH.items():
            a[name] = nc.dram_tensor(name, shape, F32, kind="Internal").ap()
        with nc.Block() as block:
            @block.sync
            def _(sp):
                sp.dma_start(a["ident"][:], a["ident_c"]).then_inc(a["consts_loaded"], 16)
        project(nc, a, k)
        a["logits"] = k.sb("logits", [P, NT, NE])
        a["gate"] = k.sb("gate", [P, NT, TOPK])
        a["slot_i"] = k.sb("slot_i", [P, NT, TOPK], U32)
        a["idx"] = k.sb("idx", [P, 2, NE + NB_OVER], U32)
        a["block_size"] = k.sb("block_size", [P, NE], I32)
        a["block_expert"] = k.sb("block_expert", [P, NB_OVER + 1], I32)
        mixers(nc, a)
        with ExitStack() as expert_stack:
            ke = Kit(nc, expert_stack)
            ex = Experts(nc, a, ke)
            ex.open(ke)
            expert_biases(nc, a, ex)
            route(nc, a, ex)
            experts(nc, a, ex)
        combine(nc, a)


SCRATCH = {
    "h_d": (SEQ, D), "projT_d": (NFM * CC, SEQ), "projM_d": (SEQ, NTM * CC), "lrT_d": (RANK, SEQ),
    "h2_d": (SEQ, D), "slot_token_d": (NSLOT, 1), "y_d": (NSLOT, D),
}


def level_masks():
    j = np.arange(P)[:, None]
    out = np.zeros((P, 6, CH // 2), np.int32)
    for level in range(6):
        s = 1 << level
        n = np.arange(CH // 2)
        i = (n // s) * 2 * s + s + n % s
        out[:, level] = (j // (2 * s) == i // (2 * s)) & (j // s % 2 == 0)
    return out


def layout(inputs):
    i = {n: np.ascontiguousarray(v) for n, v in inputs.items()}
    w = i["w_in"][0]
    o = np.cumsum([0, 256, 256, 512, RANK, 512, 256, 256, 256, 256, 256, 256, 256])
    part = lambda n: w[:, o[n]:o[n + 1]]
    cols = np.concatenate([part(n) for n in (0, 1, 5, 6, 9, 10, 11, 2, 4, 7, 8)], axis=1)
    out = {
        "x": i["x"][0], "ln_in_g": i["ln_in_g"], "ln_in_b": i["ln_in_b"],
        "w_cols": cols.reshape(KT, P, NFM + NTM, CC).transpose(2, 1, 0, 3),
        "w_lr": part(3).reshape(KT, P, RANK).transpose(1, 0, 2),
        "ident_c": np.eye(P, dtype=np.float32),
        "w_expand": i["w_gla_gate_expand"][0],
        "gate_cols": np.concatenate([i["b_gla_gate"][0].reshape(2, P), i["hgrn_lb_raw"][0].reshape(2, P)]).T,
        "restart_c": np.broadcast_to((np.arange(SEQ) % CH != 0).astype(np.float32), (P, SEQ)),
        "w_gate_up": i["w_gate_up"][0], "w_down": i["w_down"][0], "b_gate_up": i["b_gate_up"][0], "b_down": i["b_down"][0],
        "ln_ffn_g": i["ln_ffn_g"][0], "ln_ffn_b": i["ln_ffn_b"][0],
        "norm_row": np.concatenate([np.tile(i["gla_norm_g"][0], GLA_H), np.tile(i["hgrn_norm_g"][0], HG_H)]),
        "conv_cols": i["conv_w"][0].reshape(CONV_W, 2, P).transpose(2, 1, 0),
        "w_out": i["w_out"][0], "ln_mix_g": i["ln_mix_g"][0], "ln_mix_b": i["ln_mix_b"][0],
        "w_router": i["w_router"][0], "b_router": i["b_router"][0],
        "route_c": np.broadcast_to(np.concatenate([np.arange(NE), np.arange(NE) * CAP, np.arange(NB_OVER)]).astype(np.float32),
                                   (P, 2 * NE + NB_OVER)),
        "tri_c": (np.arange(P)[:, None] < np.arange(P)[None, :]).astype(np.float32),
        "token_c": np.arange(SEQ, dtype=np.float32).reshape(NT, P).T,
        "level_masks": level_masks(), "diag_mask": np.eye(P, dtype=np.int32),
    }
    return {n: np.ascontiguousarray(v) for n, v in out.items()}


def kernel(**inputs):
    import concourse.bacc as bacc
    from concourse.bass_utils import run_bass_kernel_spmd

    nc = bacc.Bacc("TRN2", target_bir_lowering=False, num_devices=1)
    arrays = layout(inputs)
    a = {n: nc.dram_tensor(n, v.shape, mybir.dt.from_np(v.dtype), kind="ExternalInput").ap() for n, v in arrays.items()}
    a["out"] = nc.dram_tensor("out", (1, SEQ, D), F32, kind="ExternalOutput").ap()
    build(nc, a)
    return run_bass_kernel_spmd(nc, [arrays], core_ids=[0]).results[0]["out"]
```

```python
from contextlib import ExitStack

import concourse.bass as bass
from concourse import mybir
import numpy as np

F32 = mybir.dt.float32
F32R = mybir.dt.float32r
I32 = mybir.dt.int32
U32 = mybir.dt.uint32
ACT = mybir.ActivationFunctionType
ALU = mybir.AluOpType
AX = mybir.AxisListType

P = 128
SEQ = 1024
D = 1024
KT = D // P
NT = SEQ // P
GLA_H, GLA_K, GLA_V, RANK = 4, D // 16, D // 8, 16
HG_H, HG_F, HG_I = 4, D // 16, D // 16
CONV_C, CONV_W = D // 4, 3
NE, TOPK, DFF = 32, 4, D
LN_EPS, RMS_EPS = 1e-5, 1e-6
ALPHA = 2.0 ** 0.25
SWIGLU_LIMIT, SWIGLU_ALPHA = 7.0, 1.702
CC = 256
NFM = 7
NTM = 6


class Kit:

    def __init__(self, nc, stack):
        self.nc, self.stack = nc, stack

    def sb(self, name, shape, dt=F32):
        return self.stack.enter_context(self.nc.sbuf_tensor(name, shape, dt))

    def ps(self, name, shape, dt=F32):
        return self.stack.enter_context(self.nc.psum_tensor(name, shape, dt))

    def sem(self, name):
        return self.stack.enter_context(self.nc.semaphore(name))


def project(nc, a, q_all, k_all, G, EG):
    with ExitStack() as stack:
        k = Kit(nc, stack)
        x_all = k.sb("x_all", [P, NT, D])
        hbuf = k.sb("hbuf", [P, 2, D])
        lng, lnb = G[:, 1], G[:, 0]
        stat = k.sb("stat", [P, NT, 2, 6])
        mv = k.sb("mv", [P, NT, 2])
        rstd = k.sb("rstd", [P, NT])
        shift = k.sb("shift", [P, NT])
        hT_hi = k.sb("hT_hi", [P, KT, SEQ], F32R)
        hT_lo = k.sb("hT_lo", [P, KT, SEQ], F32R)
        w_raw = k.sb("w_raw", [P, 2, KT, CC])
        w_hi = k.sb("w_hi", [P, 2, KT, CC], F32R)
        w_lo = k.sb("w_lo", [P, 2, KT, CC], F32R)
        stage = x_all
        wlr = x_all[:, 4, 0:KT * RANK].rearrange("p (k r) -> p k r", r=RANK)
        wlr_split = k.sb("wlr_split", [P, KT, 2 * RANK], F32R)
        z, t = (x_all[:, r:r + 2, :].rearrange("p a b -> p (a b)") for r in (4, 6))
        u = hbuf[:].rearrange("p a b -> p (a b)")
        restart = G[:, 1]
        lrT = G[0:2 * RANK, 0]
        expand = k.sb("expand", [2 * RANK, GLA_H * GLA_K])
        col = k.sb("col", [P, 4])
        lb = k.sb("lb", [P, 6])
        tmp = k.sb("tmp", [P, 4])
        s_par, s_restart = k.sem("gate_params_loaded"), k.sem("restart_loaded")
        s_z, s_zev, s_d, s_a = k.sem("logits_ready"), k.sem("logits_evacuated"), k.sem("dve_steps"), k.sem("act_steps")
        s_wlrs, s_lrev = k.sem("wlr_split_ready"), k.sem("lr_evacuated")
        flat = lambda x: x.rearrange("p a b -> p (a b)")
        row = lambda x, f: x[:, f * SEQ:(f + 1) * SEQ]
        ps = k.ps("psA", [P, 8, 512])
        s_ln, s_wlr = k.sem("ln_params_loaded"), k.sem("wlr_loaded")
        s_x = [k.sem(f"x_half{p}_loaded") for p in range(2)]
        s_w = [k.sem(f"w_raw{p}_loaded") for p in range(2)]
        s_hout = [k.sem(f"hbuf{p}_stored") for p in range(2)]
        s_out = [k.sem(f"stage{p}_stored") for p in range(2)]
        s_st, s_mv, s_ve, s_sq, s_rs = (k.sem(n) for n in ("stats_done", "mean_var_done", "var_eps_done", "sqrt_done", "shift_done"))
        s_xg, s_h = k.sem("x_times_g"), k.sem("h_ready")
        s_tp, s_hi, s_lo = k.sem("h_transposed"), k.sem("hT_hi_ready"), k.sem("hT_lo_ready")
        s_whi, s_wlo = k.sem("w_hi_ready"), k.sem("w_lo_ready")
        s_mm, s_ev = k.sem("chunk_multiplied"), k.sem("chunk_evacuated")
        s_lr = k.sem("lr_multiplied")
        n_chunks = NFM + NTM
        half = NT // 2
        LOCAL = 4

        def ps_tp(p):
            return ps[:, 2 * p:2 * p + 2, :].rearrange("p a (b c) -> p (a b) c", c=P)

        def w_high(j):
            act, p = nc.scalar, j % 2
            act.wait_ge(s_w[p], (j // 2) * 16 + 16)
            if j >= 2:
                act.wait_ge(s_mm, j - 1)
            nc.scalar.copy(w_hi[:, p], w_raw[:, p]).then_inc(s_whi, 1)

        def w_low(j):
            dve, p = nc.vector, j % 2
            dve.wait_ge(s_whi, j + 1)
            nc.vector.tensor_tensor(w_lo[:, p], w_raw[:, p], w_hi[:, p].bitcast(F32), ALU.subtract).then_inc(s_wlo, 1)

        def evacuate_local(j):
            act, p = nc.scalar, j % 2
            act.wait_ge(s_mm, j + 1)
            dst = (q_all, k_all)[j % 2][:, j // 2 * 2:j // 2 * 2 + 2, :]
            nc.scalar.activation(flat(dst), flat(ps[:, 4 * p:4 * p + 4, :]), ACT.Silu if j == 2 else ACT.Copy,
                                 scale=GLA_K ** -0.5 if j == 0 else 1.0).then_inc(s_ev, 1)

        def evacuate(j):
            act, p = nc.scalar, j % 2
            act.wait_ge(s_mm, j + 1)
            if j >= LOCAL + 2:
                act.wait_ge(s_out[p], (j - LOCAL) // 2 * 16)
            dst = stage[:, 2 * p:2 * p + 2, :]
            nc.scalar.copy(flat(dst), flat(ps[:, 4 * p:4 * p + 4, :])).then_inc(s_ev, 1)
            act.wait_ge(s_ev, j + 1)
            if j < NFM:
                act.dma_start(a["projT_d"][(j - LOCAL) * CC:(j - LOCAL + 1) * CC, :].rearrange("(f p) t -> p f t", p=P), dst).then_inc(s_out[p], 16)
            else:
                act.dma_start(a["projM_d"][:, (j - NFM) * CC:(j - NFM + 1) * CC].rearrange("(t p) c -> p t c", p=P),
                              dst.rearrange("p a (b c) -> p (a b) c", c=CC)).then_inc(s_out[p], 16)

        done = {"dve": 0, "act": 0}
        s_a2 = k.sem("act_functions")
        with nc.Block() as block:
            @block.sync
            def _(sp):
                for q in range(2):
                    sp.dma_start(x_all[:, q * half:(q + 1) * half, :],
                                 a["x"][q * half * P:(q + 1) * half * P, :].rearrange("(t p) d -> p t d", p=P)).then_inc(s_x[q], 16)
                sp.dma_start(lng, a["ln_in_g"].partition_broadcast(P)).then_inc(s_ln, 16)
                sp.dma_start(lnb, a["ln_in_b"].partition_broadcast(P)).then_inc(s_ln, 16)
                for j in range(2):
                    sp.dma_start(w_raw[:, j], a["w_cols"][j]).then_inc(s_w[j % 2], 16)
                sp.dma_start(expand[:], a["w_expand"]).then_inc(s_par, 16)
                sp.dma_start(col[:], a["gate_cols"]).then_inc(s_par, 16)
                with sp.Fori(0, half) as i:
                    for p in range(2):
                        sp.wait_ge(s_h, i * 2 + p + 1)
                        sp.dma_start(a["h_d"][bass.ds(i * 2 * P + p * P, P), :], hbuf[:, p]).then_inc(s_hout[p], 16)
                sp.dma_start(restart, a["restart_c"]).then_inc(s_restart, 16)
                sp.dma_start(wlr, a["w_lr"]).then_inc(s_wlr, 16)
                for j in range(2, n_chunks):
                    sp.wait_ge(s_wlo, j - 1)
                    sp.dma_start(w_raw[:, j % 2], a["w_cols"][j]).then_inc(s_w[j % 2], 16)
                for p in range(2):
                    sp.wait_ge(s_hout[p], 16 * half)

            @block.vector
            def _(dve):
                for tile in range(NT):
                    dve.wait_ge(s_x[tile // half], 16)
                    for c in range(2):
                        nc.vector.bn_stats(stat[:, tile, c, :], x_all[:, tile, c * 512:(c + 1) * 512]).then_inc(s_st, 1)
                dve.wait_ge(s_st, 2 * NT)
                for tile in range(NT):
                    nc.vector.bn_aggr(mv[:, tile, :], stat[:, tile]).then_inc(s_mv, 1)
                dve.wait_ge(s_mv, NT)
                nc.vector.tensor_scalar(rstd[:], mv[:, :, 1], LN_EPS, None, ALU.add).then_inc(s_ve, 1)
                dve.wait_ge(s_sq, 1)
                nc.vector.reciprocal(rstd[:], rstd[:]).then_inc(s_rs, 1)
                dve.wait_ge(s_rs, 1)
                dve.wait_ge(s_ln, 32)

                def normalise(t, p):
                    x = x_all[:, bass.ds(t, 1), :].rearrange("p a b -> p (a b)")
                    nc.vector.scalar_tensor_tensor(x, x, mv[:, bass.ds(t, 1), 0], lng, ALU.subtract, ALU.mult).then_inc(s_xg, 1)
                    dve.wait_ge(s_xg, t + 1)
                    nc.vector.scalar_tensor_tensor(hbuf[:, p], x, rstd[:, bass.ds(t, 1)], lnb, ALU.mult, ALU.add).then_inc(s_h, 1)

                def low_part(t, p):
                    dve.wait_ge(s_hi, t + 1)
                    nc.vector.tensor_tensor(hT_lo[:, :, bass.ds(t * P, P)], ps_tp(p),
                                            hT_hi[:, :, bass.ds(t * P, P)].bitcast(F32), ALU.subtract).then_inc(s_lo, 1)

                for p in range(2):
                    normalise(p, p)
                with dve.Fori(1, NT // 2) as i:
                    for p in range(2):
                        low_part(i * 2 + p - 2, p)
                        dve.wait_ge(s_hout[p], i * 16)
                        normalise(i * 2 + p, p)
                for p in range(2):
                    low_part(NT - 2 + p, p)

                def step(ins, wait=True):
                    done["dve"] += 1
                    ins.then_inc(s_d, 1)
                    if wait:
                        dve.wait_ge(s_d, done["dve"])

                hf = flat(k_all[:, 2:4])
                w_low(0)
                w_low(1)
                dve.wait_ge(s_par, 32)
                step(nc.vector.tensor_tensor(tmp[:, 0:2], col[:, 2:4], col[:, 2:4], ALU.subtract))
                dve.wait_ge(s_a, 1)
                step(nc.vector.reciprocal(tmp[:, 2:4], tmp[:, 0:2]))
                step(nc.vector.tensor_tensor(tmp[:, 0:2], tmp[:, 0:2], tmp[:, 2:4], ALU.mult))
                step(nc.vector.tensor_tensor(lb[:, 0:2], tmp[:, 0:2], tmp[:, 0:2], ALU.subtract))
                step(nc.vector.tensor_scalar(lb[:, 2:4], lb[:, 0:2], -1.0, 1.0, ALU.mult, ALU.add))
                step(nc.vector.tensor_scalar(lb[:, 4:6], lb[:, 2:4], -1.0, None, ALU.mult))
                dve.wait_ge(s_wlrs, 1)
                nc.vector.tensor_tensor(wlr_split[:, :, RANK:], wlr, wlr_split[:, :, 0:RANK].bitcast(F32), ALU.subtract).then_inc(s_wlrs, 1)
                for j in range(2, 6):
                    w_low(j)
                dve.wait_ge(s_ev, 4)
                step(nc.vector.scalar_tensor_tensor(t, hf, -1.0, hf, ALU.mult, ALU.min))
                dve.wait_ge(s_a, 2)
                for p in range(2):
                    dve.wait_ge(s_hout[p], 16 * half)
                step(nc.vector.scalar_tensor_tensor(u, hf, 0.0, t, ALU.min, ALU.subtract))
                step(nc.vector.tensor_scalar(t, u, -1.0, 80.0, ALU.mult, ALU.min))
                w_low(6)
                dve.wait_ge(s_a, 4)
                for f in range(2):
                    step(nc.vector.tensor_scalar(k_all[:, 2 + f], k_all[:, 2 + f], lb[:, 4 + f:5 + f], lb[:, 2 + f:3 + f], ALU.mult, ALU.add), False)
                    step(nc.vector.tensor_scalar(row(t, f), row(t, f), -1.0, lb[:, f:f + 1], ALU.add, ALU.mult))
                w_low(7)
                dve.wait_ge(s_a, 5)
                step(nc.vector.tensor_tensor(u, u, t, ALU.add))
                dve.wait_ge(s_restart, 16)
                for f in range(2):
                    step(nc.vector.tensor_tensor_scan(G[:, 2 + f], restart, row(u, f), 0.0, ALU.mult, ALU.add))
                w_low(8)
                dve.wait_ge(s_z, 1)
                for f in range(2):
                    last = nc.vector.tensor_scalar(row(z, f), flat(ps[:, 4 + 2 * f:6 + 2 * f, :]), col[:, f:f + 1], None, ALU.add)
                last.then_inc(s_zev, 1)
                dve.wait_ge(s_zev, 1)
                step(nc.vector.scalar_tensor_tensor(t, z, -1.0, z, ALU.mult, ALU.min))
                dve.wait_ge(s_a, 6)
                step(nc.vector.scalar_tensor_tensor(u, z, 0.0, t, ALU.min, ALU.subtract))
                for f in range(2):
                    step(nc.vector.tensor_tensor_scan(G[:, f], restart, row(u, f), 0.0, ALU.mult, ALU.add))
                for j in range(9, n_chunks):
                    w_low(j)

            @block.scalar
            def _(act):
                act.wait_ge(s_ve, 1)
                nc.scalar.activation(rstd[:], rstd[:], ACT.Sqrt).then_inc(s_sq, 1)
                with act.Fori(0, NT // 2) as i:
                    for p in range(2):
                        act.wait_ge(s_tp, i * 2 + p + 1)
                        nc.scalar.copy(hT_hi[:, :, bass.ds(i * 2 * P + p * P, P)], ps_tp(p)).then_inc(s_hi, 1)

                def step(*functions):
                    for n, (x, function, scale, bias) in enumerate(functions):
                        done["act"] += 1
                        nc.scalar.activation(x[0], x[-1], function, scale=scale, bias=bias).then_inc(s_a2, 1)
                        act.wait_ge(s_a2, done["act"])
                    act.sem_inc(s_a, 1)

                act.wait_ge(s_wlr, 16)
                nc.scalar.copy(wlr_split[:, :, 0:RANK], wlr).then_inc(s_wlrs, 1)
                w_high(0)
                w_high(1)
                act.wait_ge(s_d, 1)
                step(((tmp[:, 0:2],), ACT.Exp, 1.0, 0.0))
                for j in range(LOCAL):
                    evacuate_local(j)
                    w_high(j + 2)
                act.wait_ge(s_d, 7)
                step(((t,), ACT.Exp, 1.0, 0.0), ((t,), ACT.Ln, 1.0, 1.0))
                evacuate(4)
                w_high(6)
                act.wait_ge(s_d, 9)
                step(((flat(k_all[:, 2:4]), u), ACT.Exp, 1.0, 0.0))
                step(((t,), ACT.Exp, 1.0, 0.0))
                act.wait_ge(s_d, 13)
                step(((t,), ACT.Ln, 1.0, 1.0))
                evacuate(5)
                w_high(7)
                evacuate(6)
                w_high(8)
                act.wait_ge(s_lr, 1)
                nc.scalar.copy(lrT, flat(ps[0:2 * RANK, 4:6, :])).then_inc(s_lrev, 1)
                act.wait_ge(s_d, 17)
                step(((t,), ACT.Exp, 1.0, 0.0), ((t,), ACT.Ln, 1.0, 1.0))
                for j in range(NFM, n_chunks):
                    evacuate(j)
                    if j + 2 < n_chunks:
                        w_high(j + 2)
                act.wait_ge(s_d, 20)
                last = G[:].rearrange("p g (c t) -> p g c t", t=CH)[:, :, :, CH - 1]
                nc.scalar.activation(EG[:, 0:2], last[:, 0:2], ACT.Exp, scale=group_scale(0))
                nc.scalar.activation(EG[:, 2:4], last[:, 2:4], ACT.Exp)
                act.wait_ge(s_out[0], 16 * ((n_chunks - LOCAL + 1) // 2))
                act.wait_ge(s_out[1], 16 * ((n_chunks - LOCAL) // 2))

            @block.tensor
            def _(pe):
                pe.wait_ge(a["consts_loaded"], 16)

                def transpose_tile(t, p, first):
                    pe.wait_ge(s_h, t + 1)
                    if not first:
                        pe.wait_ge(s_lo, t - 1)
                    for kt in range(KT):
                        last = nc.tensor.transpose(ps_tp(p)[:, kt, :], hbuf[:, p, kt * P:(kt + 1) * P], a["ident"][:])
                    last.then_inc(s_tp, 1)

                for p in range(2):
                    transpose_tile(p, p, True)
                with pe.Fori(1, NT // 2) as i:
                    for p in range(2):
                        transpose_tile(i * 2 + p, p, False)
                pe.wait_ge(s_lo, NT)

                def feature_major(j, p, first=False):
                    pe.wait_ge(s_wlo, j + 1)
                    if not first:
                        pe.wait_ge(s_ev, j - 1)
                    for ft in range(2):
                        for kt in range(KT):
                            w = slice(ft * P, (ft + 1) * P)
                            for n, (wt, ht) in enumerate(((w_hi, hT_hi), (w_hi, hT_lo), (w_lo, hT_hi))):
                                for h in range(2):
                                    last = nc.tensor.matmul(ps[:, p * 4 + ft * 2 + h, :], wt[:, p, kt, w], ht[:, kt, h * 512:(h + 1) * 512],
                                                            start=(kt == 0 and n == 0), stop=(kt == KT - 1 and n == 2))
                    last.then_inc(s_mm, 1)

                def token_major(j, p):
                    pe.wait_ge(s_wlo, j + 1)
                    pe.wait_ge(s_ev, j - 1)
                    for t in range(NT):
                        for kt in range(KT):
                            for n, (wt, ht) in enumerate(((w_hi, hT_hi), (w_lo, hT_hi), (w_hi, hT_lo))):
                                last = nc.tensor.matmul(ps[:, p * 4 + t // 2, (t % 2) * CC:(t % 2 + 1) * CC], ht[:, kt, t * P:(t + 1) * P],
                                                        wt[:, p, kt, :], start=(kt == 0 and n == 0), stop=(kt == KT - 1 and n == 2))
                    last.then_inc(s_mm, 1)

                for p in range(2):
                    feature_major(p, p, True)
                with pe.Fori(1, (NFM - 1) // 2) as i:
                    for p in range(2):
                        feature_major(i * 2 + p, p)
                feature_major(NFM - 1, 0)
                pe.wait_ge(s_wlrs, 2)
                pe.wait_ge(s_ev, NFM - 1)
                for h in range(2):
                    for kt in range(KT):
                        for n, ht in enumerate((hT_hi, hT_lo)):
                            last = nc.tensor.matmul(ps[0:2 * RANK, 4 + h, :], wlr_split[:, kt, :], ht[:, kt, h * 512:(h + 1) * 512],
                                                    start=(kt == 0 and n == 0), stop=(kt == KT - 1 and n == 1))
                last.then_inc(s_lr, 1)
                pe.wait_ge(s_lrev, 1)
                pe.wait_ge(s_par, 32)
                for f in range(2):
                    for h in range(2):
                        last = nc.tensor.matmul(ps[:, 4 + 2 * f + h, :], expand[:, f * P:(f + 1) * P], lrT[:, h * 512:(h + 1) * 512],
                                                start=True, stop=True)
                last.then_inc(s_z, 1)
                pe.wait_ge(s_zev, 1)
                with pe.Fori(0, NTM // 2) as i:
                    for p in (1, 0):
                        token_major(i * 2 + (NFM + 1 - p), p)


NG = 4
LEVELS = 7
CH = P


def group_dv(g):
    return GLA_V if g < 2 else HG_I


def group_cols(g):
    return slice(2 * GLA_V * g, 2 * GLA_V * (g + 1)) if g < 2 else \
        slice(GLA_H * GLA_V + 2 * HG_I * (g - 2), GLA_H * GLA_V + 2 * HG_I * (g - 1))


def group_scale(g):
    return 1.0 / 16.0 if g < 2 else 1.0


def mix(nc, a, v_all, q_all, k_all, G, EG):
    with ExitStack() as stack:
        k = Kit(nc, stack)
        KL = k.sb("KL", [P, 2, LEVELS, SEQ])
        QL = k.sb("QL", [P, 2, LEVELS, SEQ // 2])
        QH = k.sb("QH", [P, 2, SEQ])
        KH = k.sb("KH", [P, 2, SEQ])
        E = k.sb("E", [P, 2, SEQ])
        EF = k.sb("EF", [P, SEQ])
        S = k.sb("S", [P, 2, 2, CH])
        khat = k.sb("khat", [P, 2, P])
        state = k.sb("state", [P, 2, 2, 2 * GLA_V])
        masks = k.sb("masks", [P, 6, CH // 2], I32)
        diag = k.sb("diag", [P, CH], I32)
        psX = k.ps("psX", [P, 2, 2, 512])
        psC = k.ps("psC", [P, 2, 512])
        psO = k.ps("psO", [P, 512])
        psU = k.ps("psU", [P, 512])
        s_zero, s_mask = k.sem("zeroed"), k.sem("masks_loaded")
        s_sub, s_exp, s_qm, s_km = k.sem("exponents_ready"), k.sem("decays_ready"), k.sem("q_decayed"), k.sem("k_decayed")
        s_sc, s_xd, s_xa, s_ap, s_st, s_o = (k.sem(n) for n in (
            "scores_done", "fine_levels_copied", "coarse_levels_copied", "chunk_applied", "state_ready", "o_ready"))
        s_lv, s_v = k.sem("level_copied"), k.sem("v_loaded")
        zrow = k.sb("zrow", [P, D])
        s_zrow, s_yz = k.sem("zero_row_ready"), k.sem("y_overflow_zeroed")
        steps = NG * NT

        def halves(x, level):
            return x.rearrange("p (b h s) -> p b h s", h=2, s=1 << level)

        def exponents(g, item):
            m = 8 * g + item
            if m >= 2:
                nc.vector.wait_ge(s_km, m - 1)
                nc.vector.wait_ge(s_qm, m - 1)
            e = E[:, item % 2]
            if item == 0:
                gc = G[:, g].rearrange("p (c t) -> p c t", t=CH)
                nc.vector.tensor_tensor(e.rearrange("p (c t) -> p c t", t=CH), gc[:, :, CH - 1:CH].broadcast_to((P, NT, CH)), gc,
                                        ALU.subtract).then_inc(s_sub, 1)
                return
            level, s = item - 1, 1 << (item - 1)
            gh, eh = halves(G[:, g], level), halves(e, level)
            ref = gh[:, :, 0, s - 1:s].broadcast_to((P, SEQ // (2 * s), s))
            nc.vector.tensor_tensor(eh[:, :, 0, :], ref, gh[:, :, 0, :], ALU.subtract)
            nc.vector.tensor_tensor(eh[:, :, 1, :], gh[:, :, 1, :], ref, ALU.subtract).then_inc(s_sub, 1)

        def decay_q(g, item):
            nc.vector.wait_ge(s_exp, 8 * g + item + 1)
            if item == 0:
                nc.vector.tensor_tensor(QH[:, g % 2], q_all[:, g], EF[:], ALU.mult).then_inc(s_qm, 1)
                return
            level, s = item - 1, 1 << (item - 1)
            nc.vector.tensor_tensor(QL[:, g % 2, level].rearrange("p (b s) -> p b s", s=s), halves(q_all[:, g], level)[:, :, 1, :],
                                    halves(E[:, item % 2], level)[:, :, 1, :], ALU.mult).then_inc(s_qm, 1)

        with nc.Block() as block:
            @block.sync
            def _(sp):
                m = a["projM_d"].rearrange("(t p) c -> p t c", p=P)
                sp.dma_start(v_all[:, :, 0:512], m[:, :, 0:512]).then_inc(s_v, 16)
                sp.dma_start(v_all[:, :, 512:768], m[:, :, 1024:1280]).then_inc(s_v, 16)
                sp.dma_start(masks[:], a["level_masks"]).then_inc(s_mask, 16)
                sp.dma_start(diag[:], a["diag_mask"]).then_inc(s_mask, 16)
                sp.wait_ge(s_zrow, 1)
                over = a["y_d"][NE * CAP:, :]
                n = NB_OVER * CAP // P
                sp.dma_start(over[0:n * P].rearrange("(n p) d -> p n d", p=P), zrow[:].unsqueeze(1).broadcast_to((P, n, D))).then_inc(s_yz, 16)
                sp.dma_start(over[n * P:], zrow[0:NB_OVER * CAP - n * P]).then_inc(s_yz, 16)
                sp.wait_ge(s_yz, 32)

            @block.gpsimd
            def _(pool):
                nc.gpsimd.memset(zrow[:], 0.0).then_inc(s_zrow, 1)
                nc.gpsimd.memset(S[:], 0.0).then_inc(s_zero, 1)
                nc.gpsimd.memset(KL[:], 0.0).then_inc(s_zero, 1)
                nc.gpsimd.memset(state[:], 0.0).then_inc(s_zero, 1)
                pool.wait_ge(s_zero, 3)
                for g in range(NG):
                    if g >= 2:
                        pool.wait_ge(s_ap, NT * (g - 1))
                    for item in range(8):
                        pool.wait_ge(s_exp, 8 * g + item + 1)
                        if item == 0:
                            nc.gpsimd.tensor_tensor(KH[:, g % 2], k_all[:, g], E[:, 0], ALU.mult).then_inc(s_km, 1)
                        else:
                            nc.gpsimd.tensor_tensor(halves(KL[:, g % 2, item - 1], item - 1)[:, :, 0, :], halves(k_all[:, g], item - 1)[:, :, 0, :],
                                                    halves(E[:, item % 2], item - 1)[:, :, 0, :], ALU.mult).then_inc(s_km, 1)

            @block.vector
            def _(dve):
                def prepare(g, step):
                    if step < 8:
                        exponents(g, step)
                    if step > 0:
                        decay_q(g, step - 1)

                for step in range(9):
                    prepare(0, step)
                dve.wait_ge(s_zero, 3)
                dve.wait_ge(s_mask, 32)
                for n in range(steps):
                    g, c, p = n // NT, n % NT, n % 2
                    dve.wait_ge(s_sc, n + 1)
                    for level in range(6):
                        s = 1 << level
                        out = S[:, p].rearrange("p n (b h s) -> p n b h s", h=2, s=s)[:, :, :, 1, :]
                        mask = masks[:, level].rearrange("p (b s) -> p b s", s=s).unsqueeze(1).broadcast_to((P, 2, CH // (2 * s), s))
                        src = psX[:, p, :, level * 64:level * 64 + 64].rearrange("p n (b s) -> p n b s", s=s)
                        nc.vector.copy_predicated(out, mask, src).then_inc(s_lv, 1)
                        dve.wait_ge(s_lv, 6 * n + level + 1)
                    nc.vector.copy_predicated(S[:, p], diag[:].unsqueeze(1).broadcast_to((P, 2, CH)),
                                              psX[:, p, :, 6 * 64:6 * 64 + CH]).then_inc(s_xd, 1)
                    if g + 1 < NG:
                        if c == 0 and g >= 1:
                            dve.wait_ge(s_ap, NT * g)
                        prepare(g + 1, c)
                        if c == NT - 1:
                            prepare(g + 1, NT)
                    dv = group_dv(g)
                    dve.wait_ge(s_ap, n + 1)
                    if c:
                        dve.wait_ge(s_st, n)
                    for h in range(2):
                        f, cols = slice(64 * h, 64 * h + 64), slice(h * dv, (h + 1) * dv)
                        new, update = state[f, g // 2, p, cols], psU[f, cols]
                        if c == 0:
                            last = nc.vector.tensor_copy(new, update)
                        else:
                            last = nc.vector.scalar_tensor_tensor(new, state[f, g // 2, 1 - p, cols], EG[f, g, c:c + 1], update, ALU.mult, ALU.add)
                    last.then_inc(s_st, 1)

            @block.scalar
            def _(act):
                def decays(g, item):
                    act.wait_ge(s_sub, 8 * g + item + 1)
                    if item == 0:
                        if g:
                            act.wait_ge(s_qm, 8 * g - 7)
                        nc.scalar.activation(EF[:], G[:, g], ACT.Exp, scale=group_scale(g))
                    nc.scalar.activation(E[:, item % 2], E[:, item % 2], ACT.Exp, scale=group_scale(g)).then_inc(s_exp, 1)

                for item in range(8):
                    decays(0, item)
                act.wait_ge(s_zero, 3)
                for n in range(steps):
                    g, c, p = n // NT, n % NT, n % 2
                    act.wait_ge(s_sc, n + 1)
                    if n >= 2:
                        act.wait_ge(s_ap, n - 1)
                    nc.scalar.copy(khat[:, p], psC[:, 0, 64:64 + P])
                    act.wait_ge(s_xd, n + 1)
                    nc.scalar.copy(S[0:64, p, :, 64:128], psC[0:64, :, 0:64]).then_inc(s_xa, 1)
                    if g + 1 < NG:
                        decays(g + 1, c)
                    act.wait_ge(s_ap, n + 1)
                    nc.scalar.copy(v_all[:, c, group_cols(g)], psO[:, 0:2 * group_dv(g)]).then_inc(s_o, 1)

            @block.tensor
            def _(pe):
                def scores(n):
                    g, c, p = n // NT, n % NT, n % 2
                    pe.wait_ge(s_qm, 8 * g + 8)
                    pe.wait_ge(s_km, 8 * g + 8)
                    if n >= 2:
                        pe.wait_ge(s_xd, n - 1)
                    t = slice(c * CH, (c + 1) * CH)

                    def level_scores(out, level):
                        nc.tensor.matmul(out, KL[f, g % 2, level, t], QL[f, g % 2, level, c * 64:c * 64 + 64], start=True, stop=True)

                    for h in range(2):
                        f = slice(64 * h, 64 * h + 64)
                        for level in range(6):
                            level_scores(psX[:, p, h, level * 64:level * 64 + 64], level)
                        nc.tensor.matmul(psX[:, p, h, 6 * 64:6 * 64 + CH], k_all[f, g, t], q_all[f, g, t], start=True, stop=True)
                    if n >= 1:
                        pe.wait_ge(s_xa, n)
                    for h in range(2):
                        f = slice(64 * h, 64 * h + 64)
                        level_scores(psC[:, h, 0:64], 6)
                    nc.tensor.transpose(psC[:, 0, 64:64 + P], KH[:, g % 2, t], a["ident"][:]).then_inc(s_sc, 1)

                def apply(n):
                    g, c, p = n // NT, n % NT, n % 2
                    dv = group_dv(g)
                    v = v_all[:, c, group_cols(g)]
                    pe.wait_ge(s_xd, n + 1)
                    pe.wait_ge(s_xa, n + 1)
                    if n >= 1:
                        pe.wait_ge(s_o, n)
                        pe.wait_ge(s_st, n)
                    if c:
                        nc.tensor.matmul(psO[:, 0:2 * dv], QH[:, g % 2, c * CH:(c + 1) * CH], state[:, g // 2, 1 - p, 0:2 * dv],
                                         start=True, stop=False)
                    for h in range(2):
                        cols = slice(h * dv, (h + 1) * dv)
                        nc.tensor.matmul(psO[:, cols], S[:, p, h], v[:, cols], start=(c == 0), stop=(c == 0 or h == 1))
                    nc.tensor.matmul(psU[:, 0:2 * dv], khat[:, p], v, start=True, stop=True).then_inc(s_ap, 1)

                scores(0)
                pe.wait_ge(s_v, 32)
                for n in range(steps):
                    if n + 1 < steps:
                        scores(n + 1)
                    apply(n)


def mixers(nc, a):
    with ExitStack() as stack:
        k = Kit(nc, stack)
        qkg = k.sb("qkg", [P, 3 * NG, SEQ])
        q_all, k_all, G = (qkg[:, NG * n:NG * (n + 1)] for n in range(3))
        EG = k.sb("EG", [P, NG, NT])
        project(nc, a, q_all, k_all, G, EG)
        v_all = k.sb("v_all", [P, NT, 768])
        mix(nc, a, v_all, q_all, k_all, G, EG)
        yT_hi = k.sb("yT_hi", [P, KT, SEQ], F32R)
        yT_lo = k.sb("yT_lo", [P, KT, SEQ], F32R)
        mixer_outputs(nc, a, v_all, yT_hi, yT_lo)
        project_out(nc, a, yT_hi, yT_lo, qkg)


def mixer_outputs(nc, a, o_all, yT_hi, yT_lo):
    with ExitStack() as stack:
        k = Kit(nc, stack)
        gate = k.sb("out_gate", [P, NT, 768])
        gn = k.sb("gn", [P, 768])
        sq = k.sb("sq", [P, 2, 768])
        ms = k.sb("ms", [P, NT, 8])
        cv = k.sb("cv", [P, 4, SEQ])
        u = k.sb("u", [P, SEQ])
        cw = k.sb("cw", [P, 2, CONV_W])
        ps = k.ps("psY", [P, 2, 1024])
        s_g, s_p = k.sem("gates_loaded"), k.sem("norm_params_loaded")
        s_cv = [k.sem(f"conv{f}_loaded") for f in range(2)]
        s_silu, s_sq, s_ms, s_d, s_sqrt, s_rms = (k.sem(n) for n in (
            "silu_done", "squared", "sums_done", "dve_steps", "sqrt_done", "rms_ready"))
        s_n, s_y, s_tp, s_hi, s_lo = (k.sem(n) for n in ("normed", "y_ready", "y_transposed", "yT_hi_ready", "yT_lo_ready"))
        s_gn = k.sem("gates_scaled")
        s_cs, s_chi, s_clo = k.sem("conv_steps"), k.sem("conv_hi_ready"), k.sem("conv_lo_ready")
        heads = lambda x, part: (x[:, 0:512] if part == 0 else x[:, 512:768]).rearrange("p (n d) -> p n d", n=4)

        def ps_tile(p):
            return ps[:, p, 0:768].rearrange("p (f t) -> p f t", t=P)

        with nc.Block() as block:
            @block.sync
            def _(sp):
                m = a["projM_d"].rearrange("(t p) c -> p t c", p=P)
                sp.dma_start(gate[:, :, 0:512], m[:, :, 512:1024]).then_inc(s_g, 16)
                sp.dma_start(gate[:, :, 512:768], m[:, :, 1280:1536]).then_inc(s_g, 16)
                sp.dma_start(gn[:], a["norm_row"].partition_broadcast(P)).then_inc(s_p, 16)
                sp.dma_start(cw[:], a["conv_cols"]).then_inc(s_p, 16)
                for f in range(2):
                    if f:
                        sp.wait_ge(s_clo, f)
                    for n in range(3):
                        r = CC * n + f * P
                        sp.dma_start(cv[:, n], a["projT_d"][r:r + P, :]).then_inc(s_cv[f], 16)
                sp.wait_ge(s_cv[1], 48)

            @block.vector
            def _(dve):
                steps = [0]

                def step(ins):
                    steps[0] += 1
                    ins.then_inc(s_cs, 1)
                    dve.wait_ge(s_cs, steps[0])

                for t in range(NT):
                    dve.wait_ge(s_sq, t + 1)
                    for part in range(2):
                        last = nc.vector.tensor_reduce(ms[:, t, 4 * part:4 * part + 4], heads(sq[:, t % 2], part), AX.X, ALU.add)
                    last.then_inc(s_ms, 1)
                dve.wait_ge(s_ms, NT)
                nc.vector.tensor_scalar(ms[:, :, 0:4], ms[:, :, 0:4], 1.0 / GLA_V, RMS_EPS, ALU.mult, ALU.add)
                nc.vector.tensor_scalar(ms[:, :, 4:8], ms[:, :, 4:8], 1.0 / HG_I, RMS_EPS, ALU.mult, ALU.add).then_inc(s_d, 1)
                dve.wait_ge(s_sqrt, 1)
                nc.vector.reciprocal(ms[:], ms[:]).then_inc(s_rms, 1)
                dve.wait_ge(s_rms, 1)

                def low_part(t):
                    dve.wait_ge(s_hi, t + 1)
                    nc.vector.tensor_tensor(yT_lo[:, 0:6, t * P:(t + 1) * P], ps_tile(t % 2), yT_hi[:, 0:6, t * P:(t + 1) * P].bitcast(F32),
                                            ALU.subtract).then_inc(s_lo, 1)

                for t in range(NT):
                    for part, dv in ((0, GLA_V), (1, HG_I)):
                        o = heads(o_all[:, t], part)
                        last = nc.vector.tensor_tensor(o, o, ms[:, t, 4 * part:4 * part + 4].unsqueeze(2).broadcast_to((P, 4, dv)), ALU.mult)
                    last.then_inc(s_n, 1)
                    if t > 1:
                        low_part(t - 2)
                    dve.wait_ge(s_n, t + 1)
                    dve.wait_ge(s_gn, t + 1)
                    nc.vector.tensor_tensor(o_all[:, t], o_all[:, t], gate[:, t], ALU.mult).then_inc(s_y, 1)
                low_part(NT - 2)
                low_part(NT - 1)
                dve.wait_ge(s_p, 32)
                for f in range(2):
                    dve.wait_ge(s_cv[f], 48)
                    acc = cv[:, 3]
                    step(nc.vector.tensor_tensor(u[:], cv[:, 1], cv[:, 2], ALU.mult))
                    step(nc.vector.tensor_scalar(acc, u[:], cw[:, f, 2:3], None, ALU.mult))
                    for lag in (1, 2):
                        step(nc.vector.scalar_tensor_tensor(acc[:, lag:], u[:, :SEQ - lag], cw[:, f, 2 - lag:3 - lag], acc[:, lag:], ALU.mult, ALU.add))
                    step(nc.vector.tensor_tensor(acc, acc, cv[:, 0], ALU.mult))
                    dve.wait_ge(s_chi, f + 1)
                    nc.vector.tensor_tensor(yT_lo[:, 6 + f], acc, yT_hi[:, 6 + f].bitcast(F32), ALU.subtract).then_inc(s_clo, 1)
                    dve.wait_ge(s_clo, f + 1)

            @block.gpsimd
            def _(pool):
                pool.wait_ge(s_p, 32)
                for t in range(NT):
                    pool.wait_ge(s_silu, t + 1)
                    nc.gpsimd.tensor_tensor(gate[:, t], gate[:, t], gn[:], ALU.mult).then_inc(s_gn, 1)

            @block.scalar
            def _(act):
                for t in range(NT):
                    if t >= 2:
                        act.wait_ge(s_ms, t - 1)
                    nc.scalar.activation(sq[:, t % 2], o_all[:, t], ACT.Square).then_inc(s_sq, 1)
                act.wait_ge(s_g, 32)
                for t in range(NT):
                    nc.scalar.activation(gate[:, t], gate[:, t], ACT.Silu).then_inc(s_silu, 1)
                act.wait_ge(s_d, 1)
                nc.scalar.activation(ms[:], ms[:], ACT.Sqrt).then_inc(s_sqrt, 1)
                for t in range(NT):
                    act.wait_ge(s_tp, t + 1)
                    nc.scalar.copy(yT_hi[:, 0:6, t * P:(t + 1) * P], ps_tile(t % 2)).then_inc(s_hi, 1)
                for f in range(2):
                    act.wait_ge(s_cs, 5 * f + 5)
                    nc.scalar.copy(yT_hi[:, 6 + f], cv[:, 3]).then_inc(s_chi, 1)

            @block.tensor
            def _(pe):
                for t in range(NT):
                    pe.wait_ge(s_y, t + 1)
                    if t >= 2:
                        pe.wait_ge(s_lo, t - 1)
                    for f in range(6):
                        last = nc.tensor.transpose(ps_tile(t % 2)[:, f], o_all[:, t, f * P:(f + 1) * P], a["ident"][:])
                    last.then_inc(s_tp, 1)


def project_out(nc, a, yT_hi, yT_lo, qkg):
    with ExitStack() as stack:
        k = Kit(nc, stack)
        wo_hi = k.sb("wo_hi", [P, KT, D], F32R)
        wo_lo = k.sb("wo_lo", [P, KT, D], F32R)
        wo_raw = qkg[:, 8:12].rearrange("p (a b) (c n) -> p a (b c) n", a=2, n=CC)
        lng, lnb, h = qkg[:, 0], qkg[:, 1], qkg[:, 2:4]
        r, hT = qkg[:, 4:6], qkg[:, 6:8]
        wr, br = k.sb("wr", [P, KT, NE]), k.sb("br", [P, NE])
        stat, mv, rs = k.sb("stat2", [P, 2, 2, 6]), k.sb("mv2", [P, 2, 2]), k.sb("rs2", [P, 2])
        logits = a["logits"]
        psM = k.ps("psM", [P, 2, D])
        psT = k.ps("psT", [P, D])
        psL = k.ps("psL", [P, 512])
        s_w = [k.sem(f"wo_raw{p}_loaded") for p in range(2)]
        s_h = [k.sem(f"h_in{p}_loaded") for p in range(2)]
        s_st = [k.sem(f"h2_{p}_stored") for p in range(2)]
        s_p, s_hi, s_lo, s_mm, s_d, s_sq, s_h2, s_tp, s_hT, s_lg, s_ev = (k.sem(n) for n in (
            "mix_params_loaded", "wo_hi_ready", "wo_lo_ready", "mix_multiplied", "dve_steps", "sqrt_done", "h2_ready",
            "h2_transposed", "h2T_ready", "logits_multiplied", "logits_ready"))
        n_cols = D // CC

        with nc.Block() as block:
            @block.sync
            def _(sp):
                for dst, src in ((lng, "ln_mix_g"), (lnb, "ln_mix_b"), (br[:], "b_router")):
                    sp.dma_start(dst, a[src].partition_broadcast(P)).then_inc(s_p, 16)
                sp.dma_start(wr[:], a["w_router"].rearrange("(k p) e -> p k e", p=P)).then_inc(s_p, 16)
                for c in range(n_cols):
                    if c >= 2:
                        sp.wait_ge(s_lo, c - 1)
                    sp.dma_start(wo_raw[:, c % 2], a["w_out"][:, c * CC:(c + 1) * CC].rearrange("(k p) n -> p k n", p=P)).then_inc(s_w[c % 2], 16)
                for t in range(NT):
                    p = t % 2
                    if t >= 2:
                        sp.wait_ge(s_d, 6 * (t - 2) + 1)
                    sp.dma_start(h[:, p], a["h_d"][t * P:(t + 1) * P, :]).then_inc(s_h[p], 16)
                    if t >= 1:
                        sp.wait_ge(s_h2, t)
                        sp.dma_start(a["h2_d"][(t - 1) * P:t * P, :], r[:, 1 - p]).then_inc(s_st[1 - p], 16)
                sp.wait_ge(s_h2, NT)
                sp.dma_start(a["h2_d"][(NT - 1) * P:, :], r[:, 1]).then_inc(s_st[1], 16)
                for p in range(2):
                    sp.wait_ge(s_st[p], 16 * (NT // 2))

            @block.vector
            def _(dve):
                for c in range(n_cols):
                    dve.wait_ge(s_hi, c + 1)
                    cols = slice(c * CC, (c + 1) * CC)
                    nc.vector.tensor_tensor(wo_lo[:, :, cols], wo_raw[:, c % 2], wo_hi[:, :, cols].bitcast(F32), ALU.subtract).then_inc(s_lo, 1)
                dve.wait_ge(s_p, 64)
                steps = [0]

                def step(ins, wait=True):
                    steps[0] += 1
                    ins.then_inc(s_d, 1)
                    if wait:
                        dve.wait_ge(s_d, steps[0])

                for t in range(NT):
                    p = t % 2
                    dve.wait_ge(s_mm, t + 1)
                    dve.wait_ge(s_h[p], 16 * (t // 2) + 16)
                    if t >= 2:
                        dve.wait_ge(s_st[p], 16 * (t // 2))
                        dve.wait_ge(s_tp, t - 1)
                    step(nc.vector.scalar_tensor_tensor(r[:, p], h[:, p], ALPHA, psM[:, p], ALU.mult, ALU.add))
                    nc.vector.bn_stats(stat[:, p, 0], r[:, p, 0:512])
                    step(nc.vector.bn_stats(stat[:, p, 1], r[:, p, 512:1024]))
                    step(nc.vector.bn_aggr(mv[:, p], stat[:, p]))
                    step(nc.vector.tensor_scalar(rs[:, p:p + 1], mv[:, p, 1:2], LN_EPS, None, ALU.add), False)
                    step(nc.vector.scalar_tensor_tensor(r[:, p], r[:, p], mv[:, p, 0:1], lng, ALU.subtract, ALU.mult), False)
                    if t >= 1:
                        dve.wait_ge(s_lg, t)
                        nc.vector.tensor_tensor(logits[:, t - 1], psL[:, 0:NE], br[:], ALU.add).then_inc(s_ev, 1)
                    dve.wait_ge(s_sq, t + 1)
                    step(nc.vector.reciprocal(rs[:, p:p + 1], rs[:, p:p + 1]))
                    nc.vector.scalar_tensor_tensor(r[:, p], r[:, p], rs[:, p:p + 1], lnb, ALU.mult, ALU.add).then_inc(s_h2, 1)
                dve.wait_ge(s_lg, NT)
                nc.vector.tensor_tensor(logits[:, NT - 1], psL[:, 0:NE], br[:], ALU.add).then_inc(s_ev, 1)

            @block.scalar
            def _(act):
                for c in range(n_cols):
                    act.wait_ge(s_w[c % 2], 16 * (c // 2) + 16)
                    nc.scalar.copy(wo_hi[:, :, c * CC:(c + 1) * CC], wo_raw[:, c % 2]).then_inc(s_hi, 1)
                for t in range(NT):
                    p = t % 2
                    act.wait_ge(s_d, 6 * t + 4)
                    nc.scalar.activation(rs[:, p:p + 1], rs[:, p:p + 1], ACT.Sqrt).then_inc(s_sq, 1)
                    act.wait_ge(s_tp, t + 1)
                    nc.scalar.copy(hT[:, p], psT[:]).then_inc(s_hT, 1)

            @block.tensor
            def _(pe):
                def output_tile(t):
                    p = t % 2
                    if t >= 2:
                        pe.wait_ge(s_d, 6 * (t - 2) + 1)
                    for kt in range(KT):
                        for n, (y, w) in enumerate(((yT_hi, wo_hi), (yT_hi, wo_lo), (yT_lo, wo_hi))):
                            for half in range(2):
                                c = slice(half * 512, half * 512 + 512)
                                last = nc.tensor.matmul(psM[:, p, c], y[:, kt, t * P:(t + 1) * P], w[:, kt, c],
                                                        start=(kt == 0 and n == 0), stop=(kt == KT - 1 and n == 2))
                    last.then_inc(s_mm, 1)

                def logit_tile(t):
                    p = t % 2
                    pe.wait_ge(s_h2, t + 1)
                    if t >= 1:
                        pe.wait_ge(s_hT, t)
                    for kt in range(KT):
                        last = nc.tensor.transpose(psT[:, kt * P:(kt + 1) * P], r[:, p, kt * P:(kt + 1) * P], a["ident"][:])
                    last.then_inc(s_tp, 1)
                    if t >= 1:
                        pe.wait_ge(s_ev, t)
                    pe.wait_ge(s_hT, t + 1)
                    for kt in range(KT):
                        last = nc.tensor.matmul(psL[:, 0:NE], hT[:, p, kt * P:(kt + 1) * P], wr[:, kt], start=(kt == 0), stop=(kt == KT - 1))
                    last.then_inc(s_lg, 1)

                pe.wait_ge(s_lo, n_cols)
                pe.wait_ge(s_p, 64)
                for t in range(NT):
                    output_tile(t)
                    if t >= 1:
                        logit_tile(t - 1)
                logit_tile(NT - 1)


CAP = 160
SIZES = (128, 144, CAP)
NB_OVER = 25
NSLOT = (NE + NB_OVER) * CAP


def route(nc, a, ex):
    before_exp = [0]
    gate, slot_i, idx, ids = a["gate"], a["slot_i"], a["idx"], a["block_expert"]
    with ExitStack() as stack:
        k = Kit(nc, stack)
        lg = a["logits"]
        top, topi = k.sb("top", [P, NT, 8]), k.sb("topi", [P, NT, 8], U32)
        topf = k.sb("topf", [P, NT, TOPK])
        nmax, den = k.sb("nmax", [P, NT]), k.sb("den", [P, NT])
        oh = k.sb("oh", [P, NT, TOPK, NE])
        M, T1, T2, SL = (k.sb(n, [P, NT, NE]) for n in ("M", "T1", "T2", "SL"))
        cnt, nb, first, sizef, B = (k.sb(n, [P, NE]) for n in ("count", "blocks_beyond", "blocks_before", "size", "offset"))
        cmp = k.sb("cmp", [P, NB_OVER, NE])
        bexp = k.sb("bexp", [P, NB_OVER + 1])
        cst = k.sb("cst", [P, 2 * NE + NB_OVER])
        tri, ones = k.sb("tri", [P, P]), k.sb("ones", [P, P])
        slotf = k.sb("slotf", [P, NT, TOPK])
        tok = k.sb("tok", [P, NT])
        zero = k.sb("zero", [P, NSLOT // P + 1])
        rows = k.sb("rows", [NE + NB_OVER, CAP])
        ps = ex.ps[:, 0, 0:NT * NE].rearrange("p (t e) -> p t e", e=NE)
        psC = ex.ps[:, 1]
        psI = ex.ps[:, 2:4]
        s_c, s_d, s_e, s_oh, s_pos, s_slot, s_z, s_m, s_tp, s_zero, s_rows = (k.sem(n) for n in (
            "route_consts_loaded", "dve_steps", "exp_done", "choices_ready", "positions_ready", "slots_ready", "map_zeroed",
            "map_scattered", "map_transposed", "zeros_ready", "map_rows_loaded"))
        n_iota, n_cap, n_blk = slice(0, NE), slice(NE, 2 * NE), slice(2 * NE, 2 * NE + NB_OVER)

        with nc.Block() as block:
            @block.sync
            def _(sp):
                for dst, src in ((cst, "route_c"), (tri, "tri_c"), (tok, "token_c")):
                    sp.dma_start(dst[:], a[src]).then_inc(s_c, 16)
                sp.wait_ge(s_zero, 2)
                flat = a["slot_token_d"].rearrange("s one -> (s one)")
                n = NSLOT // P
                sp.dma_start(flat[0:n * P].rearrange("(p n) -> p n", p=P), zero[:, 0:n]).then_inc(s_z, 16)
                sp.dma_start(flat[n * P:NSLOT].rearrange("(o n) -> o n", o=1), zero[0:1, 0:NSLOT - n * P]).then_inc(s_z, 16)
                for j in range(CHUNKS):
                    ex.load_chunk(sp, 0, j)
                sp.wait_ge(s_m, 16 * NT * TOPK)
                sp.dma_start(rows[:], a["slot_token_d"].rearrange("(b s) one -> b (s one)", s=CAP)).then_inc(s_rows, 16)

            @block.vector
            def _(dve):
                steps = [0]

                def step(ins, wait=True):
                    steps[0] += 1
                    ins.then_inc(s_d, 1)
                    if wait:
                        dve.wait_ge(s_d, steps[0])

                nc.vector.memset(idx[:], 0.0)
                nc.vector.memset(ones[:], 1.0).then_inc(s_zero, 1)
                nc.vector.memset(zero[:], 0.0).then_inc(s_zero, 1)
                for t in range(NT):
                    step(nc.vector.max(top[:, t], lg[:, t]), t == NT - 1)
                for t in range(NT):
                    step(nc.vector.max_index(topi[:, t], top[:, t], lg[:, t]), t == NT - 1)
                step(nc.vector.tensor_copy(topf[:], topi[:, :, 0:TOPK]), False)
                step(nc.vector.tensor_tensor(gate[:], top[:, :, 0:TOPK], top[:, :, 0:1].broadcast_to((P, NT, TOPK)), ALU.subtract))
                before_exp[0] = steps[0]
                dve.wait_ge(s_c, 48)
                step(nc.vector.tensor_tensor(oh[:].rearrange("p t k e -> p (t k) e"),
                                             topf[:].rearrange("p t k -> p (t k)").unsqueeze(2).broadcast_to((P, NT * TOPK, NE)),
                                             cst[:, n_iota].unsqueeze(1).broadcast_to((P, NT * TOPK, NE)), ALU.is_equal))
                nc.vector.tensor_reduce(M[:], oh[:].rearrange("p t k e -> p t e k"), AX.X, ALU.add).then_inc(s_oh, 1)
                dve.wait_ge(s_e, 1)
                step(nc.vector.tensor_reduce(den[:], gate[:], AX.X, ALU.add))
                step(nc.vector.reciprocal(den[:], den[:]))
                step(nc.vector.tensor_tensor(gate[:], gate[:], den[:].unsqueeze(2).broadcast_to((P, NT, TOPK)), ALU.mult), False)
                dve.wait_ge(s_pos, 1)
                step(nc.vector.tensor_copy(cnt[:], psC[:, 0:NE]))
                step(nc.vector.tensor_scalar(sizef[:], cnt[:], float(SIZES[0]), None, ALU.is_gt), False)
                step(nc.vector.tensor_scalar(nb[:], cnt[:], float(CAP), None, ALU.is_gt))
                step(nc.vector.scalar_tensor_tensor(sizef[:], cnt[:], float(SIZES[1]), sizef[:], ALU.is_gt, ALU.add))
                step(nc.vector.tensor_copy(a["block_size"][:], sizef[:]), False)
                for q in range(2, (SEQ - 1) // CAP + 1):
                    step(nc.vector.scalar_tensor_tensor(nb[:], cnt[:], float(q * CAP), nb[:], ALU.is_gt, ALU.add))
                step(nc.vector.tensor_tensor_scan(first[:], ones[:, 0:NE], nb[:], 0.0, ALU.mult, ALU.add))
                step(nc.vector.tensor_tensor(cmp[:], first[:].unsqueeze(1).broadcast_to((P, NB_OVER, NE)),
                                             cst[:, n_blk].unsqueeze(2).broadcast_to((P, NB_OVER, NE)), ALU.is_le), False)
                step(nc.vector.tensor_copy(bexp[:, NB_OVER:], first[:, NE - 1:NE]))
                step(nc.vector.tensor_reduce(bexp[:, 0:NB_OVER], cmp[:], AX.X, ALU.add), False)
                step(nc.vector.tensor_tensor(first[:], first[:], nb[:], ALU.subtract))
                step(nc.vector.tensor_scalar(bexp[:, 0:NB_OVER], bexp[:, 0:NB_OVER], float(NE - 1), None, ALU.min))
                step(nc.vector.tensor_copy(ids[:], bexp[:]), False)
                step(nc.vector.tensor_scalar(B[:], first[:], float(CAP), float(CAP * (NE - 1)), ALU.mult, ALU.add))
                step(nc.vector.tensor_tensor(B[:], B[:], cst[:, n_cap], ALU.subtract))
                wide = lambda x: x.unsqueeze(1).broadcast_to((P, NT, NE))
                step(nc.vector.tensor_scalar(T1[:], ps, float(CAP), None, ALU.is_ge))
                step(nc.vector.tensor_tensor(T1[:], T1[:], wide(B[:]), ALU.mult), False)
                step(nc.vector.tensor_tensor(T2[:], ps, wide(cst[:, n_cap]), ALU.add))
                step(nc.vector.tensor_tensor(SL[:], T1[:], T2[:], ALU.add))
                step(nc.vector.tensor_tensor(oh[:], oh[:], SL[:].unsqueeze(2).broadcast_to((P, NT, TOPK, NE)), ALU.mult))
                step(nc.vector.tensor_reduce(slotf[:], oh[:], AX.X, ALU.add))
                nc.vector.tensor_copy(slot_i[:], slotf[:]).then_inc(s_slot, 1)
                dve.wait_ge(s_tp, 1)
                nc.vector.tensor_copy(idx[:, 0, 0:NE + NB_OVER], psI[:, 0, 0:NE + NB_OVER])
                nc.vector.tensor_copy(idx[0:CAP - P, 1, 0:NE + NB_OVER], psI[0:CAP - P, 1, 0:NE + NB_OVER])

            @block.scalar
            def _(act):
                act.wait_ge(s_d, before_exp[0])
                nc.scalar.activation(gate[:], gate[:], ACT.Exp).then_inc(s_e, 1)

            @block.gpsimd
            def _(pool):
                pool.wait_ge(s_slot, 1)
                pool.wait_ge(s_z, 32)
                for t in range(NT):
                    for c in range(TOPK):
                        nc.gpsimd.indirect_dma_start(a["slot_token_d"], bass.IndirectOffsetOnAxis(slot_i[:, t, c:c + 1], 0),
                                                     tok[:, t:t + 1], None).then_inc(s_m, 16)

            @block.tensor
            def _(pe):
                pe.wait_ge(s_oh, 1)
                pe.wait_ge(s_c, 48)
                pe.wait_ge(s_zero, 2)
                for t in range(NT):
                    for q in range(t + 1):
                        nc.tensor.matmul(ps[:, t], (tri if q == t else ones)[:], M[:, q], start=(q == 0), stop=(q == t))
                for q in range(NT):
                    last = nc.tensor.matmul(psC[:, 0:NE], ones[:], M[:, q], start=(q == 0), stop=(q == NT - 1))
                last.then_inc(s_pos, 1)
                pe.wait_ge(s_rows, 16)
                n = NE + NB_OVER
                nc.tensor.transpose(psI[:, 0, 0:n], rows[:, 0:P], a["ident"][0:n, 0:n])
                nc.tensor.transpose(psI[0:CAP - P, 1, 0:n], rows[:, P:CAP], a["ident"][0:n, 0:n]).then_inc(s_tp, 1)


CW = 512
CHUNKS = 6


class Experts:

    def __init__(self, nc, a, k):
        self.nc, self.a = nc, a
        self.w = k.sb("w_expert", [P, CHUNKS, KT, CW])
        self.x0, self.x1 = k.sb("x0", [P, D]), k.sb("x1", [CAP - P, D])
        self.xT, self.actT = k.sb("xT", [P, KT, CAP]), k.sb("actT", [P, KT, CAP])
        self.g, self.sg, self.u = (k.sb(n, [P, 2, 4, CAP]) for n in ("g_clamped", "g_sigmoid", "u_clamped"))
        self.yT = k.sb("yT", [P, KT, CAP])
        self.y0, self.y1 = k.sb("y0", [P, D]), k.sb("y1", [CAP - P, D])
        self.bias = k.sb("bias", [P, 3 * KT, NE])
        self.cur = k.sb("cur_idx", [P, 2], U32)
        self.ps = k.ps("psE", [P, 8, 512])

    def open(self, k):
        names = dict(mm="chunk_multiplied", gu="gate_up_evacuated", dn="down_evacuated", sig="sigmoid_done", mul="up_times_gate",
                     act="actT_ready", xtp="x_transposed", xT="xT_ready", ytp="y_transposed", yev="y_evacuated", cur="idx_copied",
                     go="gather_released")
        self.s = {n: k.sem("ex_" + v) for n, v in names.items()}
        self.s_w = [k.sem(f"w_chunk{j}_loaded") for j in range(CHUNKS)]
        self.s_x = k.sem("x_gathered")
        self.s_y = k.sem("y_stored")

    def load_chunk(self, sp, expert, j):
        a = self.a
        if j < 4:
            src = a["w_gate_up"][bass.ds(expert, 1), :, (j % 2) * DFF + (j // 2) * CW:(j % 2) * DFF + (j // 2 + 1) * CW]
        else:
            src = a["w_down"][bass.ds(expert, 1), :, (j - 4) * CW:(j - 3) * CW]
        sp.dma_start(self.w[:, j], src.rearrange("o (k p) n -> p (o k) n", p=P)).then_inc(self.s_w[j], 16)

    def gather(self, pool, n, first=False):
        nc = self.nc
        if not first:
            pool.wait_ge(self.s["xtp"], n * 2)
        nc.gpsimd.tensor_copy(self.cur[:], self.a["idx"][:, :, bass.ds(n, 1)].rearrange("p a b -> p (a b)")).then_inc(self.s["cur"], 1)
        pool.wait_ge(self.s["cur"], n + 1)
        pool.sem_inc(self.s["go"], 1)
        nc.gpsimd.indirect_dma_start(self.x0[:], None, self.a["h2_d"], bass.IndirectOffsetOnAxis(self.cur[:, 0:1], 0)).then_inc(self.s_x, 16)
        nc.gpsimd.indirect_dma_start(self.x1[:], None, self.a["h2_d"], bass.IndirectOffsetOnAxis(self.cur[0:CAP - P, 1:2], 0)).then_inc(self.s_x, 16)

    def ps_x(self):
        return self.ps[:, 4:6, 0:2 * CAP].rearrange("p a (b t) -> p a b t", t=CAP)

    def x_transpose(self, pe, n, r, y_done):
        nc = self.nc
        if r == 0:
            pe.wait_ge(self.s_x, n * 32 + 32)
            if y_done is not None:
                pe.wait_ge(self.s["yev"], 2 * y_done)
        else:
            pe.wait_ge(self.s["xT"], 2 * n + 1)
        for q in range(4):
            cols = slice((4 * r + q) * P, (4 * r + q + 1) * P)
            out = self.ps_x()[:, q // 2, q % 2]
            nc.tensor.transpose(out[:, 0:P], self.x0[:, cols], self.a["ident"][:])
            last = nc.tensor.transpose(out[:, P:CAP], self.x1[:, cols], self.a["ident"][0:CAP - P, 0:CAP - P])
        last.then_inc(self.s["xtp"], 1)

    def x_evacuate(self, act, n, r):
        act.wait_ge(self.s["xtp"], 2 * n + r + 1)
        self.nc.scalar.copy(self.xT[:, 4 * r:4 * r + 4, :].rearrange("p (a b) t -> p a b t", b=2), self.ps_x()).then_inc(self.s["xT"], 1)

    def multiply(self, pe, n, j, first=False, slots=CAP):
        nc = self.nc
        moving = self.xT if j < 4 else self.actT
        pe.wait_ge(self.s_w[j], n * 16 + 16)
        if j == 0:
            pe.wait_ge(self.s["xT"], 2 * n + 2)
        if j < 2:
            if not first:
                pe.wait_ge(self.s["dn"], 2 * n + j - 1)
        else:
            pe.wait_ge(self.s["gu"], 4 * n + j - 1)

        def products(kts, qs=range(4)):
            for q in qs:
                out = self.ps[:, (j % 2) * 2 + q // 2, (q % 2) * CAP:(q % 2) * CAP + slots]
                for kt in kts:
                    last = nc.tensor.matmul(out, self.w[:, j, kt, q * P:(q + 1) * P], moving[:, kt, 0:slots],
                                            start=(kt == 0), stop=(kt == KT - 1))
            return last

        if j == 4:
            pe.wait_ge(self.s["act"], 2 * n + 1)
            products(range(KT // 2), (0, 2))
            pe.wait_ge(self.s["act"], 2 * n + 2)
            products(range(KT // 2, KT), (0, 2))
            products(range(KT), (1, 3)).then_inc(self.s["mm"], 1)
        else:
            products(range(KT)).then_inc(self.s["mm"], 1)

    def gate_evacuate(self, dve, n, half, expert):
        j = 2 * half
        dve.wait_ge(self.s["mm"], n * CHUNKS + j + 1)
        for q in range(4):
            last = self.nc.vector.tensor_scalar(self.g[:, half, q], self.ps[:, (j % 2) * 2 + q // 2, (q % 2) * CAP:(q % 2 + 1) * CAP],
                                                self.bias[:, 4 * half + q, bass.ds(expert, 1)], SWIGLU_LIMIT, ALU.add, ALU.min)
        last.then_inc(self.s["gu"], 1)

    def up_evacuate(self, dve, n, half, expert):
        nc, j = self.nc, 2 * half + 1
        dve.wait_ge(self.s["mm"], n * CHUNKS + j + 1)
        for q in range(4):
            last = nc.vector.tensor_scalar(self.u[:, half, q], self.ps[:, (j % 2) * 2 + q // 2, (q % 2) * CAP:(q % 2 + 1) * CAP],
                                           self.bias[:, KT + 4 * half + q, bass.ds(expert, 1)], SWIGLU_LIMIT + 1.0, ALU.add, ALU.min)
        last.then_inc(self.s["gu"], 1)
        dve.wait_ge(self.s["gu"], 4 * n + 2 * half + 2)
        nc.vector.scalar_tensor_tensor(self.u[:, half], self.u[:, half], 1.0 - SWIGLU_LIMIT, self.g[:, half], ALU.max, ALU.mult)\
            .then_inc(self.s["mul"], 1)
        dve.wait_ge(self.s["mul"], 2 * n + half + 1)
        dve.wait_ge(self.s["sig"], 2 * n + half + 1)
        nc.vector.tensor_tensor(self.actT[:, 4 * half:4 * half + 4], self.u[:, half], self.sg[:, half], ALU.mult).then_inc(self.s["act"], 1)

    def sigmoid(self, act, n, half):
        act.wait_ge(self.s["gu"], 4 * n + 2 * half + 1)
        self.nc.scalar.activation(self.sg[:, half], self.g[:, half], ACT.Sigmoid, scale=SWIGLU_ALPHA).then_inc(self.s["sig"], 1)

    def down_evacuate(self, act, n, half, expert):
        j = 4 + half
        act.wait_ge(self.s["mm"], n * CHUNKS + j + 1)
        for q in range(4):
            last = self.nc.scalar.activation(self.yT[:, 4 * half + q], self.ps[:, (j % 2) * 2 + q // 2, (q % 2) * CAP:(q % 2 + 1) * CAP],
                                             ACT.Identity, bias=self.bias[:, 2 * KT + 4 * half + q, bass.ds(expert, 1)])
        last.then_inc(self.s["dn"], 1)

    def y_transpose(self, pe, n, half, first=False):
        nc = self.nc
        pe.wait_ge(self.s["dn"], 2 * n + half + 1)
        if half == 0:
            if not first:
                pe.wait_ge(self.s["yev"], 2 * n - 1)
        bank = 6 - 2 * half
        for q in range(4):
            nc.tensor.transpose(self.ps[:, bank, q * P:(q + 1) * P], self.yT[:, 4 * half + q, 0:P], self.a["ident"][:])
            last = nc.tensor.transpose(self.ps[0:CAP - P, bank + 1, q * P:(q + 1) * P], self.yT[:, 4 * half + q, P:CAP], self.a["ident"][:])
        last.then_inc(self.s["ytp"], 1)

    def y_evacuate(self, act, n, half, first=False):
        nc = self.nc
        act.wait_ge(self.s["ytp"], 2 * n + half + 1)
        if not first and half == 0:
            act.wait_ge(self.s_y, n * 32)
        bank, cols = 6 - 2 * half, slice(half * 512, half * 512 + 512)
        nc.scalar.copy(self.y0[:, cols], self.ps[:, bank, :])
        nc.scalar.copy(self.y1[:, cols], self.ps[0:CAP - P, bank + 1, :]).then_inc(self.s["yev"], 1)

    def y_store(self, act, n):
        act.wait_ge(self.s["yev"], 2 * n + 2)
        act.dma_start(self.a["y_d"][bass.ds(n * CAP, P), :], self.y0[:]).then_inc(self.s_y, 16)
        act.dma_start(self.a["y_d"][bass.ds(n * CAP + P, CAP - P), :], self.y1[:]).then_inc(self.s_y, 16)


def expert_biases(nc, a, ex):
    with ExitStack() as stack:
        k = Kit(nc, stack)
        s_l, s_t, s_e = k.sem("biases_loaded"), k.sem("biases_transposed"), k.sem("biases_ready")
        rows = k.sb("bias_rows", [NE, 3 * D])
        with nc.Block() as block:
            @block.sync
            def _(sp):
                sp.dma_start(rows[:, 0:2 * DFF], a["b_gate_up"]).then_inc(s_l, 16)
                sp.dma_start(rows[:, 2 * DFF:2 * DFF + D], a["b_down"]).then_inc(s_l, 16)

            @block.tensor
            def _(pe):
                pe.wait_ge(s_l, 32)
                for f in range(3 * KT):
                    last = nc.tensor.transpose(ex.ps[:, f // 16, (f % 16) * NE:(f % 16 + 1) * NE], rows[:, f * P:(f + 1) * P], a["ident"][0:NE, 0:NE])
                last.then_inc(s_t, 1)

            @block.vector
            def _(dve):
                dve.wait_ge(s_t, 1)
                bank = lambda f: ex.ps[:, f // 16, (f % 16) * NE:(f % 16) * NE + KT * NE].rearrange("p (f e) -> p f e", e=NE)
                nc.vector.tensor_copy(ex.bias[:, 0:KT], bank(0))
                nc.vector.tensor_scalar(ex.bias[:, KT:2 * KT], bank(KT), 1.0, None, ALU.add)
                nc.vector.tensor_copy(ex.bias[:, 2 * KT:], bank(2 * KT)).then_inc(s_e, 1)


def experts(nc, a, ex, h2):
    def over(engine, body):
        count = engine.value_load(a["block_expert"][0:1, NB_OVER:NB_OVER + 1], min_val=0, max_val=NB_OVER)
        with engine.If(count > 0):
            with engine.Fori(0, NB_OVER) as b:
                with engine.If(b < count):
                    body(b + NE, engine.value_load(a["block_expert"][0:1, bass.ds(b, 1)], min_val=0, max_val=NE - 1))

    with nc.Block() as block:
        @block.sync
        def _(sp):
            with sp.Fori(1, NE) as e:
                for j in range(CHUNKS):
                    sp.wait_ge(ex.s["mm"], (e - 1) * CHUNKS + j + 1)
                    ex.load_chunk(sp, e, j)

            def body(n, expert):
                for j in range(CHUNKS):
                    sp.wait_ge(ex.s["mm"], (n - 1) * CHUNKS + j + 1)
                    ex.load_chunk(sp, expert, j)
            over(sp, body)
            sp.dma_start(h2[:], a["h2_d"].rearrange("(t p) d -> p t d", p=P)).then_inc(a["h2_loaded"], 16)
            sp.wait_ge(a["h2_loaded"], 16)

        @block.gpsimd
        def _(pool):
            ex.gather(pool, 0, first=True)
            with pool.Fori(1, NE) as e:
                ex.gather(pool, e)
            over(pool, lambda n, expert: ex.gather(pool, n))

        @block.scalar
        def _(act):
            def body(n, expert, ahead, first=False, pending=True):
                if pending:
                    ex.y_evacuate(act, n - 1, 1)
                    ex.y_store(act, n - 1)
                for half in range(2):
                    ex.sigmoid(act, n, half)
                if ahead:
                    ex.x_evacuate(act, n + 1, 0)
                ex.down_evacuate(act, n, 0, expert)
                if ahead:
                    ex.x_evacuate(act, n + 1, 1)
                ex.down_evacuate(act, n, 1, expert)
                ex.y_evacuate(act, n, 0, first)
                if not ahead:
                    ex.y_evacuate(act, n, 1)
                    ex.y_store(act, n)

            for r in range(2):
                ex.x_evacuate(act, 0, r)
            body(0, 0, True, first=True, pending=False)
            with act.Fori(1, NE - 1) as e:
                body(e, e, True)
            body(NE - 1, NE - 1, False)

            def over_body(n, expert):
                for r in range(2):
                    ex.x_evacuate(act, n, r)
                body(n, expert, False, pending=False)
            over(act, over_body)
            blocks = act.value_load(a["block_expert"][0:1, NB_OVER:NB_OVER + 1], min_val=0, max_val=NB_OVER) + NE
            act.wait_ge(ex.s_y, blocks * 32)
            act.sem_inc(ex.s["go"], 1)

        @block.vector
        def _(dve):
            def body(n, expert):
                for half in range(2):
                    ex.gate_evacuate(dve, n, half, expert)
                    ex.up_evacuate(dve, n, half, expert)

            with dve.Fori(0, NE) as e:
                body(e, e)
            over(dve, body)

        @block.tensor
        def _(pe):
            def body(n, ahead, first=False, pending=True, slots=CAP):
                ex.multiply(pe, n, 0, first, slots)
                if pending:
                    ex.y_transpose(pe, n - 1, 1)
                for j in range(1, 4):
                    ex.multiply(pe, n, j, first, slots)
                if ahead:
                    ex.x_transpose(pe, n + 1, 0, None if first else n)
                ex.multiply(pe, n, 4, slots=slots)
                if ahead:
                    ex.x_transpose(pe, n + 1, 1, None)
                ex.multiply(pe, n, 5, slots=slots)
                ex.y_transpose(pe, n, 0, first)
                if not ahead:
                    ex.y_transpose(pe, n, 1)

            def sized(n, ahead):
                size = pe.value_load(a["block_size"][0:1, bass.ds(n, 1)], min_val=0, max_val=len(SIZES) - 1)
                for i, slots in enumerate(SIZES):
                    with pe.If(size == i):
                        body(n, ahead, slots=slots)

            for r in range(2):
                ex.x_transpose(pe, 0, r, None)
            body(0, True, first=True, pending=False)
            with pe.Fori(1, NE - 1) as e:
                sized(e, True)
            sized(NE - 1, False)

            def over_body(n, expert):
                for r in range(2):
                    ex.x_transpose(pe, n, r, n)
                body(n, False, pending=False)
            over(pe, over_body)


def combine(nc, a, h2):
    with ExitStack() as stack:
        k = Kit(nc, stack)
        BUF = 4
        y = k.sb("y", [P, BUF, TOPK, D])
        diag = k.sb("gate_diag", [P, NT, TOPK, P])
        lng, lnb = k.sb("ffng", [P, D]), k.sb("ffnb", [P, D])
        stat, mv, rs, nm = k.sb("stat3", [P, 2, 2, 6]), k.sb("mv3", [P, 2, 2]), k.sb("rstd3", [P, 2]), k.sb("shift3", [P, 2])
        ps = k.ps("ps_sum", [P, 2, D])
        s_p, s_d, s_ve, s_sq, s_rs, s_n, s_out = (k.sem(n) for n in (
            "ffn_params_loaded", "dve_steps", "var_ready", "sqrt_done", "rstd_ready", "normed", "out_ready"))
        s_diag, s_mm, s_sum = k.sem("diagonals_ready"), k.sem("rows_summed"), k.sem("residual_added")
        s_y = [k.sem(f"y{p}_gathered") for p in range(BUF)]
        s_st = k.sem("out_stored")

        with nc.Block() as block:
            @block.gpsimd
            def _(pool):
                for t in range(NT):
                    if t >= BUF:
                        pool.wait_ge(s_mm, t - BUF + 1)
                    for c in range(TOPK):
                        nc.gpsimd.indirect_dma_start(y[:, t % BUF, c], None, a["y_d"], bass.IndirectOffsetOnAxis(a["slot_i"][:, t, c:c + 1], 0))\
                            .then_inc(s_y[t % BUF], 16)

            @block.sync
            def _(sp):
                for dst, src in ((lng, "ln_ffn_g"), (lnb, "ln_ffn_b")):
                    sp.dma_start(dst[:], a[src].partition_broadcast(P)).then_inc(s_p, 16)
                for t in range(NT):
                    sp.wait_ge(s_out, t + 1)
                    sp.dma_start(a["out"][0, t * P:(t + 1) * P, :], h2[:, t]).then_inc(s_st, 16)
                sp.wait_ge(s_st, 16 * NT)

            @block.tensor
            def _(pe):
                for t in range(NT):
                    pe.wait_ge(s_diag, t + 1)
                    pe.wait_ge(s_y[t % BUF], 16 * TOPK * (t // BUF + 1))
                    if t >= 2:
                        pe.wait_ge(s_sum, t - 1)
                    for h in range(2):
                        for c in range(TOPK):
                            last = nc.tensor.matmul(ps[:, t % 2, h * 512:(h + 1) * 512], diag[:, t, c], y[:, t % BUF, c, h * 512:(h + 1) * 512],
                                                    start=(c == 0), stop=(c == TOPK - 1))
                    last.then_inc(s_mm, 1)

            @block.vector
            def _(dve):
                steps = [0]

                def step(ins):
                    steps[0] += 1
                    ins.then_inc(s_d, 1)
                    dve.wait_ge(s_d, steps[0])

                def scale_and_shift(t):
                    dve.wait_ge(s_n, t + 1)
                    step(nc.vector.tensor_tensor(h2[:, t], h2[:, t], lng[:], ALU.mult))
                    nc.vector.tensor_tensor(h2[:, t], h2[:, t], lnb[:], ALU.add).then_inc(s_out, 1)

                for t in range(NT):
                    p = t % 2
                    dve.wait_ge(s_mm, t + 1)
                    nc.vector.scalar_tensor_tensor(h2[:, t], h2[:, t], ALPHA, ps[:, p], ALU.mult, ALU.add).then_inc(s_sum, 1)
                    dve.wait_ge(s_sum, t + 1)
                    nc.vector.bn_stats(stat[:, p, 0], h2[:, t, 0:512])
                    step(nc.vector.bn_stats(stat[:, p, 1], h2[:, t, 512:1024]))
                    step(nc.vector.bn_aggr(mv[:, p], stat[:, p]))
                    nc.vector.tensor_scalar(rs[:, p:p + 1], mv[:, p, 1:2], LN_EPS, None, ALU.add).then_inc(s_ve, 1)
                    if t == 0:
                        dve.wait_ge(s_p, 32)
                    else:
                        scale_and_shift(t - 1)
                    dve.wait_ge(s_sq, t + 1)
                    step(nc.vector.reciprocal(rs[:, p:p + 1], rs[:, p:p + 1]))
                    nc.vector.scalar_tensor_tensor(nm[:, p:p + 1], mv[:, p, 0:1], -1.0, rs[:, p:p + 1], ALU.mult, ALU.mult).then_inc(s_rs, 1)
                scale_and_shift(NT - 1)

            @block.scalar
            def _(act):
                for t in range(NT):
                    for c in range(TOPK):
                        last = nc.scalar.activation(diag[:, t, c], a["ident"][:], ACT.Copy, scale=a["gate"][:, t, c:c + 1])
                    last.then_inc(s_diag, 1)
                for t in range(NT):
                    p = t % 2
                    act.wait_ge(s_ve, t + 1)
                    nc.scalar.activation(rs[:, p:p + 1], rs[:, p:p + 1], ACT.Sqrt).then_inc(s_sq, 1)
                    act.wait_ge(s_rs, t + 1)
                    nc.scalar.activation(h2[:, t], h2[:, t], ACT.Identity, bias=nm[:, p:p + 1], scale=rs[:, p:p + 1]).then_inc(s_n, 1)


def build(nc, a):
    with ExitStack() as stack:
        k = Kit(nc, stack)
        a["ident"] = k.sb("ident", [P, P])
        a["consts_loaded"] = k.sem("consts_loaded")
        for name, shape in SCRATCH.items():
            a[name] = nc.dram_tensor(name, shape, F32, kind="Internal").ap()
        with nc.Block() as block:
            @block.sync
            def _(sp):
                sp.dma_start(a["ident"][:], a["ident_c"]).then_inc(a["consts_loaded"], 16)
        for name, shape, dt in KEPT:
            a[name] = k.sb(name, shape, dt)
        mixers(nc, a)
        h2 = k.sb("h2_all", [P, NT, D])
        a["h2_loaded"] = k.sem("h2_loaded")
        with ExitStack() as expert_stack:
            ke = Kit(nc, expert_stack)
            ex = Experts(nc, a, ke)
            ex.open(ke)
            expert_biases(nc, a, ex)
            route(nc, a, ex)
            experts(nc, a, ex, h2)
        combine(nc, a, h2)


KEPT = (
    ("logits", [P, NT, NE], F32),
    ("gate", [P, NT, TOPK], F32),
    ("slot_i", [P, NT, TOPK], U32),
    ("idx", [P, 2, NE + NB_OVER], U32),
    ("block_size", [P, NE], I32),
    ("block_expert", [P, NB_OVER + 1], I32),
)
SCRATCH = {
    "h_d": (SEQ, D), "projT_d": (3 * CC, SEQ), "projM_d": (SEQ, NTM * CC),
    "h2_d": (SEQ, D), "slot_token_d": (NSLOT, 1), "y_d": (NSLOT, D),
}


def level_masks():
    j = np.arange(P)[:, None]
    out = np.zeros((P, 6, CH // 2), np.int32)
    for level in range(6):
        s = 1 << level
        n = np.arange(CH // 2)
        i = (n // s) * 2 * s + s + n % s
        out[:, level] = (j // (2 * s) == i // (2 * s)) & (j // s % 2 == 0)
    return out


def layout(inputs):
    i = {n: np.ascontiguousarray(v) for n, v in inputs.items()}
    w = i["w_in"][0]
    o = np.cumsum([0, 256, 256, 512, RANK, 512, 256, 256, 256, 256, 256, 256, 256])
    part = lambda n: w[:, o[n]:o[n + 1]]
    cols = np.concatenate([part(n) for n in (0, 1, 5, 6, 9, 10, 11, 2, 4, 7, 8)], axis=1)
    out = {
        "x": i["x"][0], "ln_in_g": i["ln_in_g"], "ln_in_b": i["ln_in_b"],
        "w_cols": cols.reshape(KT, P, NFM + NTM, CC).transpose(2, 1, 0, 3),
        "w_lr": part(3).reshape(KT, P, RANK).transpose(1, 0, 2),
        "ident_c": np.eye(P, dtype=np.float32),
        "w_expand": np.concatenate([i["w_gla_gate_expand"][0]] * 2),
        "gate_cols": np.concatenate([i["b_gla_gate"][0].reshape(2, P), i["hgrn_lb_raw"][0].reshape(2, P)]).T,
        "restart_c": np.broadcast_to((np.arange(SEQ) % CH != 0).astype(np.float32), (P, SEQ)),
        "w_gate_up": i["w_gate_up"][0], "w_down": i["w_down"][0], "b_gate_up": i["b_gate_up"][0], "b_down": i["b_down"][0],
        "ln_ffn_g": i["ln_ffn_g"][0], "ln_ffn_b": i["ln_ffn_b"][0],
        "norm_row": np.concatenate([np.tile(i["gla_norm_g"][0], GLA_H), np.tile(i["hgrn_norm_g"][0], HG_H)]),
        "conv_cols": i["conv_w"][0].reshape(CONV_W, 2, P).transpose(2, 1, 0),
        "w_out": i["w_out"][0], "ln_mix_g": i["ln_mix_g"][0], "ln_mix_b": i["ln_mix_b"][0],
        "w_router": i["w_router"][0], "b_router": i["b_router"][0],
        "route_c": np.broadcast_to(np.concatenate([np.arange(NE), np.arange(NE) * CAP, np.arange(NB_OVER)]).astype(np.float32),
                                   (P, 2 * NE + NB_OVER)),
        "tri_c": (np.arange(P)[:, None] < np.arange(P)[None, :]).astype(np.float32),
        "token_c": np.arange(SEQ, dtype=np.float32).reshape(NT, P).T,
        "level_masks": level_masks(), "diag_mask": np.eye(P, dtype=np.int32),
    }
    return {n: np.ascontiguousarray(v) for n, v in out.items()}


def kernel(**inputs):
    import concourse.bacc as bacc
    from concourse.bass_utils import run_bass_kernel_spmd

    nc = bacc.Bacc("TRN2", target_bir_lowering=False, num_devices=1)
    arrays = layout(inputs)
    a = {n: nc.dram_tensor(n, v.shape, mybir.dt.from_np(v.dtype), kind="ExternalInput").ap() for n, v in arrays.items()}
    a["out"] = nc.dram_tensor("out", (1, SEQ, D), F32, kind="ExternalOutput").ap()
    build(nc, a)
    return run_bass_kernel_spmd(nc, [arrays], core_ids=[0]).results[0]["out"]
```

```python
from contextlib import ExitStack

import concourse.bass as bass
from concourse import mybir
import numpy as np

F32 = mybir.dt.float32
F32R = mybir.dt.float32r
I32 = mybir.dt.int32
U32 = mybir.dt.uint32
ACT = mybir.ActivationFunctionType
ALU = mybir.AluOpType
AX = mybir.AxisListType

P = 128
SEQ = 1024
D = 1024
KT = D // P
NT = SEQ // P
GLA_H, GLA_K, GLA_V, RANK = 4, D // 16, D // 8, 16
HG_H, HG_F, HG_I = 4, D // 16, D // 16
CONV_C, CONV_W = D // 4, 3
NE, TOPK, DFF = 32, 4, D
LN_EPS, RMS_EPS = 1e-5, 1e-6
ALPHA = 2.0 ** 0.25
SWIGLU_LIMIT, SWIGLU_ALPHA = 7.0, 1.702
CC = 256
NFM = 7
LOCAL = 4
NTM = 6


class Kit:

    def __init__(self, nc, stack):
        self.nc, self.stack = nc, stack

    def sb(self, name, shape, dt=F32):
        return self.stack.enter_context(self.nc.sbuf_tensor(name, shape, dt))

    def ps(self, name, shape, dt=F32):
        return self.stack.enter_context(self.nc.psum_tensor(name, shape, dt))

    def sem(self, name):
        return self.stack.enter_context(self.nc.semaphore(name))


def project(nc, a, q_all, k_all, G, EG):
    with ExitStack() as stack:
        k = Kit(nc, stack)
        x_all = k.sb("x_all", [P, NT, D])
        u = k.sb("u", [P, 2 * SEQ])[:]
        lng, lnb = G[:, 1], G[:, 0]
        stat = k.sb("stat", [P, NT, 2, 6])
        mv = k.sb("mv", [P, NT, 2])
        rstd = k.sb("rstd", [P, NT])
        shift = k.sb("shift", [P, NT])
        hT_hi = k.sb("hT_hi", [P, KT, SEQ], F32R)
        hT_lo = k.sb("hT_lo", [P, KT, SEQ], F32R)
        w_raw = k.sb("w_raw", [P, 2, KT, CC])
        w_hi = k.sb("w_hi", [P, 2, KT, CC], F32R)
        w_lo = k.sb("w_lo", [P, 2, KT, CC], F32R)
        stage = x_all
        wlr = x_all[:, 4, 0:KT * RANK].rearrange("p (k r) -> p k r", r=RANK)
        wlr_split = k.sb("wlr_split", [P, KT, 2 * RANK], F32R)
        z, t = (x_all[:, r:r + 2, :].rearrange("p a b -> p (a b)") for r in (4, 6))
        restart = G[:, 1]
        lrT = G[0:2 * RANK, 0]
        expand = k.sb("expand", [2 * RANK, GLA_H * GLA_K])
        col = k.sb("col", [P, 4])
        lb = k.sb("lb", [P, 6])
        tmp = k.sb("tmp", [P, 4])
        s_par, s_restart = k.sem("gate_params_loaded"), k.sem("restart_loaded")
        s_z, s_zev, s_d, s_a = k.sem("logits_ready"), k.sem("logits_evacuated"), k.sem("dve_steps"), k.sem("act_steps")
        s_wlrs, s_lrev = k.sem("wlr_split_ready"), k.sem("lr_evacuated")
        flat = lambda x: x.rearrange("p a b -> p (a b)")
        row = lambda x, f: x[:, f * SEQ:(f + 1) * SEQ]
        ps = k.ps("psA", [P, 8, 512])
        s_ln, s_wlr = k.sem("ln_params_loaded"), k.sem("wlr_loaded")
        s_x = [k.sem(f"x{t}_loaded") for t in range(NT)]
        s_w = [k.sem(f"w_raw{p}_loaded") for p in range(2)]
        s_hout = k.sem("h_stored")
        s_out = a["projections_stored"]
        s_st, s_mv, s_ve, s_sq, s_rs, s_sh = (k.sem(n) for n in (
            "stats_done", "mean_var_done", "var_eps_done", "sqrt_done", "rstd_done", "shift_done"))
        s_n, s_xg, s_h = k.sem("x_normalised"), k.sem("x_times_g"), k.sem("h_ready")
        s_tp, s_hi, s_lo = k.sem("h_transposed"), k.sem("hT_hi_ready"), k.sem("hT_lo_ready")
        s_whi, s_wlo = k.sem("w_hi_ready"), k.sem("w_lo_ready")
        s_mm, s_ev = k.sem("chunk_multiplied"), k.sem("chunk_evacuated")
        s_lr = k.sem("lr_multiplied")
        n_chunks = NFM + NTM
        half = NT // 2
        def ps_tp(p):
            return ps[:, 2 * p:2 * p + 2, :].rearrange("p a (b c) -> p (a b) c", c=P)

        def w_high(j):
            act, p = nc.scalar, j % 2
            act.wait_ge(s_w[p], (j // 2) * 16 + 16)
            if j >= 2:
                act.wait_ge(s_mm, j - 1)
            nc.scalar.copy(w_hi[:, p], w_raw[:, p]).then_inc(s_whi, 1)

        def w_low(j):
            dve, p = nc.vector, j % 2
            dve.wait_ge(s_whi, j + 1)
            nc.vector.tensor_tensor(w_lo[:, p], w_raw[:, p], w_hi[:, p].bitcast(F32), ALU.subtract).then_inc(s_wlo, 1)

        def evacuate_local(j):
            act, p = nc.scalar, j % 2
            act.wait_ge(s_mm, j + 1)
            dst = (q_all, k_all)[j % 2][:, j // 2 * 2:j // 2 * 2 + 2, :]
            nc.scalar.activation(flat(dst), flat(ps[:, 4 * p:4 * p + 4, :]), ACT.Silu if j == 2 else ACT.Copy,
                                 scale=GLA_K ** -0.5 if j == 0 else 1.0).then_inc(s_ev, 1)

        def evacuate(j):
            act, p = nc.scalar, j % 2
            act.wait_ge(s_mm, j + 1)
            if j >= LOCAL + 2:
                act.wait_ge(s_out[p], (j - LOCAL) // 2 * 16)
            dst = stage[:, 2 * p:2 * p + 2, :]
            nc.scalar.copy(flat(dst), flat(ps[:, 4 * p:4 * p + 4, :])).then_inc(s_ev, 1)
            act.wait_ge(s_ev, j + 1)
            if j < NFM:
                act.dma_start(a["projT_d"][(j - LOCAL) * CC:(j - LOCAL + 1) * CC, :].rearrange("(f p) t -> p f t", p=P), dst).then_inc(s_out[p], 16)
            else:
                act.dma_start(a["projM_d"][:, (j - NFM) * CC:(j - NFM + 1) * CC].rearrange("(t p) c -> p t c", p=P),
                              dst.rearrange("p a (b c) -> p (a b) c", c=CC)).then_inc(s_out[p], 16)

        done = {"dve": 0, "act": 0}
        s_a2 = k.sem("act_functions")
        with nc.Block() as block:
            @block.sync
            def _(sp):
                for t in range(NT):
                    sp.dma_start(x_all[:, t], a["x"][t * P:(t + 1) * P, :]).then_inc(s_x[t], 16)
                    if t < 2:
                        sp.dma_start((lng, lnb)[t], a[("ln_in_g", "ln_in_b")[t]].partition_broadcast(P)).then_inc(s_ln, 16)
                for j in range(2):
                    sp.dma_start(w_raw[:, j], a["w_cols"][j]).then_inc(s_w[j % 2], 16)
                sp.dma_start(expand[:], a["w_expand"]).then_inc(s_par, 16)
                sp.dma_start(col[:], a["gate_cols"]).then_inc(s_par, 16)
                with sp.Fori(0, half) as i:
                    sp.wait_ge(s_h, i * 2 + 2)
                    sp.dma_start(a["h_d"][bass.ds(i * 2 * P, 2 * P), :].rearrange("(t p) d -> p t d", p=P),
                                 x_all[:, bass.ds(i * 2, 2), :]).then_inc(s_hout, 16)
                sp.dma_start(restart, a["restart_c"]).then_inc(s_restart, 16)
                sp.wait_ge(s_hout, 16 * half)
                sp.wait_ge(s_tp, NT)
                sp.dma_start(wlr, a["w_lr"]).then_inc(s_wlr, 16)
                for j in range(2, n_chunks):
                    sp.wait_ge(s_wlo, j - 1)
                    sp.dma_start(w_raw[:, j % 2], a["w_cols"][j]).then_inc(s_w[j % 2], 16)

            @block.vector
            def _(dve):
                def statistics(i):
                    dve.wait_ge(s_x[i], 16)
                    nc.vector.bn_stats(stat[:, i, 0], x_all[:, i, 0:512])
                    nc.vector.bn_stats(stat[:, i, 1], x_all[:, i, 512:]).then_inc(s_st, 1)
                    dve.wait_ge(s_st, i + 1)
                    nc.vector.bn_aggr(mv[:, i], stat[:, i]).then_inc(s_mv, 1)
                    dve.wait_ge(s_mv, i + 1)
                    nc.vector.tensor_scalar(rstd[:, i:i + 1], mv[:, i, 1:2], LN_EPS, None, ALU.add).then_inc(s_ve, 1)

                def scales(i):
                    dve.wait_ge(s_sq, i + 1)
                    nc.vector.reciprocal(rstd[:, i:i + 1], rstd[:, i:i + 1]).then_inc(s_rs, 1)
                    dve.wait_ge(s_rs, i + 1)
                    nc.vector.scalar_tensor_tensor(shift[:, i:i + 1], mv[:, i, 0:1], -1.0, rstd[:, i:i + 1], ALU.mult, ALU.mult).then_inc(s_sh, 1)

                def times_g(i):
                    dve.wait_ge(s_n, i + 1)
                    nc.vector.tensor_tensor(x_all[:, i], x_all[:, i], lng, ALU.mult).then_inc(s_xg, 1)

                def low_part(i):
                    dve.wait_ge(s_hi, i + 1)
                    nc.vector.tensor_tensor(hT_lo[:, :, i * P:(i + 1) * P], ps_tp(i % 2), hT_hi[:, :, i * P:(i + 1) * P].bitcast(F32),
                                            ALU.subtract).then_inc(s_lo, 1)

                for i in range(NT + 3):
                    if i < NT:
                        statistics(i)
                    if i == 1:
                        dve.wait_ge(s_ln, 32)
                    if 1 <= i <= NT:
                        times_g(i - 1)
                    if i < NT:
                        scales(i)
                    if i == NT + 1:
                        w_low(0)
                    if i >= 3:
                        low_part(i - 3)

                def step(ins, wait=True):
                    done["dve"] += 1
                    ins.then_inc(s_d, 1)
                    if wait:
                        dve.wait_ge(s_d, done["dve"])

                hf = flat(k_all[:, 2:4])
                w_low(1)
                dve.wait_ge(s_par, 32)
                step(nc.vector.tensor_tensor(tmp[:, 0:2], col[:, 2:4], col[:, 2:4], ALU.subtract))
                dve.wait_ge(s_a, 1)
                step(nc.vector.reciprocal(tmp[:, 2:4], tmp[:, 0:2]))
                step(nc.vector.tensor_tensor(tmp[:, 0:2], tmp[:, 0:2], tmp[:, 2:4], ALU.mult))
                step(nc.vector.tensor_tensor(lb[:, 0:2], tmp[:, 0:2], tmp[:, 0:2], ALU.subtract))
                step(nc.vector.tensor_scalar(lb[:, 2:4], lb[:, 0:2], -1.0, 1.0, ALU.mult, ALU.add))
                step(nc.vector.tensor_scalar(lb[:, 4:6], lb[:, 2:4], -1.0, None, ALU.mult))
                dve.wait_ge(s_wlrs, 1)
                nc.vector.tensor_tensor(wlr_split[:, :, RANK:], wlr, wlr_split[:, :, 0:RANK].bitcast(F32), ALU.subtract).then_inc(s_wlrs, 1)
                for j in range(2, 6):
                    w_low(j)
                dve.wait_ge(s_ev, 4)
                dve.wait_ge(s_hout, 16 * half)
                step(nc.vector.scalar_tensor_tensor(t, hf, -1.0, hf, ALU.mult, ALU.min))
                dve.wait_ge(s_a, 2)
                step(nc.vector.scalar_tensor_tensor(u, hf, 0.0, t, ALU.min, ALU.subtract))
                step(nc.vector.tensor_scalar(t, u, -1.0, 80.0, ALU.mult, ALU.min))
                w_low(6)
                dve.wait_ge(s_a, 4)
                for f in range(2):
                    step(nc.vector.tensor_scalar(k_all[:, 2 + f], k_all[:, 2 + f], lb[:, 4 + f:5 + f], lb[:, 2 + f:3 + f], ALU.mult, ALU.add), False)
                    step(nc.vector.tensor_scalar(row(t, f), row(t, f), -1.0, lb[:, f:f + 1], ALU.add, ALU.mult))
                w_low(7)
                dve.wait_ge(s_a, 5)
                step(nc.vector.tensor_tensor(u, u, t, ALU.add))
                dve.wait_ge(s_restart, 16)
                for f in range(2):
                    step(nc.vector.tensor_tensor_scan(G[:, 2 + f], restart, row(u, f), 0.0, ALU.mult, ALU.add))
                w_low(8)
                dve.wait_ge(s_z, 1)
                for f in range(2):
                    last = nc.vector.tensor_scalar(row(z, f), flat(ps[:, 4 + 2 * f:6 + 2 * f, :]), col[:, f:f + 1], None, ALU.add)
                last.then_inc(s_zev, 1)
                dve.wait_ge(s_zev, 1)
                step(nc.vector.scalar_tensor_tensor(t, z, -1.0, z, ALU.mult, ALU.min))
                dve.wait_ge(s_a, 6)
                step(nc.vector.scalar_tensor_tensor(u, z, 0.0, t, ALU.min, ALU.subtract))
                for f in range(2):
                    step(nc.vector.tensor_tensor_scan(G[:, f], restart, row(u, f), 0.0, ALU.mult, ALU.add))
                for j in range(9, n_chunks):
                    w_low(j)

            @block.gpsimd
            def _(pool):
                pool.wait_ge(s_ln, 32)
                for i in range(NT):
                    pool.wait_ge(s_xg, i + 1)
                    nc.gpsimd.tensor_tensor(x_all[:, i], x_all[:, i], lnb, ALU.add).then_inc(s_h, 1)

            @block.scalar
            def _(act):
                def high_part(i):
                    act.wait_ge(s_tp, i + 1)
                    nc.scalar.copy(hT_hi[:, :, i * P:(i + 1) * P], ps_tp(i % 2)).then_inc(s_hi, 1)

                for i in range(NT):
                    act.wait_ge(s_ve, i + 1)
                    nc.scalar.activation(rstd[:, i:i + 1], rstd[:, i:i + 1], ACT.Sqrt).then_inc(s_sq, 1)
                    act.wait_ge(s_sh, i + 1)
                    nc.scalar.activation(x_all[:, i], x_all[:, i], ACT.Identity, bias=shift[:, i:i + 1], scale=rstd[:, i:i + 1]).then_inc(s_n, 1)
                    if i >= 2:
                        high_part(i - 2)
                w_high(0)
                high_part(NT - 2)
                w_high(1)
                high_part(NT - 1)

                def step(*functions):
                    for n, (x, function, scale, bias) in enumerate(functions):
                        done["act"] += 1
                        nc.scalar.activation(x[0], x[-1], function, scale=scale, bias=bias).then_inc(s_a2, 1)
                        act.wait_ge(s_a2, done["act"])
                    act.sem_inc(s_a, 1)

                act.wait_ge(s_d, 1)
                step(((tmp[:, 0:2],), ACT.Exp, 1.0, 0.0))
                act.wait_ge(s_wlr, 16)
                nc.scalar.copy(wlr_split[:, :, 0:RANK], wlr).then_inc(s_wlrs, 1)
                for j in range(LOCAL):
                    evacuate_local(j)
                    w_high(j + 2)
                act.wait_ge(s_d, 7)
                step(((t,), ACT.Exp, 1.0, 0.0), ((t,), ACT.Ln, 1.0, 1.0))
                act.wait_ge(s_hout, 16 * half)
                evacuate(4)
                w_high(6)
                act.wait_ge(s_d, 9)
                step(((flat(k_all[:, 2:4]), u), ACT.Exp, 1.0, 0.0))
                step(((t,), ACT.Exp, 1.0, 0.0))
                act.wait_ge(s_d, 13)
                step(((t,), ACT.Ln, 1.0, 1.0))
                evacuate(5)
                w_high(7)
                evacuate(6)
                w_high(8)
                act.wait_ge(s_lr, 1)
                nc.scalar.copy(lrT, flat(ps[0:2 * RANK, 4:6, :])).then_inc(s_lrev, 1)
                act.wait_ge(s_d, 17)
                step(((t,), ACT.Exp, 1.0, 0.0), ((t,), ACT.Ln, 1.0, 1.0))
                for j in range(NFM, n_chunks - 2):
                    evacuate(j)
                    w_high(j + 2)
                act.wait_ge(s_d, 20)
                last = G[:].rearrange("p g (c t) -> p g c t", t=CH)[:, :, :, CH - 1]
                nc.scalar.activation(EG[:, 0:2], last[:, 0:2], ACT.Exp, scale=group_scale(0))
                nc.scalar.activation(EG[:, 2:4], last[:, 2:4], ACT.Exp)
                evacuate(n_chunks - 2)
                evacuate(n_chunks - 1)

            @block.tensor
            def _(pe):
                pe.wait_ge(a["consts_loaded"], 16)

                for t in range(NT):
                    pe.wait_ge(s_h, t + 1)
                    if t >= 2:
                        pe.wait_ge(s_lo, t - 1)
                    for kt in range(KT):
                        last = nc.tensor.transpose(ps_tp(t % 2)[:, kt, :], x_all[:, t, kt * P:(kt + 1) * P], a["ident"][:])
                    last.then_inc(s_tp, 1)
                pe.wait_ge(s_lo, NT)

                def feature_major(j, p, first=False):
                    pe.wait_ge(s_wlo, j + 1)
                    if not first:
                        pe.wait_ge(s_ev, j - 1)
                    for ft in range(2):
                        for kt in range(KT):
                            w = slice(ft * P, (ft + 1) * P)
                            for n, (wt, ht) in enumerate(((w_hi, hT_hi), (w_hi, hT_lo), (w_lo, hT_hi))):
                                for h in range(2):
                                    last = nc.tensor.matmul(ps[:, p * 4 + ft * 2 + h, :], wt[:, p, kt, w], ht[:, kt, h * 512:(h + 1) * 512],
                                                            start=(kt == 0 and n == 0), stop=(kt == KT - 1 and n == 2))
                    last.then_inc(s_mm, 1)

                def token_major(j, p):
                    pe.wait_ge(s_wlo, j + 1)
                    pe.wait_ge(s_ev, j - 1)
                    for t in range(NT):
                        for kt in range(KT):
                            for n, (wt, ht) in enumerate(((w_hi, hT_hi), (w_lo, hT_hi), (w_hi, hT_lo))):
                                last = nc.tensor.matmul(ps[:, p * 4 + t // 2, (t % 2) * CC:(t % 2 + 1) * CC], ht[:, kt, t * P:(t + 1) * P],
                                                        wt[:, p, kt, :], start=(kt == 0 and n == 0), stop=(kt == KT - 1 and n == 2))
                    last.then_inc(s_mm, 1)

                for p in range(2):
                    feature_major(p, p, True)
                with pe.Fori(1, (NFM - 1) // 2) as i:
                    for p in range(2):
                        feature_major(i * 2 + p, p)
                feature_major(NFM - 1, 0)
                pe.wait_ge(s_wlrs, 2)
                pe.wait_ge(s_ev, NFM - 1)
                for h in range(2):
                    for kt in range(KT):
                        for n, ht in enumerate((hT_hi, hT_lo)):
                            last = nc.tensor.matmul(ps[0:2 * RANK, 4 + h, :], wlr_split[:, kt, :], ht[:, kt, h * 512:(h + 1) * 512],
                                                    start=(kt == 0 and n == 0), stop=(kt == KT - 1 and n == 1))
                last.then_inc(s_lr, 1)
                pe.wait_ge(s_lrev, 1)
                pe.wait_ge(s_par, 32)
                for f in range(2):
                    for h in range(2):
                        last = nc.tensor.matmul(ps[:, 4 + 2 * f + h, :], expand[:, f * P:(f + 1) * P], lrT[:, h * 512:(h + 1) * 512],
                                                start=True, stop=True)
                last.then_inc(s_z, 1)
                pe.wait_ge(s_zev, 1)
                with pe.Fori(0, NTM // 2) as i:
                    for p in (1, 0):
                        token_major(i * 2 + (NFM + 1 - p), p)


NG = 4
LEVELS = 7
CH = P


def group_dv(g):
    return GLA_V if g < 2 else HG_I


def group_cols(g):
    return slice(2 * GLA_V * g, 2 * GLA_V * (g + 1)) if g < 2 else \
        slice(GLA_H * GLA_V + 2 * HG_I * (g - 2), GLA_H * GLA_V + 2 * HG_I * (g - 1))


def group_scale(g):
    return 1.0 / 16.0 if g < 2 else 1.0


def mix(nc, a, v_all, qkg, EG, ms, views):
    with ExitStack() as stack:
        k = Kit(nc, stack)
        KL = k.sb("KL", [P, 2, LEVELS, SEQ])
        QL = k.sb("QL", [P, 2, LEVELS, SEQ // 2])
        QH = k.sb("QH", [P, 2, SEQ])
        KH = k.sb("KH", [P, 2, SEQ])
        E = k.sb("E", [P, 2, SEQ])
        EF = k.sb("EF", [P, SEQ])
        S = k.sb("S", [P, 2, 2, CH])
        khat = k.sb("khat", [P, 2, P])
        state = k.sb("state", [P, 2, 2, 2 * GLA_V])
        masks = k.sb("masks", [P, 6, CH // 2], I32)
        diag = k.sb("diag", [P, CH], I32)
        psX = k.ps("psX", [P, 2, 2, 512])
        psC = k.ps("psC", [P, 2, 512])
        psO = k.ps("psO", [P, 512])
        psU = k.ps("psU", [P, 512])
        s_zero, s_mask = k.sem("zeroed"), k.sem("masks_loaded")
        s_sub, s_exp, s_qm, s_km = k.sem("exponents_ready"), k.sem("decays_ready"), k.sem("q_decayed"), k.sem("k_decayed")
        s_sc, s_xd, s_xa, s_ap, s_st, s_o = (k.sem(n) for n in (
            "scores_done", "fine_levels_copied", "coarse_levels_copied", "chunk_applied", "state_ready", "o_ready"))
        s_lv, s_v = k.sem("level_copied"), k.sem("v_loaded")
        zrow = k.sb("zrow", [P, D])
        q_all, k_all, G = (qkg[:, NG * n:NG * (n + 1)] for n in range(3))
        gates, conv = views
        gn, cw = k.sb("gn", [P, 768]), k.sb("cw", [P, 2, CONV_W])
        bch = KL[:, 0, 0:6].rearrange("p (f n) t -> p f n t", n=3)
        sq = QL[:, 0].rearrange("p a b -> p (a b)")[:, 0:2 * 768].rearrange("p (a b) -> p a b", a=2)
        s_kl, s_p, s_g, s_silu, s_sq, s_ms = (k.sem(n) for n in (
            "kl_zeroed", "norm_params_loaded", "gates_loaded", "silu_done", "squared", "sums_done"))
        s_cv = [k.sem(f"conv{f}_loaded") for f in range(2)]
        s_gn, s_cs = k.sem("gates_scaled"), k.sem("conv_steps")
        LAST = (NG - 1) * NT
        s_zrow, s_yz = k.sem("zero_row_ready"), k.sem("y_overflow_zeroed")
        steps = NG * NT
        ITEMS = [(0, 1)] + [(c + 1,) for c in range(1, NT - 1)] + [()]

        def halves(x, level):
            return x.rearrange("p (b h s) -> p b h s", h=2, s=1 << level)

        def exponents(g, item):
            m = 8 * g + item
            if m >= 2:
                nc.vector.wait_ge(s_km, m - 1)
                nc.vector.wait_ge(s_qm, m - 1)
            e = E[:, item % 2]
            if item == 0:
                gc = G[:, g].rearrange("p (c t) -> p c t", t=CH)
                nc.vector.tensor_tensor(e.rearrange("p (c t) -> p c t", t=CH), gc[:, :, CH - 1:CH].broadcast_to((P, NT, CH)), gc,
                                        ALU.subtract).then_inc(s_sub, 1)
                return
            level, s = item - 1, 1 << (item - 1)
            gh, eh = halves(G[:, g], level), halves(e, level)
            ref = gh[:, :, 0, s - 1:s].broadcast_to((P, SEQ // (2 * s), s))
            nc.vector.tensor_tensor(eh[:, :, 0, :], ref, gh[:, :, 0, :], ALU.subtract)
            nc.vector.tensor_tensor(eh[:, :, 1, :], gh[:, :, 1, :], ref, ALU.subtract).then_inc(s_sub, 1)

        def decay_q(g, item):
            nc.vector.wait_ge(s_exp, 8 * g + item + 1)
            if item == 0:
                nc.vector.tensor_tensor(QH[:, g % 2], q_all[:, g], EF[:], ALU.mult).then_inc(s_qm, 1)
                return
            level, s = item - 1, 1 << (item - 1)
            nc.vector.tensor_tensor(QL[:, g % 2, level].rearrange("p (b s) -> p b s", s=s), halves(q_all[:, g], level)[:, :, 1, :],
                                    halves(E[:, item % 2], level)[:, :, 1, :], ALU.mult).then_inc(s_qm, 1)

        with nc.Block() as block:
            @block.sync
            def _(sp):
                m = a["projM_d"].rearrange("(t p) c -> p t c", p=P)
                for p in range(2):
                    sp.wait_ge(a["projections_stored"][p], 16 * ((NFM + NTM - LOCAL + 1 - p) // 2))
                sp.dma_start(v_all[:, :, 0:512], m[:, :, 0:512]).then_inc(s_v, 16)
                sp.dma_start(v_all[:, :, 512:768], m[:, :, 1024:1280]).then_inc(s_v, 16)
                sp.dma_start(masks[:], a["level_masks"]).then_inc(s_mask, 16)
                sp.dma_start(diag[:], a["diag_mask"]).then_inc(s_mask, 16)
                sp.wait_ge(s_zrow, 1)
                over = a["y_d"][NE * CAP:, :]
                n = NB_OVER * CAP // P
                sp.dma_start(over[0:n * P].rearrange("(n p) d -> p n d", p=P), zrow[:].unsqueeze(1).broadcast_to((P, n, D))).then_inc(s_yz, 16)
                sp.dma_start(over[n * P:], zrow[0:NB_OVER * CAP - n * P]).then_inc(s_yz, 16)
                sp.dma_start(gn[:], a["norm_row"].partition_broadcast(P)).then_inc(s_p, 16)
                sp.dma_start(cw[:], a["conv_cols"]).then_inc(s_p, 16)
                sp.wait_ge(s_ap, LAST)
                sp.wait_ge(s_exp, 8 * NG)
                for gate, c0 in zip(gates, (512, 1280)):
                    sp.dma_start(gate, m[:, :, c0:c0 + gate.shape[2]]).then_inc(s_g, 16)
                for f in range(2):
                    for r in range(3):
                        row = CC * r + f * P
                        sp.dma_start(bch[:, f, r], a["projT_d"][row:row + P, :]).then_inc(s_cv[f], 16)
                sp.wait_ge(s_yz, 32)

            @block.gpsimd
            def _(pool):
                nc.gpsimd.memset(KL[:, 0], 0.0).then_inc(s_kl, 1)
                for g in range(NG):
                    if g == 1:
                        nc.gpsimd.memset(zrow[:], 0.0).then_inc(s_zrow, 1)
                        nc.gpsimd.memset(KL[:, 1], 0.0).then_inc(s_kl, 1)
                    if g < 2:
                        pool.wait_ge(s_kl, g + 1)
                    if g >= 2:
                        pool.wait_ge(s_ap, NT * (g - 1))
                    for item in range(8):
                        pool.wait_ge(s_exp, 8 * g + item + 1)
                        if item == 0:
                            nc.gpsimd.tensor_tensor(KH[:, g % 2], k_all[:, g], E[:, 0], ALU.mult).then_inc(s_km, 1)
                        else:
                            nc.gpsimd.tensor_tensor(halves(KL[:, g % 2, item - 1], item - 1)[:, :, 0, :], halves(k_all[:, g], item - 1)[:, :, 0, :],
                                                    halves(E[:, item % 2], item - 1)[:, :, 0, :], ALU.mult).then_inc(s_km, 1)

                pool.wait_ge(s_p, 32)
                for t in range(NT):
                    pool.wait_ge(s_silu, t + 1)
                    for gate, c0 in zip(gates, (0, 512)):
                        nc.gpsimd.tensor_tensor(gate[:, t], gate[:, t], gn[:, c0:c0 + gate.shape[2]], ALU.mult).then_inc(s_gn, 1)

            @block.vector
            def _(dve):
                def prepare(g, step):
                    if step < 8:
                        exponents(g, step)
                    if step > 0:
                        decay_q(g, step - 1)

                def sums(t):
                    dve.wait_ge(s_sq, t + 1)
                    for part in range(2):
                        last = nc.vector.tensor_reduce(ms[:, t, 4 * part:4 * part + 4], heads(sq[:, t % 2], part), AX.X, ALU.add)
                    last.then_inc(s_ms, 1)

                def convolution(step):
                    f = step // 5
                    b, u, h = (bch[:, f, r] for r in range(3))
                    y = conv[:, f]
                    if step % 5 == 0:
                        dve.wait_ge(s_cv[f], 48)
                        ins = nc.vector.tensor_tensor(u, u, h, ALU.mult)
                    elif step % 5 == 1:
                        ins = nc.vector.tensor_scalar(y, u, cw[:, f, 2:3], None, ALU.mult)
                    elif step % 5 < 4:
                        lag = step % 5 - 1
                        ins = nc.vector.scalar_tensor_tensor(y[:, lag:], u[:, :SEQ - lag], cw[:, f, 2 - lag:3 - lag], y[:, lag:], ALU.mult, ALU.add)
                    else:
                        ins = nc.vector.tensor_tensor(y, y, b, ALU.mult)
                    ins.then_inc(s_cs, 1)
                    dve.wait_ge(s_cs, step + 1)

                for step in range(9):
                    prepare(0, step)
                nc.vector.memset(S[:], 0.0).then_inc(s_zero, 1)
                nc.vector.memset(state[:], 0.0).then_inc(s_zero, 1)
                dve.wait_ge(s_zero, 2)
                dve.wait_ge(s_mask, 32)
                for n in range(steps):
                    g, c, p = n // NT, n % NT, n % 2
                    dve.wait_ge(s_sc, n + 1)
                    for level in range(6):
                        s = 1 << level
                        out = S[:, p].rearrange("p n (b h s) -> p n b h s", h=2, s=s)[:, :, :, 1, :]
                        mask = masks[:, level].rearrange("p (b s) -> p b s", s=s).unsqueeze(1).broadcast_to((P, 2, CH // (2 * s), s))
                        src = psX[:, p, :, level * 64:level * 64 + 64].rearrange("p n (b s) -> p n b s", s=s)
                        nc.vector.copy_predicated(out, mask, src).then_inc(s_lv, 1)
                        dve.wait_ge(s_lv, 6 * n + level + 1)
                    nc.vector.copy_predicated(S[:, p], diag[:].unsqueeze(1).broadcast_to((P, 2, CH)),
                                              psX[:, p, :, 6 * 64:6 * 64 + CH]).then_inc(s_xd, 1)
                    if g + 1 < NG:
                        if c == 0 and g >= 1:
                            dve.wait_ge(s_ap, NT * g)
                        for step in ITEMS[c]:
                            prepare(g + 1, step)
                        if c == NT - 2:
                            prepare(g + 1, 8)
                    else:
                        if c >= 1:
                            sums(c - 1)
                        if c == 2:
                            dve.wait_ge(s_p, 32)
                        if 2 <= c < 7:
                            for i in range(2):
                                convolution(2 * (c - 2) + i)
                    dv = group_dv(g)
                    dve.wait_ge(s_ap, n + 1)
                    if c:
                        dve.wait_ge(s_st, n)
                    for h in range(2):
                        f, cols = slice(64 * h, 64 * h + 64), slice(h * dv, (h + 1) * dv)
                        new, update = state[f, g // 2, p, cols], psU[f, cols]
                        if c == 0:
                            last = nc.vector.tensor_copy(new, update)
                        else:
                            last = nc.vector.scalar_tensor_tensor(new, state[f, g // 2, 1 - p, cols], EG[f, g, c:c + 1], update, ALU.mult, ALU.add)
                    last.then_inc(s_st, 1)
                sums(NT - 1)

            @block.scalar
            def _(act):
                def silu(t):
                    for gate in gates:
                        last = nc.scalar.activation(gate[:, t], gate[:, t], ACT.Silu)
                    last.then_inc(s_silu, 1)

                def decays(g, item):
                    act.wait_ge(s_sub, 8 * g + item + 1)
                    if item == 0:
                        if g:
                            act.wait_ge(s_qm, 8 * g - 7)
                        nc.scalar.activation(EF[:], G[:, g], ACT.Exp, scale=group_scale(g))
                    nc.scalar.activation(E[:, item % 2], E[:, item % 2], ACT.Exp, scale=group_scale(g)).then_inc(s_exp, 1)

                for item in range(8):
                    decays(0, item)
                act.wait_ge(s_zero, 2)
                for n in range(steps):
                    g, c, p = n // NT, n % NT, n % 2
                    act.wait_ge(s_sc, n + 1)
                    if n >= 2:
                        act.wait_ge(s_ap, n - 1)
                    nc.scalar.copy(khat[:, p], psC[:, 0, 64:64 + P])
                    act.wait_ge(s_xd, n + 1)
                    nc.scalar.copy(S[0:64, p, :, 64:128], psC[0:64, :, 0:64]).then_inc(s_xa, 1)
                    if g + 1 < NG:
                        for item in ITEMS[c]:
                            decays(g + 1, item)
                    act.wait_ge(s_ap, n + 1)
                    nc.scalar.copy(v_all[:, c, group_cols(g)], psO[:, 0:2 * group_dv(g)]).then_inc(s_o, 1)
                    if n >= LAST:
                        act.wait_ge(s_o, n + 1)
                        if c >= 2:
                            act.wait_ge(s_ms, c - 1)
                        nc.scalar.activation(sq[:, p], v_all[:, c], ACT.Square).then_inc(s_sq, 1)
                        if c == 3:
                            act.wait_ge(s_g, 32)
                        if c >= 3:
                            for t in range(2 * (c - 3), min(2 * (c - 2), NT)):
                                silu(t)

            @block.tensor
            def _(pe):
                def scores(n):
                    g, c, p = n // NT, n % NT, n % 2
                    pe.wait_ge(s_qm, 8 * g + 8)
                    pe.wait_ge(s_km, 8 * g + 8)
                    if n >= 2:
                        pe.wait_ge(s_xd, n - 1)
                    t = slice(c * CH, (c + 1) * CH)

                    def level_scores(out, f, level):
                        nc.tensor.matmul(out, KL[f, g % 2, level, t], QL[f, g % 2, level, c * 64:c * 64 + 64], start=True, stop=True)

                    for level in range(6):
                        for h in range(2):
                            f = slice(64 * h, 64 * h + 64)
                            level_scores(psX[:, p, h, level * 64:level * 64 + 64], f, level)
                    for h in range(2):
                        f = slice(64 * h, 64 * h + 64)
                        nc.tensor.matmul(psX[:, p, h, 6 * 64:6 * 64 + CH], k_all[f, g, t], q_all[f, g, t], start=True, stop=True)
                    if n >= 1:
                        pe.wait_ge(s_xa, n)
                    for h in range(2):
                        f = slice(64 * h, 64 * h + 64)
                        level_scores(psC[:, h, 0:64], f, 6)
                    nc.tensor.transpose(psC[:, 0, 64:64 + P], KH[:, g % 2, t], a["ident"][:]).then_inc(s_sc, 1)

                def apply(n):
                    g, c, p = n // NT, n % NT, n % 2
                    dv = group_dv(g)
                    v = v_all[:, c, group_cols(g)]
                    pe.wait_ge(s_xd, n + 1)
                    pe.wait_ge(s_xa, n + 1)
                    if n >= 1:
                        pe.wait_ge(s_o, n)
                        pe.wait_ge(s_st, n)
                    if c:
                        nc.tensor.matmul(psO[:, 0:2 * dv], QH[:, g % 2, c * CH:(c + 1) * CH], state[:, g // 2, 1 - p, 0:2 * dv],
                                         start=True, stop=False)
                    for h in range(2):
                        cols = slice(h * dv, (h + 1) * dv)
                        nc.tensor.matmul(psO[:, cols], S[:, p, h], v[:, cols], start=(c == 0), stop=(c == 0 or h == 1))
                    nc.tensor.matmul(psU[:, 0:2 * dv], khat[:, p], v, start=True, stop=True).then_inc(s_ap, 1)

                scores(0)
                pe.wait_ge(s_v, 32)
                for n in range(steps):
                    if n + 1 < steps:
                        scores(n + 1)
                    apply(n)


def mixers(nc, a):
    with ExitStack() as stack:
        k = Kit(nc, stack)
        qkg = k.sb("qkg", [P, 3 * NG, SEQ])
        q_all, k_all, G = (qkg[:, NG * n:NG * (n + 1)] for n in range(3))
        EG = k.sb("EG", [P, NG, NT])
        a["projections_stored"] = [k.sem(f"stage{p}_stored") for p in range(2)]
        project(nc, a, q_all, k_all, G, EG)
        v_all = k.sb("v_all", [P, NT, 768])
        ms = k.sb("mean_squares", [P, NT, 2 * GLA_H])
        gates = (G.rearrange("p a b -> p (a b)").rearrange("p (t c) -> p t c", c=512),
                 k_all[:, 0:2].rearrange("p a b -> p (a b)").rearrange("p (t c) -> p t c", c=256))
        conv = q_all[:, 0:2]
        mix(nc, a, v_all, qkg, EG, ms, (gates, conv))
        project_out(nc, a, v_all, qkg, ms, (gates, conv))


def heads(x, part):
    return (x[:, 0:512] if part == 0 else x[:, 512:768]).rearrange("p (n d) -> p n d", n=4)


def project_out(nc, a, o_all, qkg, ms, views):
    with ExitStack() as stack:
        k = Kit(nc, stack)
        OC = P
        n_cols = D // OC
        gates, conv = views
        h, r = qkg[:, 2:4], qkg[:, 6:8]
        yT_hi, yT_lo = k.sb("yT_hi", [P, 2, KT, P], F32R), k.sb("yT_lo", [P, 2, KT, P], F32R)
        RAW = 4
        wo_raw = k.sb("wo_raw", [P, RAW, KT, OC])
        wo_hi, wo_lo = k.sb("wo_hi", [P, KT, D], F32R), k.sb("wo_lo", [P, KT, D], F32R)
        lng, lnb = k.sb("mixg", [P, D]), k.sb("mixb", [P, D])
        hT = k.sb("h2T", [P, 2, D])
        wr, br = k.sb("wr", [P, KT, NE]), k.sb("br", [P, NE])
        stat, mv, rs = k.sb("stat2", [P, 2, 2, 6]), k.sb("mv2", [P, 2, 2]), k.sb("rs2", [P, 2])
        logits = a["logits"]
        psM = k.ps("psM", [P, 2, D])
        psT = k.ps("psT", [P, D])
        psL = k.ps("psL", [P, 512])
        s_w = [k.sem(f"wo_raw{p}_loaded") for p in range(RAW)]
        s_h = [k.sem(f"h_in{p}_loaded") for p in range(2)]
        s_st = [k.sem(f"h2_{p}_stored") for p in range(2)]
        s_p, s_whi, s_wlo, s_mm, s_d, s_sq, s_h2, s_tp, s_hT, s_lg, s_ev = (k.sem(n) for n in (
            "mix_params_loaded", "wo_hi_ready", "wo_lo_ready", "mix_multiplied", "dve_steps", "sqrt_done", "h2_ready",
            "h2_transposed", "h2T_ready", "logits_multiplied", "logits_ready"))
        s_ms, s_rsq, s_rms, s_n, s_y, s_ytp, s_hi, s_lo = (k.sem(n) for n in (
            "mean_squares_ready", "rms_ready", "rms_inverted", "normed", "y_ready", "y_transposed", "yT_hi_ready", "yT_lo_ready"))
        y_tile = psT[:, 0:768].rearrange("p (f t) -> p f t", t=P)
        token = lambda t: conv[:, :, t * P:(t + 1) * P]

        with nc.Block() as block:
            @block.sync
            def _(sp):
                for c in range(n_cols):
                    if c >= RAW:
                        sp.wait_ge(s_wlo, c - RAW + 1)
                    sp.dma_start(wo_raw[:, c % RAW], a["w_out"][:, c * OC:(c + 1) * OC].rearrange("(k p) n -> p k n", p=P)).then_inc(s_w[c % RAW], 16)
                for dst, src in ((lng, "ln_mix_g"), (lnb, "ln_mix_b"), (br, "b_router")):
                    sp.dma_start(dst[:], a[src].partition_broadcast(P)).then_inc(s_p, 16)
                sp.dma_start(wr[:], a["w_router"].rearrange("(k p) e -> p k e", p=P)).then_inc(s_p, 16)
                for t in range(NT):
                    p = t % 2
                    if t >= 2:
                        sp.wait_ge(s_d, 6 * (t - 2) + 1)
                    sp.dma_start(h[:, p], a["h_d"][t * P:(t + 1) * P, :]).then_inc(s_h[p], 16)
                    if t >= 1:
                        sp.wait_ge(s_h2, t)
                        sp.dma_start(a["h2_d"][(t - 1) * P:t * P, :], r[:, 1 - p]).then_inc(s_st[1 - p], 16)
                sp.wait_ge(s_h2, NT)
                sp.dma_start(a["h2_d"][(NT - 1) * P:, :], r[:, 1]).then_inc(s_st[1], 16)
                for p in range(2):
                    sp.wait_ge(s_st[p], 16 * (NT // 2))

            @block.vector
            def _(dve):
                def w_low(c):
                    dve.wait_ge(s_whi, c + 1)
                    cols = slice(c * OC, (c + 1) * OC)
                    nc.vector.tensor_tensor(wo_lo[:, :, cols], wo_raw[:, c % RAW], wo_hi[:, :, cols].bitcast(F32), ALU.subtract).then_inc(s_wlo, 1)

                def scale_y(t):
                    for part, dv in ((0, GLA_V), (1, HG_I)):
                        o = heads(o_all[:, t], part)
                        last = nc.vector.tensor_tensor(o, o, ms[:, t, 4 * part:4 * part + 4].unsqueeze(2).broadcast_to((P, 4, dv)), ALU.mult)
                    last.then_inc(s_n, 1)
                    dve.wait_ge(s_n, t + 1)
                    for gate, c0 in zip(gates, (0, 512)):
                        o = o_all[:, t, c0:c0 + gate.shape[2]]
                        last = nc.vector.tensor_tensor(o, o, gate[:, t], ALU.mult)
                    last.then_inc(s_y, 1)

                def low_part(t):
                    dve.wait_ge(s_hi, t + 1)
                    nc.vector.tensor_tensor(yT_lo[:, t % 2, 6:8], token(t), yT_hi[:, t % 2, 6:8].bitcast(F32), ALU.subtract)
                    nc.vector.tensor_tensor(yT_lo[:, t % 2, 0:6], y_tile, yT_hi[:, t % 2, 0:6].bitcast(F32), ALU.subtract).then_inc(s_lo, 1)

                nc.vector.tensor_scalar(ms[:, :, 0:4], ms[:, :, 0:4], 1.0 / GLA_V, RMS_EPS, ALU.mult, ALU.add)
                nc.vector.tensor_scalar(ms[:, :, 4:8], ms[:, :, 4:8], 1.0 / HG_I, RMS_EPS, ALU.mult, ALU.add).then_inc(s_ms, 1)
                dve.wait_ge(s_rsq, 1)
                nc.vector.reciprocal(ms[:], ms[:]).then_inc(s_rms, 1)
                dve.wait_ge(s_rms, 1)
                scale_y(0)
                w_low(0)
                w_low(1)
                low_part(0)
                scale_y(1)
                for c in range(2, n_cols):
                    w_low(c)
                low_part(1)
                scale_y(2)
                dve.wait_ge(s_p, 64)
                steps = [0]

                def step(ins, wait=True):
                    steps[0] += 1
                    ins.then_inc(s_d, 1)
                    if wait:
                        dve.wait_ge(s_d, steps[0])

                for t in range(NT):
                    p = t % 2
                    dve.wait_ge(s_mm, t + 1)
                    dve.wait_ge(s_h[p], 16 * (t // 2) + 16)
                    if t >= 2:
                        dve.wait_ge(s_st[p], 16 * (t // 2))
                        dve.wait_ge(s_tp, t - 1)
                    step(nc.vector.scalar_tensor_tensor(r[:, p], h[:, p], ALPHA, psM[:, p], ALU.mult, ALU.add))
                    nc.vector.bn_stats(stat[:, p, 0], r[:, p, 0:512])
                    step(nc.vector.bn_stats(stat[:, p, 1], r[:, p, 512:1024]))
                    step(nc.vector.bn_aggr(mv[:, p], stat[:, p]))
                    step(nc.vector.tensor_scalar(rs[:, p:p + 1], mv[:, p, 1:2], LN_EPS, None, ALU.add), False)
                    step(nc.vector.scalar_tensor_tensor(r[:, p], r[:, p], mv[:, p, 0:1], lng[:], ALU.subtract, ALU.mult), False)
                    if t >= 1:
                        dve.wait_ge(s_lg, t)
                        nc.vector.tensor_tensor(logits[:, t - 1], psL[:, 0:NE], br[:], ALU.add).then_inc(s_ev, 1)
                    dve.wait_ge(s_sq, t + 1)
                    step(nc.vector.reciprocal(rs[:, p:p + 1], rs[:, p:p + 1]))
                    nc.vector.scalar_tensor_tensor(r[:, p], r[:, p], rs[:, p:p + 1], lnb[:], ALU.mult, ALU.add).then_inc(s_h2, 1)
                    if t + 2 < NT:
                        low_part(t + 2)
                    if t + 3 < NT:
                        scale_y(t + 3)
                dve.wait_ge(s_lg, NT)
                nc.vector.tensor_tensor(logits[:, NT - 1], psL[:, 0:NE], br[:], ALU.add).then_inc(s_ev, 1)

            @block.scalar
            def _(act):
                def w_high(c):
                    act.wait_ge(s_w[c % RAW], 16 * (c // RAW) + 16)
                    nc.scalar.copy(wo_hi[:, :, c * OC:(c + 1) * OC], wo_raw[:, c % RAW]).then_inc(s_whi, 1)

                def high_part(t):
                    act.wait_ge(s_ytp, t + 1)
                    nc.scalar.copy(yT_hi[:, t % 2, 6:8], token(t))
                    nc.scalar.copy(yT_hi[:, t % 2, 0:6], y_tile).then_inc(s_hi, 1)

                def h2_feature_major(t):
                    act.wait_ge(s_tp, t + 1)
                    nc.scalar.copy(hT[:, t % 2], psT[:]).then_inc(s_hT, 1)

                act.wait_ge(s_ms, 1)
                nc.scalar.activation(ms[:], ms[:], ACT.Sqrt).then_inc(s_rsq, 1)
                w_high(0)
                w_high(1)
                high_part(0)
                for c in range(2, n_cols):
                    w_high(c)
                high_part(1)
                for t in range(NT):
                    p = t % 2
                    if t >= 1:
                        h2_feature_major(t - 1)
                    act.wait_ge(s_d, 6 * t + 4)
                    nc.scalar.activation(rs[:, p:p + 1], rs[:, p:p + 1], ACT.Sqrt).then_inc(s_sq, 1)
                    if t + 2 < NT:
                        high_part(t + 2)
                h2_feature_major(NT - 1)

            @block.tensor
            def _(pe):
                def y_transpose(t):
                    pe.wait_ge(s_y, t + 1)
                    if t in (1, 2):
                        pe.wait_ge(s_lo, t)
                    if t >= 3:
                        pe.wait_ge(s_hT, t - 2)
                    for f in range(6):
                        last = nc.tensor.transpose(y_tile[:, f], o_all[:, t, f * P:(f + 1) * P], a["ident"][:])
                    last.then_inc(s_ytp, 1)

                def output_tile(t):
                    p = t % 2
                    pe.wait_ge(s_lo, t + 1)
                    if t >= 2:
                        pe.wait_ge(s_d, 6 * (t - 2) + 1)
                    for kt in range(KT):
                        for n, (y, w) in enumerate(((yT_hi, wo_hi), (yT_hi, wo_lo), (yT_lo, wo_hi))):
                            for half in range(2):
                                c = slice(half * 512, half * 512 + 512)
                                last = nc.tensor.matmul(psM[:, p, c], y[:, p, kt], w[:, kt, c],
                                                        start=(kt == 0 and n == 0), stop=(kt == KT - 1 and n == 2))
                    last.then_inc(s_mm, 1)

                def logit_tile(t):
                    p = t % 2
                    pe.wait_ge(s_h2, t + 1)
                    pe.wait_ge(s_lo, min(t + 3, NT))
                    for kt in range(KT):
                        last = nc.tensor.transpose(psT[:, kt * P:(kt + 1) * P], r[:, p, kt * P:(kt + 1) * P], a["ident"][:])
                    last.then_inc(s_tp, 1)
                    if t >= 1:
                        pe.wait_ge(s_ev, t)
                    pe.wait_ge(s_hT, t + 1)
                    for kt in range(KT):
                        last = nc.tensor.matmul(psL[:, 0:NE], hT[:, p, kt * P:(kt + 1) * P], wr[:, kt], start=(kt == 0), stop=(kt == KT - 1))
                    last.then_inc(s_lg, 1)

                y_transpose(0)
                y_transpose(1)
                pe.wait_ge(s_wlo, n_cols)
                pe.wait_ge(s_p, 64)
                for t in range(NT):
                    output_tile(t)
                    if t >= 1:
                        logit_tile(t - 1)
                    if t + 2 < NT:
                        y_transpose(t + 2)
                logit_tile(NT - 1)


CAP = 160
TAIL = CAP - 128
FOLD = 128 // TAIL
SIZES = (128, 136, 144, CAP)
NB_OVER = 25
NSLOT = (NE + NB_OVER) * CAP


def route(nc, a, ex):
    before_exp = [0]
    gate, slot_i, idx, ids = a["gate"], a["slot_i"], a["idx"], a["block_expert"]
    NB = NE + NB_OVER
    NBE = NB + NB % 2
    with ExitStack() as stack:
        k = Kit(nc, stack)
        lg = a["logits"]
        top, topi = k.sb("top", [P, NT, 8]), k.sb("topi", [P, NT, 8], U32)
        topf = k.sb("topf", [P, NT, TOPK])
        den = k.sb("den", [P, NT])
        oh, picked = (x[:].rearrange("p h q t -> p (h q t)")[:, 0:NT * TOPK * NE].rearrange("p (t k e) -> p t k e", k=TOPK, e=NE)
                      for x in (ex.g, ex.u))
        M, C = k.sb("M", [P, NT, NE]), k.sb("C", [P, NT + 1, NE])
        cnt, nb, first, before, sizef = (k.sb(n, [P, NE]) for n in ("count", "blocks_beyond", "blocks_through", "blocks_before", "size"))
        cmp = k.sb("cmp", [P, NB_OVER, NE])
        bexp = k.sb("bexp", [P, NB_OVER])
        n_places = 2 * P
        cst = k.sb("cst", [P, NBE + n_places])
        fold = k.sb("fold", [P, 1])
        tri, ones = k.sb("tri", [P, P]), k.sb("ones", [P, P])
        pos, full, base, block, slotf = (k.sb(n, [P, NT, TOPK]) for n in ("position", "full_blocks", "base", "block", "slotf"))
        tok = k.sb("tok", [P, NT])
        ROWS = 4
        place_row = k.sb("place_row", [P, ROWS, n_places], F32R)
        block_oh = k.sb("block_oh", [P, NT, TOPK, NBE])
        block_row = k.sb("block_row", [P, NT, TOPK, NBE], F32R)
        ps = ex.ps[:, 0, 0:NT * NE].rearrange("p (t e) -> p t e", e=NE)
        psC = ex.ps[:, 1]
        psI = ex.ps[:, 2:4]
        s_c, s_d, s_e, s_oh, s_pos, s_row, s_used, s_ones = (k.sem(n) for n in (
            "route_consts_loaded", "dve_steps", "exp_done", "choices_ready", "positions_ready", "rows_ready", "rows_used",
            "ones_ready"))
        per_pair = lambda x: x.rearrange("p t k -> p (t k)")
        wide = lambda x, n: per_pair(x).unsqueeze(2).broadcast_to((P, NT * TOPK, n))
        pairs = lambda x: x.rearrange("p t k e -> p (t k) e")

        with nc.Block() as block_:
            @block_.sync
            def _(sp):
                for dst, src in ((cst, "route_c"), (fold, "fold_c"), (tri, "tri_c"), (tok, "token_c")):
                    sp.dma_start(dst[:], a[src]).then_inc(s_c, 16)
                for j in range(CHUNKS):
                    ex.load_chunk(sp, 0, j)

            @block_.vector
            def _(dve):
                steps = [0]

                def step(ins, wait=True):
                    steps[0] += 1
                    ins.then_inc(s_d, 1)
                    if wait:
                        dve.wait_ge(s_d, steps[0])

                nc.vector.memset(ones[:], 1.0).then_inc(s_ones, 1)
                nc.vector.memset(C[:, 0], 0.0).then_inc(s_ones, 1)
                for t in range(NT):
                    step(nc.vector.max(top[:, t], lg[:, t]), t == NT - 1)
                for t in range(NT):
                    step(nc.vector.max_index(topi[:, t], top[:, t], lg[:, t]), t == NT - 1)
                step(nc.vector.tensor_copy(topf[:], topi[:, :, 0:TOPK]), False)
                step(nc.vector.tensor_tensor(gate[:], top[:, :, 0:TOPK], top[:, :, 0:1].broadcast_to((P, NT, TOPK)), ALU.subtract))
                before_exp[0] = steps[0]
                dve.wait_ge(s_c, 64)
                step(nc.vector.tensor_tensor(pairs(oh), wide(topf[:], NE), cst[:, 0:NE].unsqueeze(1).broadcast_to((P, NT * TOPK, NE)),
                                             ALU.is_equal))
                step(nc.vector.tensor_reduce(M[:], oh.rearrange("p t k e -> p t e k"), AX.X, ALU.add))
                for t in range(NT):
                    nc.vector.tensor_tensor(C[:, t + 1], C[:, t], M[:, t], ALU.add).then_inc(s_oh, 1)
                    dve.wait_ge(s_oh, t + 1)
                dve.wait_ge(s_e, 1)
                step(nc.vector.tensor_reduce(den[:], gate[:], AX.X, ALU.add))
                step(nc.vector.reciprocal(den[:], den[:]))
                step(nc.vector.tensor_tensor(gate[:], gate[:], den[:].unsqueeze(2).broadcast_to((P, NT, TOPK)), ALU.mult), False)
                dve.wait_ge(s_pos, 1)
                step(nc.vector.tensor_tensor(picked, oh, ps.unsqueeze(2).broadcast_to((P, NT, TOPK, NE)), ALU.mult), False)
                step(nc.vector.tensor_copy(cnt[:], psC[:, 0:NE]))
                step(nc.vector.tensor_reduce(pos[:], picked, AX.X, ALU.add), False)
                step(nc.vector.tensor_scalar(nb[:], cnt[:], float(CAP), None, ALU.is_gt))
                for q in range(2, (SEQ - 1) // CAP + 1):
                    step(nc.vector.scalar_tensor_tensor(nb[:], cnt[:], float(q * CAP), nb[:], ALU.is_gt, ALU.add))
                step(nc.vector.tensor_tensor_scan(first[:], ones[:, 0:NE], nb[:], 0.0, ALU.mult, ALU.add))
                step(nc.vector.tensor_tensor(before[:], first[:], nb[:], ALU.subtract))
                step(nc.vector.tensor_tensor(picked, oh, before[:].unsqueeze(1).unsqueeze(1).broadcast_to((P, NT, TOPK, NE)), ALU.mult))
                step(nc.vector.tensor_reduce(base[:], picked, AX.X, ALU.add), False)
                step(nc.vector.tensor_scalar(full[:], pos[:], float(CAP), None, ALU.is_ge))
                for q in range(2, (SEQ - 1) // CAP + 1):
                    step(nc.vector.scalar_tensor_tensor(full[:], pos[:], float(q * CAP), full[:], ALU.is_ge, ALU.add))
                step(nc.vector.scalar_tensor_tensor(base[:], base[:], float(NE - 1), full[:], ALU.add, ALU.add))
                step(nc.vector.tensor_tensor(base[:], base[:], topf[:], ALU.subtract), False)
                step(nc.vector.tensor_scalar(block[:], full[:], 1.0, None, ALU.min))
                step(nc.vector.tensor_tensor(block[:], block[:], base[:], ALU.mult))
                step(nc.vector.tensor_tensor(block[:], block[:], topf[:], ALU.add), False)
                step(nc.vector.scalar_tensor_tensor(pos[:], full[:], -float(CAP), pos[:], ALU.mult, ALU.add))
                step(nc.vector.tensor_tensor(pairs(block_oh[:]), wide(block[:], NBE), cst[:, 0:NBE].unsqueeze(1).broadcast_to((P, NT * TOPK, NBE)),
                                             ALU.is_equal))
                nc.vector.tensor_tensor(block_row[:].rearrange("p t k b -> p t (k b)"), block_oh[:].rearrange("p t k b -> p t (k b)"),
                                        tok[:].unsqueeze(2).broadcast_to((P, NT, TOPK * NBE)), ALU.mult).then_inc(s_row, 1)
                for i in range(NT * TOPK):
                    if i >= ROWS:
                        dve.wait_ge(s_used, i - ROWS + 1)
                    nc.vector.tensor_scalar(place_row[:, i % ROWS], cst[:, NBE:], pos[:, i // TOPK, i % TOPK:i % TOPK + 1], None, ALU.is_equal)\
                        .then_inc(s_row, 1)
                step(nc.vector.scalar_tensor_tensor(slotf[:], block[:], float(CAP), pos[:], ALU.mult, ALU.add))
                nc.vector.tensor_copy(slot_i[:], slotf[:])
                step(nc.vector.tensor_tensor(cmp[:], first[:].unsqueeze(1).broadcast_to((P, NB_OVER, NE)),
                                             cst[:, 0:NB_OVER].unsqueeze(2).broadcast_to((P, NB_OVER, NE)), ALU.is_le))
                step(nc.vector.tensor_reduce(bexp[:, 0:NB_OVER], cmp[:], AX.X, ALU.add))
                step(nc.vector.tensor_scalar(bexp[:, 0:NB_OVER], bexp[:, 0:NB_OVER], float(NE - 1), None, ALU.min))
                nc.vector.tensor_copy(ids[:, 0:NB_OVER], bexp[:, 0:NB_OVER])
                nc.vector.tensor_copy(ids[:, NB_OVER:], first[:, NE - 1:NE])
                step(nc.vector.tensor_scalar(sizef[:], cnt[:], float(SIZES[0]), None, ALU.is_gt))
                for size in SIZES[1:-1]:
                    step(nc.vector.scalar_tensor_tensor(sizef[:], cnt[:], float(size), sizef[:], ALU.is_gt, ALU.add))
                nc.vector.tensor_copy(a["block_size"][:], sizef[:])
                dve.wait_ge(s_used, NT * TOPK)
                nc.vector.tensor_copy(idx[:, 0], psI[:, 0, 0:NB])
                nc.vector.tensor_scalar(idx[:, 1], psI[:, 1, 0:NB], float(FOLD), fold[:], ALU.mult, ALU.add)

            @block_.scalar
            def _(act):
                act.wait_ge(s_d, before_exp[0])
                nc.scalar.activation(gate[:], gate[:], ACT.Exp).then_inc(s_e, 1)

            @block_.tensor
            def _(pe):
                pe.wait_ge(s_oh, NT)
                pe.wait_ge(s_c, 64)
                pe.wait_ge(s_ones, 2)
                nc.tensor.matmul(ex.ps[:, 0, 0:NT * NE], tri[:], M[:].rearrange("p t e -> p (t e)"), start=True, stop=False)
                nc.tensor.matmul(ex.ps[:, 0, 0:NT * NE], ones[:], C[:, 0:NT].rearrange("p t e -> p (t e)"), start=False, stop=True)
                nc.tensor.matmul(psC[:, 0:NE], ones[:], C[:, NT], start=True, stop=True).then_inc(s_pos, 1)
                for i in range(NT * TOPK):
                    pe.wait_ge(s_row, i + 2)
                    for part in range(2):
                        last = nc.tensor.matmul(psI[:, part, 0:NBE], place_row[:, i % ROWS, part * P:(part + 1) * P], block_row[:, i // TOPK, i % TOPK],
                                                start=(i == 0), stop=(i == NT * TOPK - 1))
                    last.then_inc(s_used, 1)


CW = 512
CHUNKS = 6


class Experts:

    def __init__(self, nc, a, k):
        self.nc, self.a = nc, a
        self.w = k.sb("w_expert", [P, CHUNKS, KT, CW])
        self.x0, self.x1 = k.sb("x0", [P, D]), k.sb("x1", [P, D // FOLD])
        self.xT, self.actT = k.sb("xT", [P, KT, CAP]), k.sb("actT", [P, KT, CAP])
        self.g, self.sg, self.u = (k.sb(n, [P, 2, 4, CAP]) for n in ("g_clamped", "g_sigmoid", "u_clamped"))
        self.yT = k.sb("yT", [P, 2, CAP, 4])
        self.y0, self.y1 = k.sb("y0", [P, D]), k.sb("y1", [P, 2, P])
        self.bias = k.sb("bias", [P, 3 * KT, NE])
        self.cur = k.sb("cur_idx", [P, 2], U32)
        self.ps = k.ps("psE", [P, 8, 512])

    def open(self, k):
        names = dict(mm="chunk_multiplied", gu="gate_up_evacuated", dn="down_evacuated", sig="sigmoid_done", mul="up_times_gate",
                     act="actT_ready", xtp="x_transposed", xT="xT_ready", ytp="y_transposed", yev="y_evacuated", cur="idx_copied",
                     go="gather_released")
        self.s = {n: k.sem("ex_" + v) for n, v in names.items()}
        self.s_w = [k.sem(f"w_chunk{j}_loaded") for j in range(CHUNKS)]
        self.s_x = k.sem("x_gathered")
        self.s_y = k.sem("y_stored")

    def load_chunk(self, sp, expert, j):
        a = self.a
        if j < 4:
            src = a["w_gate_up"][bass.ds(expert, 1), :, (j % 2) * DFF + (j // 2) * CW:(j % 2) * DFF + (j // 2 + 1) * CW]
        else:
            src = a["w_down"][bass.ds(expert, 1), :, (j - 4) * CW:(j - 3) * CW]
        sp.dma_start(self.w[:, j], src.rearrange("o (k p) n -> p (o k) n", p=P)).then_inc(self.s_w[j], 16)

    def gather(self, pool, n, first=False):
        nc = self.nc
        if not first:
            pool.wait_ge(self.s["xtp"], n)
        nc.gpsimd.tensor_copy(self.cur[:], self.a["idx"][:, :, bass.ds(n, 1)].rearrange("p a b -> p (a b)")).then_inc(self.s["cur"], 1)
        pool.wait_ge(self.s["cur"], n + 1)
        pool.sem_inc(self.s["go"], 1)
        nc.gpsimd.indirect_dma_start(self.x0[:], None, self.a["h2_d"], bass.IndirectOffsetOnAxis(self.cur[:, 0:1], 0)).then_inc(self.s_x, 16)
        nc.gpsimd.indirect_dma_start(self.x1[:], None, self.a["h2_d"].rearrange("s (b c) -> (s b) c", b=FOLD),
                                     bass.IndirectOffsetOnAxis(self.cur[:, 1:2], 0)).then_inc(self.s_x, 16)

    def x_transpose(self, pe, n, y_done):
        nc = self.nc
        pe.wait_ge(self.s_x, n * 32 + 32)
        if y_done is not None:
            pe.wait_ge(self.s["yev"], 2 * y_done)
        for kt in range(KT):
            nc.tensor.transpose(self.ps[:, 4 + kt // 4, kt % 4 * P:(kt % 4 + 1) * P], self.x0[:, kt * P:(kt + 1) * P], self.a["ident"][:])
        for j in range(2):
            last = nc.tensor.transpose(self.ps[:, 7, (j + 1) * P:(j + 2) * P], self.x1[:, j * P:(j + 1) * P], self.a["ident"][:])
        last.then_inc(self.s["xtp"], 1)

    def x_evacuate(self, act, n):
        nc = self.nc
        act.wait_ge(self.s["xtp"], n + 1)
        nc.scalar.copy(self.xT[:, :, 0:P].rearrange("p (a b) t -> p a b t", a=2), self.ps[:, 4:6].rearrange("p a (b t) -> p a b t", t=P))
        nc.scalar.copy(self.xT[:, :, P:CAP].rearrange("p (b j) s -> p b j s", j=2),
                       self.ps[:, 7, P:3 * P].rearrange("p (j b s) -> p b j s", j=2, b=FOLD)).then_inc(self.s["xT"], 1)

    def multiply(self, pe, n, j, first=False, slots=CAP):
        nc = self.nc
        moving = self.xT if j < 4 else self.actT
        pe.wait_ge(self.s_w[j], n * 16 + 16)
        if j == 0:
            pe.wait_ge(self.s["xT"], n + 1)
        if j < 2:
            if not first:
                pe.wait_ge(self.s["dn"], 2 * n + j - 1)
        else:
            pe.wait_ge(self.s["gu"], 4 * n + j - 1)

        def products(kts, qs=range(4)):
            for q in qs:
                out = self.ps[:, (j % 2) * 2 + q // 2, (q % 2) * CAP:(q % 2) * CAP + slots]
                for kt in kts:
                    last = nc.tensor.matmul(out, self.w[:, j, kt, q * P:(q + 1) * P], moving[:, kt, 0:slots],
                                            start=(kt == 0), stop=(kt == KT - 1))
            return last

        if j == 4:
            pe.wait_ge(self.s["act"], 2 * n + 1)
            products(range(KT // 2), (0, 2))
            pe.wait_ge(self.s["act"], 2 * n + 2)
            products(range(KT // 2, KT), (0, 2))
            products(range(KT), (1, 3)).then_inc(self.s["mm"], 1)
        else:
            products(range(KT)).then_inc(self.s["mm"], 1)

    def gate_evacuate(self, dve, n, half, expert):
        j = 2 * half
        dve.wait_ge(self.s["mm"], n * CHUNKS + j + 1)
        for q in range(4):
            last = self.nc.vector.tensor_scalar(self.g[:, half, q], self.ps[:, (j % 2) * 2 + q // 2, (q % 2) * CAP:(q % 2 + 1) * CAP],
                                                self.bias[:, 4 * half + q, bass.ds(expert, 1)], SWIGLU_LIMIT, ALU.add, ALU.min)
        last.then_inc(self.s["gu"], 1)

    def up_evacuate(self, dve, n, half, expert):
        nc, j = self.nc, 2 * half + 1
        dve.wait_ge(self.s["mm"], n * CHUNKS + j + 1)
        for q in range(4):
            last = nc.vector.tensor_scalar(self.u[:, half, q], self.ps[:, (j % 2) * 2 + q // 2, (q % 2) * CAP:(q % 2 + 1) * CAP],
                                           self.bias[:, KT + 4 * half + q, bass.ds(expert, 1)], SWIGLU_LIMIT + 1.0, ALU.add, ALU.min)
        last.then_inc(self.s["gu"], 1)
        dve.wait_ge(self.s["gu"], 4 * n + 2 * half + 2)
        nc.vector.scalar_tensor_tensor(self.u[:, half], self.u[:, half], 1.0 - SWIGLU_LIMIT, self.g[:, half], ALU.max, ALU.mult)\
            .then_inc(self.s["mul"], 1)
        dve.wait_ge(self.s["mul"], 2 * n + half + 1)
        dve.wait_ge(self.s["sig"], 2 * n + half + 1)
        nc.vector.tensor_tensor(self.actT[:, 4 * half:4 * half + 4], self.u[:, half], self.sg[:, half], ALU.mult).then_inc(self.s["act"], 1)

    def sigmoid(self, act, n, half):
        act.wait_ge(self.s["gu"], 4 * n + 2 * half + 1)
        self.nc.scalar.activation(self.sg[:, half], self.g[:, half], ACT.Sigmoid, scale=SWIGLU_ALPHA).then_inc(self.s["sig"], 1)

    def down_evacuate(self, act, n, half, expert):
        j = 4 + half
        act.wait_ge(self.s["mm"], n * CHUNKS + j + 1)
        for q in range(4):
            last = self.nc.scalar.activation(self.yT[:, half, :, q], self.ps[:, (j % 2) * 2 + q // 2, (q % 2) * CAP:(q % 2 + 1) * CAP],
                                             ACT.Identity, bias=self.bias[:, 2 * KT + 4 * half + q, bass.ds(expert, 1)])
        last.then_inc(self.s["dn"], 1)

    def y_transpose(self, pe, n, half, first=False):
        nc = self.nc
        pe.wait_ge(self.s["dn"], 2 * n + half + 1)
        if half == 0:
            if not first:
                pe.wait_ge(self.s["yev"], 2 * n - 1)
        bank = 6 - 2 * half
        for q in range(4):
            nc.tensor.transpose(self.ps[:, bank, q * P:(q + 1) * P], self.yT[:, half, 0:P, q], self.a["ident"][:])
        nc.tensor.transpose(self.ps[:, bank + 1, 0:P], self.yT[:, half, P:CAP].rearrange("p s q -> p (s q)"), self.a["ident"][:]).then_inc(self.s["ytp"], 1)

    def y_evacuate(self, act, n, half, first=False):
        nc = self.nc
        act.wait_ge(self.s["ytp"], 2 * n + half + 1)
        if not first and half == 0:
            act.wait_ge(self.s_y, n * 48)
        bank, cols = 6 - 2 * half, slice(half * 512, half * 512 + 512)
        nc.scalar.copy(self.y0[:, cols], self.ps[:, bank, :])
        nc.scalar.copy(self.y1[:, half], self.ps[:, bank + 1, 0:P]).then_inc(self.s["yev"], 1)

    def y_store(self, act, n):
        act.wait_ge(self.s["yev"], 2 * n + 2)
        act.dma_start(self.a["y_d"][bass.ds(n * CAP, P), :], self.y0[:]).then_inc(self.s_y, 16)
        for half in range(2):
            act.dma_start(self.a["y_d"][bass.ds(n * CAP + P, TAIL), half * 512:half * 512 + 512].rearrange("s (q f) -> s q f", q=FOLD),
                          self.y1[:, half]).then_inc(self.s_y, 16)


def expert_biases(nc, a, ex):
    with ExitStack() as stack:
        k = Kit(nc, stack)
        s_l, s_t, s_e = k.sem("biases_loaded"), k.sem("biases_transposed"), k.sem("biases_ready")
        rows = k.sb("bias_rows", [NE, 3 * D])
        with nc.Block() as block:
            @block.sync
            def _(sp):
                sp.dma_start(rows[:, 0:2 * DFF], a["b_gate_up"]).then_inc(s_l, 16)
                sp.dma_start(rows[:, 2 * DFF:2 * DFF + D], a["b_down"]).then_inc(s_l, 16)

            @block.tensor
            def _(pe):
                pe.wait_ge(s_l, 32)
                for f in range(3 * KT):
                    last = nc.tensor.transpose(ex.ps[:, f // 16, (f % 16) * NE:(f % 16 + 1) * NE], rows[:, f * P:(f + 1) * P], a["ident"][0:NE, 0:NE])
                last.then_inc(s_t, 1)

            @block.vector
            def _(dve):
                dve.wait_ge(s_t, 1)
                bank = lambda f: ex.ps[:, f // 16, (f % 16) * NE:(f % 16) * NE + KT * NE].rearrange("p (f e) -> p f e", e=NE)
                nc.vector.tensor_copy(ex.bias[:, 0:KT], bank(0))
                nc.vector.tensor_scalar(ex.bias[:, KT:2 * KT], bank(KT), 1.0, None, ALU.add)
                nc.vector.tensor_copy(ex.bias[:, 2 * KT:], bank(2 * KT)).then_inc(s_e, 1)


def experts(nc, a, ex, h2):
    def over(engine, body):
        count = engine.value_load(a["block_expert"][0:1, NB_OVER:NB_OVER + 1], min_val=0, max_val=NB_OVER)
        with engine.If(count > 0):
            with engine.Fori(0, NB_OVER) as b:
                with engine.If(b < count):
                    body(b + NE, engine.value_load(a["block_expert"][0:1, bass.ds(b, 1)], min_val=0, max_val=NE - 1))

    with nc.Block() as block:
        @block.sync
        def _(sp):
            with sp.Fori(1, NE) as e:
                for j in range(CHUNKS):
                    sp.wait_ge(ex.s["mm"], (e - 1) * CHUNKS + j + 1)
                    ex.load_chunk(sp, e, j)

            def body(n, expert):
                for j in range(CHUNKS):
                    sp.wait_ge(ex.s["mm"], (n - 1) * CHUNKS + j + 1)
                    ex.load_chunk(sp, expert, j)
            over(sp, body)
            sp.dma_start(h2[:], a["h2_d"].rearrange("(t p) d -> p t d", p=P)).then_inc(a["h2_loaded"], 16)
            sp.wait_ge(a["h2_loaded"], 16)

        @block.gpsimd
        def _(pool):
            ex.gather(pool, 0, first=True)
            with pool.Fori(1, NE) as e:
                ex.gather(pool, e)
            over(pool, lambda n, expert: ex.gather(pool, n))

        @block.scalar
        def _(act):
            def body(n, expert, ahead, first=False, pending=True):
                if pending:
                    ex.y_evacuate(act, n - 1, 1)
                    ex.y_store(act, n - 1)
                for half in range(2):
                    ex.sigmoid(act, n, half)
                if ahead:
                    ex.x_evacuate(act, n + 1)
                ex.down_evacuate(act, n, 0, expert)
                ex.down_evacuate(act, n, 1, expert)
                ex.y_evacuate(act, n, 0, first)
                if not ahead:
                    ex.y_evacuate(act, n, 1)
                    ex.y_store(act, n)

            ex.x_evacuate(act, 0)
            body(0, 0, True, first=True, pending=False)
            with act.Fori(1, NE - 1) as e:
                body(e, e, True)
            body(NE - 1, NE - 1, False)

            def over_body(n, expert):
                ex.x_evacuate(act, n)
                body(n, expert, False, pending=False)
            over(act, over_body)
            blocks = act.value_load(a["block_expert"][0:1, NB_OVER:NB_OVER + 1], min_val=0, max_val=NB_OVER) + NE
            act.wait_ge(ex.s_y, blocks * 48)
            act.sem_inc(ex.s["go"], 1)

        @block.vector
        def _(dve):
            def body(n, expert):
                for half in range(2):
                    ex.gate_evacuate(dve, n, half, expert)
                    ex.up_evacuate(dve, n, half, expert)

            with dve.Fori(0, NE) as e:
                body(e, e)
            over(dve, body)

        @block.tensor
        def _(pe):
            def body(n, ahead, first=False, pending=True, slots=CAP):
                ex.multiply(pe, n, 0, first, slots)
                if pending:
                    ex.y_transpose(pe, n - 1, 1)
                for j in range(1, 4):
                    ex.multiply(pe, n, j, first, slots)
                if ahead:
                    ex.x_transpose(pe, n + 1, None if first else n)
                ex.multiply(pe, n, 4, slots=slots)
                ex.multiply(pe, n, 5, slots=slots)
                ex.y_transpose(pe, n, 0, first)
                if not ahead:
                    ex.y_transpose(pe, n, 1)

            def sized(n, ahead):
                size = pe.value_load(a["block_size"][0:1, bass.ds(n, 1)], min_val=0, max_val=len(SIZES) - 1)
                for i, slots in enumerate(SIZES):
                    with pe.If(size == i):
                        body(n, ahead, slots=slots)

            ex.x_transpose(pe, 0, None)
            body(0, True, first=True, pending=False)
            with pe.Fori(1, NE - 1) as e:
                sized(e, True)
            sized(NE - 1, False)

            def over_body(n, expert):
                ex.x_transpose(pe, n, n)
                body(n, False, pending=False)
            over(pe, over_body)


def combine(nc, a, h2):
    with ExitStack() as stack:
        k = Kit(nc, stack)
        BUF = 4
        y = k.sb("y", [P, BUF, TOPK, D])
        diag = k.sb("gate_diag", [P, NT, TOPK, P])
        lng, lnb = k.sb("ffng", [P, D]), k.sb("ffnb", [P, D])
        stat, mv, rs, nm = k.sb("stat3", [P, 2, 2, 6]), k.sb("mv3", [P, 2, 2]), k.sb("rstd3", [P, 2]), k.sb("shift3", [P, 2])
        ps = k.ps("ps_sum", [P, 2, D])
        s_p, s_d, s_ve, s_sq, s_rs, s_n, s_out = (k.sem(n) for n in (
            "ffn_params_loaded", "dve_steps", "var_ready", "sqrt_done", "rstd_ready", "normed", "out_ready"))
        s_diag, s_mm, s_sum = k.sem("diagonals_ready"), k.sem("rows_summed"), k.sem("residual_added")
        s_y = [k.sem(f"y{p}_gathered") for p in range(BUF)]
        s_st = k.sem("out_stored")

        with nc.Block() as block:
            @block.gpsimd
            def _(pool):
                for t in range(NT):
                    if t >= BUF:
                        pool.wait_ge(s_mm, t - BUF + 1)
                    for c in range(TOPK):
                        nc.gpsimd.indirect_dma_start(y[:, t % BUF, c], None, a["y_d"], bass.IndirectOffsetOnAxis(a["slot_i"][:, t, c:c + 1], 0))\
                            .then_inc(s_y[t % BUF], 16)

            @block.sync
            def _(sp):
                sp.wait_ge(s_y[0], 16 * TOPK)
                for dst, src in ((lng, "ln_ffn_g"), (lnb, "ln_ffn_b")):
                    sp.dma_start(dst[:], a[src].partition_broadcast(P)).then_inc(s_p, 16)
                for t in range(NT):
                    sp.wait_ge(s_out, t + 1)
                    sp.dma_start(a["out"][0, t * P:(t + 1) * P, :], h2[:, t]).then_inc(s_st, 16)
                sp.wait_ge(s_st, 16 * NT)

            @block.tensor
            def _(pe):
                for t in range(NT):
                    pe.wait_ge(s_diag, t + 1)
                    pe.wait_ge(s_y[t % BUF], 16 * TOPK * (t // BUF + 1))
                    if t >= 2:
                        pe.wait_ge(s_sum, t - 1)
                    for h in range(2):
                        for c in range(TOPK):
                            last = nc.tensor.matmul(ps[:, t % 2, h * 512:(h + 1) * 512], diag[:, t, c], y[:, t % BUF, c, h * 512:(h + 1) * 512],
                                                    start=(c == 0), stop=(c == TOPK - 1))
                    last.then_inc(s_mm, 1)

            @block.vector
            def _(dve):
                steps = [0]

                def step(ins):
                    steps[0] += 1
                    ins.then_inc(s_d, 1)
                    dve.wait_ge(s_d, steps[0])

                def scale_and_shift(t):
                    dve.wait_ge(s_n, t + 1)
                    step(nc.vector.tensor_tensor(h2[:, t], h2[:, t], lng[:], ALU.mult))
                    nc.vector.tensor_tensor(h2[:, t], h2[:, t], lnb[:], ALU.add).then_inc(s_out, 1)

                for t in range(NT):
                    p = t % 2
                    dve.wait_ge(s_mm, t + 1)
                    nc.vector.scalar_tensor_tensor(h2[:, t], h2[:, t], ALPHA, ps[:, p], ALU.mult, ALU.add).then_inc(s_sum, 1)
                    dve.wait_ge(s_sum, t + 1)
                    nc.vector.bn_stats(stat[:, p, 0], h2[:, t, 0:512])
                    step(nc.vector.bn_stats(stat[:, p, 1], h2[:, t, 512:1024]))
                    step(nc.vector.bn_aggr(mv[:, p], stat[:, p]))
                    nc.vector.tensor_scalar(rs[:, p:p + 1], mv[:, p, 1:2], LN_EPS, None, ALU.add).then_inc(s_ve, 1)
                    if t == 0:
                        dve.wait_ge(s_p, 32)
                    else:
                        scale_and_shift(t - 1)
                    dve.wait_ge(s_sq, t + 1)
                    step(nc.vector.reciprocal(rs[:, p:p + 1], rs[:, p:p + 1]))
                    nc.vector.scalar_tensor_tensor(nm[:, p:p + 1], mv[:, p, 0:1], -1.0, rs[:, p:p + 1], ALU.mult, ALU.mult).then_inc(s_rs, 1)
                scale_and_shift(NT - 1)

            @block.scalar
            def _(act):
                for t in range(NT):
                    for c in range(TOPK):
                        last = nc.scalar.activation(diag[:, t, c], a["ident"][:], ACT.Copy, scale=a["gate"][:, t, c:c + 1])
                    last.then_inc(s_diag, 1)
                for t in range(NT):
                    p = t % 2
                    act.wait_ge(s_ve, t + 1)
                    nc.scalar.activation(rs[:, p:p + 1], rs[:, p:p + 1], ACT.Sqrt).then_inc(s_sq, 1)
                    act.wait_ge(s_rs, t + 1)
                    nc.scalar.activation(h2[:, t], h2[:, t], ACT.Identity, bias=nm[:, p:p + 1], scale=rs[:, p:p + 1]).then_inc(s_n, 1)


def build(nc, a):
    with ExitStack() as stack:
        k = Kit(nc, stack)
        a["ident"] = k.sb("ident", [P, P])
        a["consts_loaded"] = k.sem("consts_loaded")
        for name, shape in SCRATCH.items():
            a[name] = nc.dram_tensor(name, shape, F32, kind="Internal").ap()
        with nc.Block() as block:
            @block.sync
            def _(sp):
                sp.dma_start(a["ident"][:], a["ident_c"]).then_inc(a["consts_loaded"], 16)
        for name, shape, dt in KEPT:
            a[name] = k.sb(name, shape, dt)
        mixers(nc, a)
        h2 = k.sb("h2_all", [P, NT, D])
        a["h2_loaded"] = k.sem("h2_loaded")
        with ExitStack() as expert_stack:
            ke = Kit(nc, expert_stack)
            ex = Experts(nc, a, ke)
            ex.open(ke)
            expert_biases(nc, a, ex)
            route(nc, a, ex)
            experts(nc, a, ex, h2)
        combine(nc, a, h2)


KEPT = (
    ("logits", [P, NT, NE], F32),
    ("gate", [P, NT, TOPK], F32),
    ("slot_i", [P, NT, TOPK], U32),
    ("idx", [P, 2, NE + NB_OVER], U32),
    ("block_size", [P, NE], I32),
    ("block_expert", [P, NB_OVER + 1], I32),
)
SCRATCH = {
    "h_d": (SEQ, D), "projT_d": (3 * CC, SEQ), "projM_d": (SEQ, NTM * CC),
    "h2_d": (SEQ, D), "y_d": (NSLOT, D),
}


def level_masks():
    j = np.arange(P)[:, None]
    out = np.zeros((P, 6, CH // 2), np.int32)
    for level in range(6):
        s = 1 << level
        n = np.arange(CH // 2)
        i = (n // s) * 2 * s + s + n % s
        out[:, level] = (j // (2 * s) == i // (2 * s)) & (j // s % 2 == 0)
    return out


def layout(inputs):
    i = {n: np.ascontiguousarray(v) for n, v in inputs.items()}
    w = i["w_in"][0]
    o = np.cumsum([0, 256, 256, 512, RANK, 512, 256, 256, 256, 256, 256, 256, 256])
    part = lambda n: w[:, o[n]:o[n + 1]]
    cols = np.concatenate([part(n) for n in (0, 1, 5, 6, 9, 10, 11, 2, 4, 7, 8)], axis=1)
    out = {
        "x": i["x"][0], "ln_in_g": i["ln_in_g"], "ln_in_b": i["ln_in_b"],
        "w_cols": cols.reshape(KT, P, NFM + NTM, CC).transpose(2, 1, 0, 3),
        "w_lr": part(3).reshape(KT, P, RANK).transpose(1, 0, 2),
        "ident_c": np.eye(P, dtype=np.float32),
        "w_expand": np.concatenate([i["w_gla_gate_expand"][0]] * 2),
        "gate_cols": np.concatenate([i["b_gla_gate"][0].reshape(2, P), i["hgrn_lb_raw"][0].reshape(2, P)]).T,
        "restart_c": np.broadcast_to((np.arange(SEQ) % CH != 0).astype(np.float32), (P, SEQ)),
        "w_gate_up": i["w_gate_up"][0], "w_down": i["w_down"][0], "b_gate_up": i["b_gate_up"][0], "b_down": i["b_down"][0],
        "ln_ffn_g": i["ln_ffn_g"][0], "ln_ffn_b": i["ln_ffn_b"][0],
        "norm_row": np.concatenate([np.tile(i["gla_norm_g"][0], GLA_H), np.tile(i["hgrn_norm_g"][0], HG_H)]),
        "conv_cols": i["conv_w"][0].reshape(CONV_W, 2, P).transpose(2, 1, 0),
        "w_out": i["w_out"][0], "ln_mix_g": i["ln_mix_g"][0], "ln_mix_b": i["ln_mix_b"][0],
        "w_router": i["w_router"][0], "b_router": i["b_router"][0],
        "route_c": np.broadcast_to(np.concatenate([np.arange(-(-(NE + NB_OVER) // 2) * 2), np.arange(P), P + np.arange(P) % TAIL]).astype(np.float32),
                                   (P, -(-(NE + NB_OVER) // 2) * 2 + 2 * P)),
        "fold_c": (np.arange(P) // TAIL).astype(np.float32).reshape(P, 1),
        "tri_c": (np.arange(P)[:, None] < np.arange(P)[None, :]).astype(np.float32),
        "token_c": np.arange(SEQ, dtype=np.float32).reshape(NT, P).T,
        "level_masks": level_masks(), "diag_mask": np.eye(P, dtype=np.int32),
    }
    return {n: np.ascontiguousarray(v) for n, v in out.items()}


def kernel(**inputs):
    import concourse.bacc as bacc
    from concourse.bass_utils import run_bass_kernel_spmd

    nc = bacc.Bacc("TRN2", target_bir_lowering=False, num_devices=1)
    arrays = layout(inputs)
    a = {n: nc.dram_tensor(n, v.shape, mybir.dt.from_np(v.dtype), kind="ExternalInput").ap() for n, v in arrays.items()}
    a["out"] = nc.dram_tensor("out", (1, SEQ, D), F32, kind="ExternalOutput").ap()
    build(nc, a)
    return run_bass_kernel_spmd(nc, [arrays], core_ids=[0]).results[0]["out"]
```
